# Optimizing a Trainium2 kernel written in Bass

```python
import math
import jax
import jax.numpy as jnp
from jax import lax
import numpy as np
import jax, jax.numpy as jnp

D_MODEL = 1024
BATCH = 1
SEQ = 256
DEPTH = 2

GRID_W = 64
HEAD_DIM = 64
N_HEADS_TOTAL = D_MODEL // HEAD_DIM
GROUP_HEADS = N_HEADS_TOTAL // 4
GROUP_KV_HEADS = GROUP_HEADS // 2
GQA_GROUP = GROUP_HEADS // GROUP_KV_HEADS
MIX_WIDTH = 4 * GROUP_HEADS * HEAD_DIM
ROPE_THETA = 10000.0
NORM_EPS = 1e-6
Q_BLOCK = 128
NEG_INF = -1e30

NA_WIN_ROWS = 8
NA_WIN_COLS = 16

MLA_Q_RANK = D_MODEL // 4
MLA_KV_RANK = D_MODEL // 8
MLA_NOPE = HEAD_DIM
MLA_ROPE = HEAD_DIM // 2
MLA_V = HEAD_DIM

SW_WINDOW = 128

D_FF = 2816
CONV_W = 3

SPLIT_SIZES = (
    GROUP_HEADS * HEAD_DIM, GROUP_HEADS * HEAD_DIM, GROUP_HEADS * HEAD_DIM,
    MLA_Q_RANK, MLA_KV_RANK, MLA_ROPE,
    GROUP_HEADS * HEAD_DIM, GROUP_KV_HEADS * HEAD_DIM, GROUP_KV_HEADS * HEAD_DIM,
    GROUP_HEADS * HEAD_DIM, GROUP_KV_HEADS * HEAD_DIM, GROUP_KV_HEADS * HEAD_DIM,
)
IN_COLS = sum(SPLIT_SIZES)


def rms_norm(x, gain):
    xf = x.astype(jnp.float32)
    y = xf * lax.rsqrt(jnp.mean(xf * xf, axis=-1, keepdims=True) + NORM_EPS) * gain.astype(jnp.float32)
    return y.astype(x.dtype)

def rope_angles(pos, dim):
    inv = ROPE_THETA ** (-jnp.arange(0, dim, 2, dtype=jnp.float32) / dim)
    return pos.astype(jnp.float32)[:, None] * inv[None, :]

def apply_rope(x, ang):
    cos = jnp.cos(ang)[None, :, None, :]
    sin = jnp.sin(ang)[None, :, None, :]
    x1, x2 = jnp.split(x.astype(jnp.float32), 2, axis=-1)
    out = jnp.concatenate([x1 * cos - x2 * sin, x2 * cos + x1 * sin], axis=-1)
    return out.astype(x.dtype)

def axial_rope(x, ang_row, ang_col):
    half = x.shape[-1] // 2
    return jnp.concatenate([apply_rope(x[..., :half], ang_row), apply_rope(x[..., half:], ang_col)], axis=-1)

def split_columns(z):
    points = []
    acc = 0
    for n in SPLIT_SIZES[:-1]:
        acc += n
        points.append(acc)
    return jnp.split(z, points, axis=-1)

def dense_attention_blocked(q, k, v, scale):
    b, s, hkv, g, dq = q.shape
    nb = s // Q_BLOCK
    qb = q.reshape(b, nb, Q_BLOCK, hkv, g, dq).transpose(1, 0, 2, 3, 4, 5)

    def one_block(q_blk):
        sc = jnp.einsum('bqhgd,bkhd->bhgqk', q_blk, k).astype(jnp.float32) * scale
        p = jax.nn.softmax(sc, axis=-1).astype(v.dtype)
        return jnp.einsum('bhgqk,bkhd->bqhgd', p, v)

    out = lax.map(one_block, qb)
    return out.transpose(1, 0, 2, 3, 4, 5).reshape(b, s, hkv, g, v.shape[-1])

def sliding_window_sink_attention(q, k, v, sink, scale):
    b, s, hkv, g, d = q.shape
    nb = s // Q_BLOCK
    pad = ((0, 0), (Q_BLOCK, Q_BLOCK), (0, 0), (0, 0))
    kp = jnp.pad(k, pad).reshape(b, nb + 2, Q_BLOCK, hkv, d)
    vp = jnp.pad(v, pad).reshape(b, nb + 2, Q_BLOCK, hkv, d)
    kb = jnp.concatenate([kp[:, :-2], kp[:, 1:-1], kp[:, 2:]], axis=2)
    vb = jnp.concatenate([vp[:, :-2], vp[:, 1:-1], vp[:, 2:]], axis=2)
    qb = q.reshape(b, nb, Q_BLOCK, hkv, g, d)
    sc = jnp.einsum('bnqhgd,bnkhd->bnhgqk', qb, kb).astype(jnp.float32) * scale
    blk = jnp.arange(nb)[:, None] * Q_BLOCK
    qpos = blk + jnp.arange(Q_BLOCK)[None, :]
    kpos = blk - Q_BLOCK + jnp.arange(3 * Q_BLOCK)[None, :]
    valid = (jnp.abs(qpos[:, :, None] - kpos[:, None, :]) <= SW_WINDOW) & ((kpos >= 0) & (kpos < s))[:, None, :]
    sc = jnp.where(valid[None, :, None, None], sc, NEG_INF)
    sink_l = jnp.broadcast_to(sink.reshape(hkv, g).astype(jnp.float32)[None, None, :, :, None, None],
                              sc.shape[:-1] + (1,))
    p = jax.nn.softmax(jnp.concatenate([sc, sink_l], axis=-1), axis=-1)[..., :-1]
    out = jnp.einsum('bnhgqk,bnkhd->bnqhgd', p.astype(v.dtype), vb)
    return out.reshape(b, s, hkv, g, d)

def neighbourhood_attention_2d(q, k, v, rpb):
    b, s, h, d = q.shape
    rows = s // GRID_W
    kr = min(NA_WIN_ROWS, rows)
    kc = NA_WIN_COLS
    qg = q.reshape(b, rows, GRID_W, h, d)
    kg = k.reshape(b, rows, GRID_W, h, d)
    vg = v.reshape(b, rows, GRID_W, h, d)
    col = jnp.arange(GRID_W)
    col_start = jnp.clip(col - kc // 2, 0, GRID_W - kc)
    col_idx = col_start[:, None] + jnp.arange(kc)[None, :]
    col_off = col_idx - col[:, None] + (NA_WIN_COLS - 1)
    row_ids = jnp.arange(rows)
    row_start = jnp.clip(row_ids - kr // 2, 0, rows - kr)
    scale = HEAD_DIM ** -0.5

    def one_row(args):
        r, rs = args
        q_r = lax.dynamic_index_in_dim(qg, r, axis=1, keepdims=False)
        k_band = lax.dynamic_slice_in_dim(kg, rs, kr, axis=1)
        v_band = lax.dynamic_slice_in_dim(vg, rs, kr, axis=1)
        k_nb = k_band[:, :, col_idx]
        v_nb = v_band[:, :, col_idx]
        row_off = rs + jnp.arange(kr) - r + (NA_WIN_ROWS - 1)
        bias = rpb[:, row_off[:, None, None], col_off[None, :, :]]
        sc = jnp.einsum('bchd,bacwhd->bhcaw', q_r, k_nb).astype(jnp.float32) * scale
        sc = sc + bias.transpose(0, 2, 1, 3)[None].astype(jnp.float32)
        p = jax.nn.softmax(sc.reshape(b, h, GRID_W, kr * kc), axis=-1)
        p = p.reshape(b, h, GRID_W, kr, kc).astype(v.dtype)
        return jnp.einsum('bhcaw,bacwhd->bchd', p, v_nb)

    out = lax.map(one_row, (row_ids, row_start))
    return out.transpose(1, 0, 2, 3, 4).reshape(b, s, h, d)

def conv_gated_mlp(h, w_up, conv_w, conv_b, w_down):
    u = h @ w_up
    s = u.shape[1]
    half = CONV_W // 2
    up = jnp.pad(u, ((0, 0), (half, half), (0, 0)))
    c = conv_b
    for i in range(CONV_W):
        c = c + up[:, i:i + s] * conv_w[i]
    gate, val = jnp.split(c, 2, axis=-1)
    return (jax.nn.gelu(gate, approximate=True) * val) @ w_down

def first_inputs(seed: int = 0) -> dict:
    key = jax.random.key(seed)
    ks = jax.random.split(key, 20)
    f32 = jnp.float32

    def dense(k, shape, fan_in):
        return jax.random.normal(k, shape, f32) * fan_in ** -0.5

    def gain(k, n):
        return 1.0 + 0.05 * jax.random.normal(k, (DEPTH, n), f32)

    return {
        'x': jax.random.normal(ks[0], (BATCH, SEQ, D_MODEL), f32),
        'mix_pre_gain': gain(ks[1], D_MODEL),
        'w_in': dense(ks[2], (DEPTH, D_MODEL, IN_COLS), D_MODEL),
        'na_rpb': 0.1 * jax.random.normal(ks[3], (DEPTH, GROUP_HEADS, 2 * NA_WIN_ROWS - 1, 2 * NA_WIN_COLS - 1), f32),
        'mla_q_gain': gain(ks[4], MLA_Q_RANK),
        'mla_w_uq': dense(ks[5], (DEPTH, MLA_Q_RANK, GROUP_HEADS * (MLA_NOPE + MLA_ROPE)), MLA_Q_RANK),
        'mla_kv_gain': gain(ks[6], MLA_KV_RANK),
        'mla_w_ukv': dense(ks[7], (DEPTH, MLA_KV_RANK, GROUP_HEADS * (MLA_NOPE + MLA_V)), MLA_KV_RANK),
        'ax_q_gain': gain(ks[8], HEAD_DIM),
        'ax_k_gain': gain(ks[9], HEAD_DIM),
        'sw_sink': 0.5 * jax.random.normal(ks[10], (DEPTH, GROUP_HEADS), f32),
        'w_out': dense(ks[11], (DEPTH, MIX_WIDTH, D_MODEL), MIX_WIDTH),
        'mix_post_gain': gain(ks[12], D_MODEL),
        'ffn_pre_gain': gain(ks[13], D_MODEL),
        'w_up': dense(ks[14], (DEPTH, D_MODEL, 2 * D_FF), D_MODEL),
        'conv_w': dense(ks[15], (DEPTH, CONV_W, 2 * D_FF), CONV_W),
        'conv_b': 0.01 * jax.random.normal(ks[16], (DEPTH, 2 * D_FF), f32),
        'w_down': dense(ks[17], (DEPTH, D_FF, D_MODEL), D_FF),
        'ffn_post_gain': gain(ks[18], D_MODEL),
    }

def first_block(x, mix_pre_gain, w_in, na_rpb, mla_q_gain, mla_w_uq, mla_kv_gain, mla_w_ukv,
              ax_q_gain, ax_k_gain, sw_sink, w_out, mix_post_gain, ffn_pre_gain, w_up,
              conv_w, conv_b, w_down, ffn_post_gain):
    b, s, _ = x.shape
    t = jnp.arange(s)
    ang_full = rope_angles(t, HEAD_DIM)
    ang_mla = rope_angles(t, MLA_ROPE)
    ang_row = rope_angles(t // GRID_W, HEAD_DIM // 2)
    ang_col = rope_angles(t % GRID_W, HEAD_DIM // 2)

    def heads(z, n):
        return z.reshape(b, s, n, -1)

    for l in range(DEPTH):
        h = rms_norm(x, mix_pre_gain[l])
        (a_q, a_k, a_v, b_cq, b_ckv, b_kr,
         c_q, c_k, c_v, d_q, d_k, d_v) = split_columns(h @ w_in[l])

        o_a = neighbourhood_attention_2d(heads(a_q, GROUP_HEADS), heads(a_k, GROUP_HEADS),
                                         heads(a_v, GROUP_HEADS), na_rpb[l])

        q_b = (rms_norm(b_cq, mla_q_gain[l]) @ mla_w_uq[l]).reshape(b, s, GROUP_HEADS, MLA_NOPE + MLA_ROPE)
        q_nope, q_pe = jnp.split(q_b, [MLA_NOPE], axis=-1)
        q_b = jnp.concatenate([q_nope, apply_rope(q_pe, ang_mla)], axis=-1)
        kv_b = (rms_norm(b_ckv, mla_kv_gain[l]) @ mla_w_ukv[l]).reshape(b, s, GROUP_HEADS, MLA_NOPE + MLA_V)
        k_nope, v_b = jnp.split(kv_b, [MLA_NOPE], axis=-1)
        k_pe = apply_rope(b_kr.reshape(b, s, 1, MLA_ROPE), ang_mla)
        k_b = jnp.concatenate([k_nope, jnp.broadcast_to(k_pe, (b, s, GROUP_HEADS, MLA_ROPE))], axis=-1)
        o_b = dense_attention_blocked(q_b[:, :, :, None, :], k_b, v_b, (MLA_NOPE + MLA_ROPE) ** -0.5)

        q_c = axial_rope(rms_norm(heads(c_q, GROUP_HEADS), ax_q_gain[l]), ang_row, ang_col)
        k_c = axial_rope(rms_norm(heads(c_k, GROUP_KV_HEADS), ax_k_gain[l]), ang_row, ang_col)
        o_c = dense_attention_blocked(q_c.reshape(b, s, GROUP_KV_HEADS, GQA_GROUP, HEAD_DIM), k_c,
                                      heads(c_v, GROUP_KV_HEADS), HEAD_DIM ** -0.5)

        q_d = apply_rope(heads(d_q, GROUP_HEADS), ang_full).reshape(b, s, GROUP_KV_HEADS, GQA_GROUP, HEAD_DIM)
        k_d = apply_rope(heads(d_k, GROUP_KV_HEADS), ang_full)
        o_d = sliding_window_sink_attention(q_d, k_d, heads(d_v, GROUP_KV_HEADS), sw_sink[l], HEAD_DIM ** -0.5)

        mixed = jnp.concatenate([o_a.reshape(b, s, -1), o_b.reshape(b, s, -1),
                                 o_c.reshape(b, s, -1), o_d.reshape(b, s, -1)], axis=-1) @ w_out[l]
        x = x + rms_norm(mixed, mix_post_gain[l])

        h = rms_norm(x, ffn_pre_gain[l])
        y = conv_gated_mlp(h, w_up[l], conv_w[l], conv_b[l], w_down[l])
        x = x + rms_norm(y, ffn_post_gain[l])
    return x


HEAD_DIM_2 = D_MODEL // 16
SB_HEADS = 6
ML_HEADS = 6
SG_GROUPS = 4
SB_WIDTH = SB_HEADS * HEAD_DIM_2
ML_WIDTH = ML_HEADS * HEAD_DIM_2
SG_WIDTH = SG_GROUPS * HEAD_DIM_2
MIX_HEADS = SB_HEADS + ML_HEADS + SG_GROUPS
MIX_WIDTH_2 = SB_WIDTH + ML_WIDTH + SG_WIDTH
IN_SIZES = (SB_WIDTH, SB_WIDTH, SB_WIDTH, 2 * ML_WIDTH, ML_WIDTH, ML_WIDTH, ML_HEADS, ML_HEADS, 2 * SG_WIDTH)
IN_WIDTH = sum(IN_SIZES)
ML_CHUNK = 128
SG_CHUNK = 128
CONV_WIDTH = 4
PEER_HEADS = 8
PEER_NKEYS = 128
PEER_EXPERTS = PEER_NKEYS * PEER_NKEYS
PEER_SUBDIM = 128
PEER_TOPK = 16
PEER_BLOCK = 128


def rms_norm_2(x, g):
    x32 = x.astype(jnp.float32)
    return x32 * lax.rsqrt(jnp.mean(x32 * x32, axis=-1, keepdims=True) + NORM_EPS) * g.astype(jnp.float32)

def split_heads(t, n_heads):
    b, s, _ = t.shape
    return t.reshape(b, s, n_heads, HEAD_DIM_2).transpose(0, 2, 1, 3)

def causal_conv(t, w, b):
    s = t.shape[1]
    tp = jnp.pad(t, ((0, 0), (CONV_WIDTH - 1, 0), (0, 0)))
    out = b.astype(jnp.float32)
    for j in range(CONV_WIDTH):
        out = out + tp[:, j:j + s] * w[j]
    return out

def stick_breaking_attention(q, k, v):
    s_len = q.shape[2]
    scale = HEAD_DIM_2 ** -0.5
    outs = []
    for blk in range(s_len // Q_BLOCK):
        start = blk * Q_BLOCK
        end = start + Q_BLOCK
        z = jnp.einsum('bhqd,bhkd->bhqk', q[:, :, start:end], k[:, :, :end]) * scale
        before = jnp.arange(end)[None, :] < (start + jnp.arange(Q_BLOCK))[:, None]
        log_keep = jnp.where(before, -jax.nn.softplus(z), 0.0)
        log_keep_after = lax.cumsum(log_keep, axis=3, reverse=True) - log_keep
        w = jnp.where(before, jnp.exp(jax.nn.log_sigmoid(z) + log_keep_after), 0.0)
        outs.append(jnp.einsum('bhqk,bhkd->bhqd', w, v[:, :, :end]))
    return jnp.concatenate(outs, axis=2)

def mlstm_chunkwise(q, k, v, i_pre, f_pre):
    b, h, s_len, d = q.shape
    nc = s_len // ML_CHUNK
    log_f = jax.nn.log_sigmoid(f_pre)

    def chunks(t):
        return jnp.moveaxis(t.reshape(b, h, nc, ML_CHUNK, *t.shape[3:]), 2, 0)

    tril = jnp.tril(jnp.ones((ML_CHUNK, ML_CHUNK), dtype=bool))

    def step(carry, inp):
        c_mat, n_vec, m = carry
        qc, kc, vc, ic, lfc = inp
        bcum = jnp.cumsum(lfc, axis=-1)
        dmat = jnp.where(tril, bcum[..., :, None] - bcum[..., None, :] + ic[..., None, :], -jnp.inf)
        m_inter = bcum + m[..., None]
        m_t = jnp.maximum(m_inter, jnp.max(dmat, axis=-1))
        inter_scale = jnp.exp(m_inter - m_t)
        qk = jnp.einsum('bhtd,bhsd->bhts', qc, kc) * jnp.exp(dmat - m_t[..., None])
        num = jnp.einsum('bhts,bhsd->bhtd', qk, vc) + inter_scale[..., None] * jnp.einsum('bhtd,bhde->bhte', qc, c_mat)
        den = jnp.sum(qk, axis=-1) + inter_scale * jnp.einsum('bhtd,bhd->bht', qc, n_vec)
        h_out = num / jnp.maximum(jnp.abs(den), jnp.exp(-m_t))[..., None]
        b_last = bcum[..., -1]
        g_s = b_last[..., None] - bcum + ic
        m_new = jnp.maximum(b_last + m, jnp.max(g_s, axis=-1))
        w_s = jnp.exp(g_s - m_new[..., None])
        decay = jnp.exp(b_last + m - m_new)
        c_new = decay[..., None, None] * c_mat + jnp.einsum('bhs,bhsd,bhse->bhde', w_s, kc, vc)
        n_new = decay[..., None] * n_vec + jnp.einsum('bhs,bhsd->bhd', w_s, kc)
        return (c_new, n_new, m_new), h_out

    init = (jnp.zeros((b, h, d, d), jnp.float32), jnp.zeros((b, h, d), jnp.float32), jnp.zeros((b, h), jnp.float32))
    _, hs = lax.scan(step, init, (chunks(q), chunks(k), chunks(v), chunks(i_pre), chunks(log_f)))
    return jnp.moveaxis(hs, 0, 2).reshape(b, h, s_len, d)

def spatial_gating(u, v, w_s, b_s):
    b, s_len, _ = u.shape
    nc = s_len // SG_CHUNK
    tril = jnp.tril(jnp.ones((SG_CHUNK, SG_CHUNK), dtype=jnp.float32))
    v5 = v.reshape(b, nc, SG_CHUNK, SG_GROUPS, HEAD_DIM_2)
    gate = jnp.einsum('gts,bcsgd->bctgd', w_s.astype(jnp.float32) * tril, v5) + b_s.astype(jnp.float32).T[:, :, None]
    return (u.reshape(b, nc, SG_CHUNK, SG_GROUPS, HEAD_DIM_2) * gate).reshape(b, s_len, SG_GROUPS, HEAD_DIM_2)

def mixing_sublayer(xn, w_in, sb_qn_g, sb_kn_g, ml_conv_w, ml_conv_b, ml_i_b, ml_f_b,
                    sg_vn_g, sg_w, sg_b, out_g, w_out):
    b, s_len, _ = xn.shape
    z = jnp.matmul(xn, w_in).astype(jnp.float32)
    cuts = [int(c) for c in np.cumsum(IN_SIZES)[:-1]]
    sb_q, sb_k, sb_v, ml_qk, ml_v, ml_o, ml_i, ml_f, sg_uv = jnp.split(z, cuts, axis=-1)
    head_g = out_g.astype(jnp.float32).reshape(MIX_HEADS, HEAD_DIM_2)

    q = rms_norm_2(split_heads(sb_q, SB_HEADS), sb_qn_g)
    k = rms_norm_2(split_heads(sb_k, SB_HEADS), sb_kn_g)
    y_sb = stick_breaking_attention(q, k, split_heads(sb_v, SB_HEADS)).transpose(0, 2, 1, 3)
    y_sb = rms_norm_2(y_sb, head_g[:SB_HEADS])

    qk = jax.nn.silu(causal_conv(ml_qk, ml_conv_w.astype(jnp.float32), ml_conv_b))
    mq = split_heads(qk[..., :ML_WIDTH], ML_HEADS)
    mk = split_heads(qk[..., ML_WIDTH:], ML_HEADS) * (HEAD_DIM_2 ** -0.5)
    i_pre = (ml_i + ml_i_b.astype(jnp.float32)).transpose(0, 2, 1)
    f_pre = (ml_f + ml_f_b.astype(jnp.float32)).transpose(0, 2, 1)
    y_ml = mlstm_chunkwise(mq, mk, split_heads(ml_v, ML_HEADS), i_pre, f_pre).transpose(0, 2, 1, 3)
    o_gate = jax.nn.sigmoid(ml_o).reshape(b, s_len, ML_HEADS, HEAD_DIM_2)
    y_ml = rms_norm_2(y_ml, head_g[SB_HEADS:SB_HEADS + ML_HEADS]) * o_gate

    uv = jax.nn.gelu(sg_uv)
    u = uv[..., :SG_WIDTH]
    v = rms_norm_2(uv[..., SG_WIDTH:].reshape(b, s_len, SG_GROUPS, HEAD_DIM_2),
                 sg_vn_g.reshape(SG_GROUPS, HEAD_DIM_2)).reshape(b, s_len, SG_WIDTH)
    y_sg = rms_norm_2(spatial_gating(u, v, sg_w, sg_b), head_g[SB_HEADS + ML_HEADS:])

    y = jnp.concatenate([y_sb, y_ml, y_sg], axis=2).reshape(b, s_len, MIX_WIDTH_2)
    return jnp.matmul(y.astype(xn.dtype), w_out)

def peer_ffn(xn, wq, sub_keys, u_tab, v_tab):
    b, s_len, d = xn.shape
    t = b * s_len
    xt = xn.reshape(t, d)
    q = jnp.matmul(xt, wq).astype(jnp.float32).reshape(t, PEER_HEADS, 2, PEER_SUBDIM)
    scores = jnp.einsum('thcd,hcnd->thcn', q, sub_keys.astype(jnp.float32))
    sv, si = lax.top_k(scores, PEER_TOPK)
    cand_s = (sv[:, :, 0, :, None] + sv[:, :, 1, None, :]).reshape(t, PEER_HEADS, PEER_TOPK * PEER_TOPK)
    cand_i = (si[:, :, 0, :, None] * PEER_NKEYS + si[:, :, 1, None, :]).reshape(t, PEER_HEADS, PEER_TOPK * PEER_TOPK)
    best_s, best_p = lax.top_k(cand_s, PEER_TOPK)
    idx = jnp.take_along_axis(cand_i, best_p, axis=-1)
    gate = jax.nn.softmax(best_s, axis=-1)
    nb = t // PEER_BLOCK

    def expert_block(args):
        xb, ib, gb = args
        act = jnp.einsum('td,thkd->thk', xb.astype(jnp.float32), u_tab[ib].astype(jnp.float32))
        wgt = jax.nn.gelu(act) * gb
        return jnp.einsum('thk,thkd->td', wgt, v_tab[ib].astype(jnp.float32))

    y = lax.map(expert_block, (xt.reshape(nb, PEER_BLOCK, d),
                               idx.reshape(nb, PEER_BLOCK, PEER_HEADS, PEER_TOPK),
                               gate.reshape(nb, PEER_BLOCK, PEER_HEADS, PEER_TOPK)))
    return y.reshape(b, s_len, d)

def second_inputs(seed: int = 0) -> dict:
    key = jax.random.key(seed)
    ks = jax.random.split(key, 20)
    f32 = jnp.float32
    nrm = lambda k, shape, scale: jax.random.normal(k, shape, f32) * scale
    return {
        "x": nrm(ks[0], (BATCH, SEQ, D_MODEL), 1.0),
        "norm1_g": 1.0 + nrm(ks[1], (DEPTH, D_MODEL), 0.02),
        "w_in": nrm(ks[2], (DEPTH, D_MODEL, IN_WIDTH), D_MODEL ** -0.5),
        "sb_qn_g": 1.0 + nrm(ks[3], (DEPTH, HEAD_DIM_2), 0.02),
        "sb_kn_g": 1.0 + nrm(ks[4], (DEPTH, HEAD_DIM_2), 0.02),
        "ml_conv_w": nrm(ks[5], (DEPTH, CONV_WIDTH, 2 * ML_WIDTH), CONV_WIDTH ** -0.5),
        "ml_conv_b": nrm(ks[6], (DEPTH, 2 * ML_WIDTH), 0.02),
        "ml_i_b": nrm(ks[7], (DEPTH, ML_HEADS), 0.1),
        "ml_f_b": jnp.linspace(3.0, 6.0, ML_HEADS, dtype=f32)[None, :] + nrm(ks[8], (DEPTH, ML_HEADS), 0.02),
        "sg_vn_g": 1.0 + nrm(ks[9], (DEPTH, SG_WIDTH), 0.02),
        "sg_w": nrm(ks[10], (DEPTH, SG_GROUPS, SG_CHUNK, SG_CHUNK), SG_CHUNK ** -0.5),
        "sg_b": 1.0 + nrm(ks[11], (DEPTH, SG_GROUPS, SG_CHUNK), 0.02),
        "out_g": 1.0 + nrm(ks[12], (DEPTH, MIX_WIDTH_2), 0.02),
        "w_out": nrm(ks[13], (DEPTH, MIX_WIDTH_2, D_MODEL), MIX_WIDTH_2 ** -0.5),
        "norm2_g": 1.0 + nrm(ks[14], (DEPTH, D_MODEL), 0.02),
        "peer_wq": nrm(ks[15], (DEPTH, D_MODEL, PEER_HEADS * 2 * PEER_SUBDIM), D_MODEL ** -0.5),
        "peer_keys": nrm(ks[16], (DEPTH, PEER_HEADS, 2, PEER_NKEYS, PEER_SUBDIM), PEER_SUBDIM ** -0.5),
        "peer_u": nrm(ks[17], (DEPTH, PEER_EXPERTS, D_MODEL), D_MODEL ** -0.5),
        "peer_v": nrm(ks[18], (DEPTH, PEER_EXPERTS, D_MODEL), (PEER_HEADS * PEER_TOPK) ** -0.5),
    }

def second_block(x, norm1_g, w_in, sb_qn_g, sb_kn_g, ml_conv_w, ml_conv_b, ml_i_b, ml_f_b,
              sg_vn_g, sg_w, sg_b, out_g, w_out, norm2_g, peer_wq, peer_keys, peer_u, peer_v):
    for l in range(DEPTH):
        xn = rms_norm_2(x, norm1_g[l]).astype(x.dtype)
        x = x + mixing_sublayer(xn, w_in[l], sb_qn_g[l], sb_kn_g[l], ml_conv_w[l], ml_conv_b[l],
                                ml_i_b[l], ml_f_b[l], sg_vn_g[l], sg_w[l], sg_b[l], out_g[l],
                                w_out[l]).astype(x.dtype)
        xn = rms_norm_2(x, norm2_g[l]).astype(x.dtype)
        x = x + peer_ffn(xn, peer_wq[l], peer_keys[l], peer_u[l], peer_v[l]).astype(x.dtype)
    return x


def setup_inputs(seed=0):
    out = dict(first_inputs(seed))
    for name, value in second_inputs(seed + 1).items():
        if name != "x":
            out[name + "_2"] = value
    return out


def reference(
    x, mix_pre_gain, w_in, na_rpb, mla_q_gain, mla_w_uq, mla_kv_gain, mla_w_ukv, ax_q_gain,
    ax_k_gain, sw_sink, w_out, mix_post_gain, ffn_pre_gain, w_up, conv_w, conv_b, w_down,
    ffn_post_gain, norm1_g_2, w_in_2, sb_qn_g_2, sb_kn_g_2, ml_conv_w_2, ml_conv_b_2, ml_i_b_2,
    ml_f_b_2, sg_vn_g_2, sg_w_2, sg_b_2, out_g_2, w_out_2, norm2_g_2, peer_wq_2, peer_keys_2,
    peer_u_2, peer_v_2,
):
    x = first_block(
        x, mix_pre_gain, w_in, na_rpb, mla_q_gain, mla_w_uq, mla_kv_gain, mla_w_ukv, ax_q_gain,
        ax_k_gain, sw_sink, w_out, mix_post_gain, ffn_pre_gain, w_up, conv_w, conv_b, w_down,
        ffn_post_gain,
    )
    return second_block(
        x, norm1_g_2, w_in_2, sb_qn_g_2, sb_kn_g_2, ml_conv_w_2, ml_conv_b_2, ml_i_b_2,
        ml_f_b_2, sg_vn_g_2, sg_w_2, sg_b_2, out_g_2, w_out_2, norm2_g_2, peer_wq_2,
        peer_keys_2, peer_u_2, peer_v_2,
    )


_drawn_inputs = setup_inputs


def setup_inputs(seed=0):
    import zlib

    import numpy as np

    out = dict(_drawn_inputs(seed))
    spreads = {}
    factors = {'mla_q_gain': 2.866,
     'ax_q_gain': 3.139,
     'ax_k_gain': 3.065,
     'sw_sink': 8.0,
     'conv_b': 4.167,
     'norm1_g_2': 4.338,
     'sb_qn_g_2': 8.0,
     'sb_kn_g_2': 8.0,
     'ml_conv_b_2': 8.0,
     'ml_i_b_2': 64.0,
     'sg_vn_g_2': 8.0,
     'sg_b_2': 8.0,
     'out_g_2': 5.346,
     'norm2_g_2': 8.0}
    for name, (base, spread) in spreads.items():
        noise = np.random.default_rng([zlib.crc32(name.encode()), seed]).standard_normal(out[name].shape)
        drawn = base * np.exp(spread * noise) if base else spread * noise
        out[name] = jnp.asarray(drawn.astype(out[name].dtype))
    for name, factor in factors.items():
        out[name] = (out[name] * factor).astype(out[name].dtype)
    return out
```

```python
from contextlib import ExitStack

import numpy as np
import concourse.bass as bass
from concourse import mybir

F32 = mybir.dt.float32
BF16 = mybir.dt.bfloat16
U32 = mybir.dt.uint32
ALU = mybir.AluOpType
ACT = mybir.ActivationFunctionType
AX = mybir.AxisListType.X

P = 128
T = 256
NT = T // P
D = 1024
KD = D // P
L = 2
HD = 64
EPS = 1e-6
BIG = 1e30
GRID = 64

A_Q, A_K, A_V = 0, 256, 512
B_CQ, B_CKV, B_KR = 768, 1024, 1152
C_Q, C_K, C_V = 1184, 1440, 1568
D_Q, D_K, D_V = 1696, 1952, 2080
IN1 = 2208
FF = 2816
NF = FF // P

MLQK, MLQK_W = 1152, 768
SB_Q, SB_K, SB_V = 0, 384, 768
ML_V, ML_O, ML_IF, SG_UV = 1152, 1536, 1920, 1932
IN2 = 3212
Z2 = IN2 - MLQK_W
NH6 = 6
SGG = 4

NSET = 16
PH = 8
TOPK = 16
NKEY = 128


def constant_plan():
    sizes = [("ident", P), ("iota", P), ("mask_na", 2 * T), ("mask_sw", 2 * T),
             ("strict01", 2 * T), ("strict_big", 2 * T), ("causal_big", 2 * T), ("tril_t", P),
             ("suffix", P), ("ones", P), ("cos_full", 2 * 32), ("sin_full", 2 * 32),
             ("cos_mla", 2 * 16), ("sin_mla", 2 * 16), ("cos_row", 2 * 16), ("sin_row", 2 * 16),
             ("cos_col", 2 * 16), ("sin_col", 2 * 16), ("pick", NH6 * P)]
    plan, at = {}, 0
    for name, width in sizes:
        plan[name] = (at, width)
        at += width
    return plan, at


CONST, NCONST = constant_plan()


def build(nc, a, out, dbg=None, blocks=(1, 2)):
    with ExitStack() as ctx:
        sb = lambda name, shape, dt=F32: ctx.enter_context(nc.sbuf_tensor(name, shape, dt))
        X = sb("X", [P, NT, D])
        HT = sb("HT", [P, KD, T])
        CON = sb("CON", [P, NCONST])
        ZERO = sb("ZERO", [P, 512], BF16)
        STAT = sb("STAT", [P, 256])
        HALF = sb("HALF", [P, 64])
        ARENA_N = 42752
        ARENA = sb("ARENA", [P, ARENA_N])
        bank = [ctx.enter_context(nc.psum_tensor(f"bank{i}", [P, 512], F32)) for i in range(8)]

        semaphores = {}

        def S(name):
            if name not in semaphores:
                semaphores[name] = nc.alloc_semaphore(name)
            return semaphores[name]

        def clear_all():
            nums = sorted(s.num for s in semaphores.values())
            assert nums == list(range(nums[0], nums[-1] + 1)), nums
            nc.all_engine_barrier(sems_to_clear=range(nums[0], nums[-1] + 1))

        def view(ap, *dims, off=0):
            return bass.AP(ap.tensor, ap.offset + off, [list(ap.ap[0])] + [list(d) for d in dims])

        def const(name, *dims, parts=P, off=0):
            at, width = CONST[name]
            ap = CON[0:parts, at:at + width]
            return view(ap, *dims, off=off) if dims else ap

        ident = const("ident")

        def arena(at, n, parts=P):
            assert at + n <= ARENA_N, (at, n)
            return ARENA[0:parts, at:at + n]

        def shaped(at, *shape):
            n = int(np.prod(shape))
            ap = arena(at, n)
            strides = [int(np.prod(shape[i + 1:])) for i in range(len(shape))]
            return view(ap, *zip(strides, shape))

        with nc.Block() as b:
            @b.sync
            def _(sp):
                sp.dma_start(CON[:, :], a["consts"][:, :]).then_inc(S("set_up_loaded"), 16)
                sp.dma_start(X[:, :, :], a["x"][0].rearrange("(t p) d -> p t d", p=P)
                             ).then_inc(S("set_up_loaded"), 16)
                sp.wait_ge(S("set_up_loaded"), 32)

            @b.vector
            def _(dve):
                nc.vector.memset(ZERO[:, :], 0.0)
                nc.vector.memset(HALF[:, :], -0.5)

        def pool_rstd(pool, ss, scale, n):
            nc.gpsimd.tensor_scalar(ss, ss, scale, EPS, ALU.mult, ALU.add)
            pool.drain()
            shape = [c for _, c in list(ss.ap)[1:]]
            h = view(HALF[:, 0:n], *([(shape[1], shape[0]), (1, shape[1])] if len(shape) == 2 else [(1, n)]))
            return nc.gpsimd.tensor_tensor(ss, ss, h, ALU.pow)

        def norm_to_ht(tag, l, gain_dram, xn_at, gain_at, junk_at, extra_loads=None):
            xn = shaped(xn_at, NT, D)
            gain = arena(gain_at, KD)
            junk = shaped(junk_at, NT, D)
            ss = STAT[:, 0:NT]
            with nc.Block() as b:
                @b.sync
                def _(sp):
                    sp.dma_start(gain, gain_dram[l, :, :]).then_inc(S(tag + "_gain_loaded"), 16)
                    if extra_loads:
                        extra_loads(sp)

                @b.scalar
                def _(act):
                    for t in range(NT):
                        nc.scalar.activation(junk[:, t, :], X[:, t, :], ACT.Square,
                                             accum_out=ss[:, t:t + 1]).then_inc(S(tag + "_squares"), 1)
                    act.wait_ge(S(tag + "_gain_loaded"), 16)
                    for k in range(0, KD, 2):
                        act.wait_ge(S(tag + "_turned"), k + 1)
                        nc.scalar.mul(HT[:, k, :], bank[k % 4][:, 0:T], gain[:, k:k + 1]
                                      ).then_inc(S(tag + "_out_even"), 1)

                @b.gpsimd
                def _(pool):
                    pool.wait_ge(S(tag + "_squares"), NT)
                    pool_rstd(pool, ss, 1.0 / D, NT).then_inc(S(tag + "_rstd"), 1)

                @b.vector
                def _(dve):
                    dve.wait_ge(S(tag + "_rstd"), 1)
                    for t in range(NT):
                        nc.vector.tensor_scalar(xn[:, t, :], X[:, t, :], ss[:, t:t + 1], None, ALU.mult
                                                ).then_inc(S(tag + "_xn"), 1)
                    dve.wait_ge(S(tag + "_gain_loaded"), 16)
                    for k in range(1, KD, 2):
                        dve.wait_ge(S(tag + "_turned"), k + 1)
                        nc.vector.tensor_scalar(HT[:, k, :], bank[k % 4][:, 0:T], gain[:, k:k + 1], None,
                                                ALU.mult).then_inc(S(tag + "_out_odd"), 1)

                @b.tensor
                def _(pe):
                    pe.wait_ge(S(tag + "_xn"), NT)
                    for k in range(KD):
                        if k >= 4:
                            pe.wait_ge(S(tag + ("_out_odd" if k % 2 else "_out_even")), (k - 4) // 2 + 1)
                        for t in range(NT):
                            last = nc.tensor.transpose(bank[k % 4][:, t * P:(t + 1) * P],
                                                       xn[:, t, k * P:(k + 1) * P], ident)
                        last.then_inc(S(tag + "_turned"), 1)

        def turn_to_ht(tag, src):
            with nc.Block() as b:
                @b.scalar
                def _(act):
                    for k in range(0, KD, 2):
                        act.wait_ge(S(tag + "_turned"), k + 1)
                        nc.scalar.copy(HT[:, k, :], bank[k % 4][:, 0:T]).then_inc(S(tag + "_out_even"), 1)

                @b.vector
                def _(dve):
                    for k in range(1, KD, 2):
                        dve.wait_ge(S(tag + "_turned"), k + 1)
                        nc.vector.tensor_copy(HT[:, k, :], bank[k % 4][:, 0:T]
                                              ).then_inc(S(tag + "_out_odd"), 1)

                @b.tensor
                def _(pe):
                    for k in range(KD):
                        if k >= 4:
                            pe.wait_ge(S(tag + ("_out_odd" if k % 2 else "_out_even")), (k - 4) // 2 + 1)
                        for t in range(NT):
                            last = nc.tensor.transpose(bank[k % 4][:, t * P:(t + 1) * P],
                                                       src[:, t, k * P:(k + 1) * P], ident)
                        last.then_inc(S(tag + "_turned"), 1)

        RING = 3
        RING_N = KD * 512

        def linear_load(sp, tag, w_view, ring_at, chunks, c):
            slot = c % RING
            kind, n0, w, _ = chunks[c]
            dst = view(arena(ring_at + slot * RING_N, RING_N), (512, KD), (1, w))
            sp.dma_start(dst, w_view[:, :, n0:n0 + w]).then_inc(S(f"{tag}_w_loaded{slot}"), 16)

        def linear(tag, w_view, ring_at, chunks, dst_of, preloaded=0, extra_loads=None, extra_dve=None):
            fills = []
            for c, (kind, n0, w, d0) in enumerate(chunks):
                n = NT if kind == "rows" else w // P
                fills += [(c, i == n - 1, i) for i in range(n)]
            ends = {c: m + 1 for m, (c, last, _) in enumerate(fills) if last}

            def taken(m):
                return ("act", "dve")[m % 2], m // 2 + 1

            def dst(m):
                c, _, i = fills[m]
                kind, n0, w, d0 = chunks[c]
                if kind == "rows":
                    return dst_of(kind, i, d0, w), bank[m % 4][:, 0:w]
                return dst_of(kind, d0 + i, 0, T), bank[m % 4][:, 0:T]

            with nc.Block() as b:
                @b.sync
                def _(sp):
                    if extra_loads:
                        extra_loads(sp)
                    for c in range(preloaded, len(chunks)):
                        if c >= RING:
                            sp.wait_ge(S(tag + "_filled"), ends[c - RING])
                        linear_load(sp, tag, w_view, ring_at, chunks, c)

                @b.tensor
                def _(pe):
                    for m, (c, _, i) in enumerate(fills):
                        kind, n0, w, d0 = chunks[c]
                        slot = view(arena(ring_at + (c % RING) * RING_N, RING_N), (512, KD), (1, 512))
                        if i == 0:
                            pe.wait_ge(S(f"{tag}_w_loaded{c % RING}"), 16 * (c // RING + 1))
                        if m >= 4:
                            who, count = taken(m - 4)
                            pe.wait_ge(S(f"{tag}_taken_{who}"), count)
                        for k in range(KD):
                            if kind == "rows":
                                last = nc.tensor.matmul(bank[m % 4][:, 0:w], HT[:, k, i * P:(i + 1) * P],
                                                        slot[:, k, 0:w], start=(k == 0), stop=(k == KD - 1))
                            else:
                                last = nc.tensor.matmul(bank[m % 4][:, 0:T], slot[:, k, i * P:(i + 1) * P],
                                                        HT[:, k, :], start=(k == 0), stop=(k == KD - 1))
                        last.then_inc(S(tag + "_filled"), 1)

                @b.scalar
                def _(act):
                    for m in range(0, len(fills), 2):
                        act.wait_ge(S(tag + "_filled"), m + 1)
                        to, frm = dst(m)
                        nc.scalar.copy(to, frm).then_inc(S(tag + "_taken_act"), 1)

                @b.vector
                def _(dve):
                    for m in range(1, len(fills), 2):
                        dve.wait_ge(S(tag + "_filled"), m + 1)
                        to, frm = dst(m)
                        nc.vector.tensor_copy(to, frm).then_inc(S(tag + "_taken_dve"), 1)
                    if extra_dve:
                        extra_dve(dve)

        def add_normed(tag, m, gain, gain_sem, junk, last_x_store=None):
            ss = STAT[:, 0:NT]
            with nc.Block() as b:
                @b.scalar
                def _(act):
                    for t in range(NT):
                        nc.scalar.activation(junk[:, t, :], m[:, t, :], ACT.Square,
                                             accum_out=ss[:, t:t + 1]).then_inc(S(tag + "_squares"), 1)

                @b.gpsimd
                def _(pool):
                    pool.wait_ge(S(tag + "_squares"), NT)
                    pool_rstd(pool, ss, 1.0 / D, NT).then_inc(S(tag + "_rstd"), 1)

                @b.vector
                def _(dve):
                    dve.wait_ge(S(tag + "_rstd"), 1)
                    dve.wait_ge(S(gain_sem), 16)
                    for t in range(NT):
                        nc.vector.scalar_tensor_tensor(m[:, t, :], m[:, t, :], ss[:, t:t + 1], gain,
                                                       ALU.mult, ALU.mult)
                    dve.drain()
                    nc.vector.tensor_tensor(X[:, :, :], X[:, :, :], m[:, :, :], ALU.add)

        def rope(dve, x1, x2, y1, y2, cos, sin, t1, t2):
            tt = nc.vector.tensor_tensor
            dve.drain()
            tt(t1, x1, cos, ALU.mult)
            tt(t2, x2, sin, ALU.mult)
            dve.drain()
            tt(y1, t1, t2, ALU.subtract)
            dve.drain()
            tt(t1, x2, cos, ALU.mult)
            tt(t2, x1, sin, ALU.mult)
            dve.drain()
            return tt(y2, t1, t2, ALU.add)

        def first_layer(l):
            Z_AT = 0
            RING_AT = Z_AT + NT * IN1
            at = RING_AT + RING * RING_N

            def take(n):
                nonlocal at
                at += n
                return at - n

            z = shaped(Z_AT, NT, IN1)
            bias_at = take(4 * NT * T)
            bias = shaped(bias_at, 4, NT, T)
            rot_c = shaped(take(NT * 6 * HD), NT, 6 * HD)
            rot_d = shaped(take(NT * 6 * HD), NT, 6 * HD)
            lat = shaped(take(NT * 384), NT, 384)
            latT = shaped(take(3 * T), 3, T)
            qb = shaped(take(NT * 384), NT, 384)
            kvb = shaped(take(NT * 512), NT, 512)
            kb = shaped(take(NT * 384), NT, 384)
            qkT_at = take(18 * T)
            qkT = shaped(qkT_at, 18, T)
            mixed_at = take(NT * D)
            mixed = shaped(mixed_at, NT, D)
            gains_at = take(8 + 4 + 384 + 4)
            post_gain_at = take(2 * D)
            w_uq = shaped(take(2 * 384), 2, 384)
            w_ukv = arena(take(512), 512)
            s_sb = shaped(take(2 * NT * T), 2, NT, T)
            p_at = take(2 * NT * T)
            p_sb = shaped(p_at, 2, NT, T)
            pT = shaped(take(2 * 2 * T), 2, 2, T)
            mla_gain = arena(gains_at + 8, 3)
            ax_gain = arena(gains_at + 12, 384)
            sink = arena(gains_at + 396, 4)
            mix_post = arena(post_gain_at, D)
            ffn_post = arena(post_gain_at + D, D)

            w_in = a["w_in"][l].rearrange("(k p) n -> p k n", p=P)
            w_out = a["w_out"][l].rearrange("(k p) n -> p k n", p=P)
            in_chunks = [("rows", n, min(512, IN1 - n), n) for n in range(0, IN1, 512)]
            out_chunks = [("rows", n, 512, n) for n in range(0, D, 512)]

            def early_loads(sp):
                for c in range(RING):
                    linear_load(sp, "in1", w_in, RING_AT, in_chunks, c)
                sp.dma_start(mla_gain, a["mla_gain"][l, :, :]).then_inc(S("prep_params"), 16)
                sp.dma_start(ax_gain, a["ax_gain"][bass.ds(l, 1), :].broadcast_to([P, 384])).then_inc(S("prep_params"), 16)
                sp.dma_start(w_uq, a["mla_w_uq"][l].rearrange("(k p) n -> p k n", p=P)).then_inc(S("prep_params"), 16)
                sp.dma_start(w_ukv, a["mla_w_ukv"][l, :, :]).then_inc(S("prep_params"), 16)
                sp.dma_start(sink, a["sw_sink"][bass.ds(l, 1), :].broadcast_to([P, 4])).then_inc(S("sink_loaded"), 16)
                sp.dma_start(mix_post, a["mix_post_gain"][bass.ds(l, 1), :].broadcast_to([P, D])
                             ).then_inc(S("mix_post_loaded"), 16)
                sp.dma_start(ffn_post, a["ffn_post_gain"][bass.ds(l, 1), :].broadcast_to([P, D])
                             ).then_inc(S("ffn_post_loaded"), 16)
                sp.dma_start(arena(bias_at, 4 * NT * T), a["rpb_rows"][l, :, :]).then_inc(S("rpb_loaded"), 16)

            norm_to_ht("pre", l, a["mix_pre_gain"], mixed_at, gains_at, qkT_at, early_loads)
            linear("in1", w_in, RING_AT, in_chunks,
                   lambda kind, t, n0, w: z[:, t, n0:n0 + w], preloaded=RING)

            ssB = STAT[:, 0:4]
            ssC = view(STAT[:, 16:28], (6, NT), (1, 6))
            sq = shaped(mixed_at, NT, 6 * HD)
            c_in = shaped(p_at, NT, 6 * HD)
            t1_at = mixed_at + 768
            t2_at = t1_at + 400
            groups = []
            for g in range(2):
                groups.append((lambda t, g=g: z[:, t, A_Q + g * P:A_Q + (g + 1) * P], P))
            for g in range(2):
                groups.append((lambda t, g=g: z[:, t, A_K + g * P:A_K + (g + 1) * P], P))
            for rot in (rot_d, rot_c):
                for g in range(3):
                    groups.append((lambda t, g=g, rot=rot: rot[:, t, g * P:(g + 1) * P], P))
            for h in range(4):
                groups.append((lambda t, h=h: qb[:, t, h * 96:(h + 1) * 96], 96))
            for h in range(4):
                groups.append((lambda t, h=h: kb[:, t, h * 96:(h + 1) * 96], 96))
            READY = [0] * 4 + [1] * 3 + [2] * 3 + [3] * 8

            with nc.Block() as b:
                @b.sync
                def _(sp):
                    for c in range(2):
                        linear_load(sp, "out1", w_out, RING_AT, out_chunks, c)

                @b.scalar
                def _(act):
                    junk = shaped(mixed_at + 1600, 256)
                    for t in range(NT):
                        nc.scalar.activation(junk, z[:, t, B_CQ:B_CQ + 256], ACT.Square,
                                             accum_out=ssB[:, t:t + 1])
                        act.drain()
                        nc.scalar.activation(junk[:, 0:128], z[:, t, B_CKV:B_CKV + 128], ACT.Square,
                                             accum_out=ssB[:, 2 + t:3 + t])
                        act.drain()
                    act.sem_inc(S("lat_squares"), 1)
                    act.wait_ge(S("prep_params"), 64)
                    for i in range(3):
                        act.wait_ge(S("lat_turned"), i + 1)
                        nc.scalar.mul(latT[:, i, :], bank[i][:, 0:T], mla_gain[:, i:i + 1]
                                      ).then_inc(S("latT_ready"), 1)
                    for t in range(NT):
                        act.wait_ge(S("lat_up"), 2 * t + 1)
                        nc.scalar.copy(qb[:, t, :], bank[4 + t][:, 0:384])
                        act.wait_ge(S("lat_up"), 2 * t + 2)
                        nc.scalar.copy(kvb[:, t, :], bank[6 + t][:, :]).then_inc(S("up_ready"), 1)
                    for g in range(0, 18, 2):
                        act.wait_ge(S("qk_turned"), g + 1)
                        n = groups[g][1]
                        nc.scalar.copy(qkT[0:n, g, :], bank[g % 4][0:n, 0:T]).then_inc(S("qk_out_even"), 1)

                @b.gpsimd
                def _(pool):
                    pool.wait_ge(S("rpb_loaded"), 16)
                    for h in range(4):
                        nc.gpsimd.tensor_tensor(bias[:, h, :, :], bias[:, h, :, :],
                                                const("mask_na", (T, NT), (1, T)), ALU.add)
                    pool.wait_ge(S("lat_squares"), 1)
                    nc.gpsimd.tensor_scalar(ssB[:, 0:2], ssB[:, 0:2], 1.0 / 256, EPS, ALU.mult, ALU.add)
                    nc.gpsimd.tensor_scalar(ssB[:, 2:4], ssB[:, 2:4], 1.0 / 128, EPS, ALU.mult, ALU.add)
                    pool.drain()
                    nc.gpsimd.tensor_tensor(ssB, ssB, HALF[:, 0:4], ALU.pow).then_inc(S("lat_rstd"), 1)
                    pool.wait_ge(S("ax_squares"), 1)
                    pool_rstd(pool, STAT[:, 16:28], 1.0 / HD, 12).then_inc(S("ax_rstd"), 1)

                @b.vector
                def _(dve):
                    tt = nc.vector.tensor_tensor
                    cqk = z[:, :, C_Q:C_Q + 384]
                    tt(sq, cqk, cqk, ALU.mult)
                    dve.drain()
                    nc.vector.reduce_sum(ssC, view(sq, (384, NT), (HD, 6), (1, HD)), AX
                                         ).then_inc(S("ax_squares"), 1)
                    dve.wait_ge(S("lat_rstd"), 1)
                    for t in range(NT):
                        nc.vector.tensor_scalar(lat[:, t, 0:256], z[:, t, B_CQ:B_CQ + 256], ssB[:, t:t + 1],
                                                None, ALU.mult)
                        nc.vector.tensor_scalar(lat[:, t, 256:384], z[:, t, B_CKV:B_CKV + 128],
                                                ssB[:, 2 + t:3 + t], None, ALU.mult).then_inc(S("lat_ready"), 1)
                    def half(src, stride, base, heads, width, w):
                        return view(src[:, 0:1, base:base + 1], (stride, NT), (width, heads), (1, w))
                    def tmp(base, heads, w):
                        return view(arena(base, 400), (heads * w, NT), (w, heads), (1, w))
                    def angle(name, heads, w):
                        return const(name, (w, NT), (0, heads), (1, w))
                    pairs = ((0, 2 * HD), (HD, 2 * HD), (4 * HD, HD))
                    for g, (c0, step) in enumerate(pairs):
                        rope(dve, half(z, IN1, D_Q + c0, 2, step, 32), half(z, IN1, D_Q + c0 + 32, 2, step, 32),
                             half(rot_d, 384, g * P, 2, HD, 32), half(rot_d, 384, g * P + 32, 2, HD, 32),
                             angle("cos_full", 2, 32), angle("sin_full", 2, 32),
                             tmp(t1_at, 2, 32), tmp(t2_at, 2, 32))
                    dve.drain()
                    dve.sem_inc(S("qk_source"), 1)
                    dve.wait_ge(S("ax_rstd"), 1)
                    dve.wait_ge(S("prep_params"), 64)
                    c3 = view(cqk, (IN1, NT), (HD, 6), (1, HD))
                    tt(view(sq, (384, NT), (HD, 6), (1, HD)), c3, view(ssC, (6, NT), (1, 6), (0, HD)), ALU.mult)
                    dve.drain()
                    for g, (c0, step) in enumerate(pairs):
                        tt(half(c_in, 384, g * P, 2, HD, HD), half(sq, 384, c0, 2, step, HD),
                           view(ax_gain, (0, NT), (step, 2), (1, HD), off=c0), ALU.mult)
                    for base, ang in ((0, "row"), (32, "col")):
                        rope(dve, half(c_in, 384, base, 6, HD, 16), half(c_in, 384, base + 16, 6, HD, 16),
                             half(rot_c, 384, base, 6, HD, 16), half(rot_c, 384, base + 16, 6, HD, 16),
                             angle("cos_" + ang, 6, 16), angle("sin_" + ang, 6, 16),
                             tmp(t1_at, 6, 16), tmp(t2_at, 6, 16))
                    dve.drain()
                    dve.sem_inc(S("qk_source"), 1)
                    dve.wait_ge(S("up_ready"), NT)
                    rope(dve, half(qb, 384, 64, 4, 96, 16), half(qb, 384, 80, 4, 96, 16),
                         half(sq, 384, 0, 4, 32, 16), half(sq, 384, 16, 4, 32, 16),
                         angle("cos_mla", 4, 16), angle("sin_mla", 4, 16), tmp(t1_at, 4, 16), tmp(t2_at, 4, 16))
                    dve.drain()
                    nc.vector.tensor_copy(half(qb, 384, 64, 4, 96, 32), half(sq, 384, 0, 4, 32, 32))
                    rope(dve, half(z, IN1, B_KR, 1, 32, 16), half(z, IN1, B_KR + 16, 1, 32, 16),
                         half(sq, 384, 128, 1, 32, 16), half(sq, 384, 144, 1, 32, 16),
                         angle("cos_mla", 1, 16), angle("sin_mla", 1, 16), tmp(t1_at, 1, 16), tmp(t2_at, 1, 16))
                    dve.drain()
                    nc.vector.tensor_copy(half(kb, 384, 64, 4, 96, 32), view(sq[:, 0:1, 128:129], (384, NT), (0, 4), (1, 32)))
                    nc.vector.tensor_copy(half(kb, 384, 0, 4, 96, HD), half(kvb, 512, 0, 4, P, HD)
                                          )
                    dve.drain()
                    dve.sem_inc(S("qk_source"), 1)
                    for g in range(1, 18, 2):
                        dve.wait_ge(S("qk_turned"), g + 1)
                        n = groups[g][1]
                        nc.vector.tensor_copy(qkT[0:n, g, :], bank[g % 4][0:n, 0:T]).then_inc(S("qk_out_odd"), 1)

                @b.tensor
                def _(pe):
                    pe.wait_ge(S("lat_ready"), NT)
                    for i in range(3):
                        for t in range(NT):
                            last = nc.tensor.transpose(bank[i][:, t * P:(t + 1) * P],
                                                       lat[:, t, i * P:(i + 1) * P], ident)
                        last.then_inc(S("lat_turned"), 1)
                    pe.wait_ge(S("prep_params"), 64)
                    pe.wait_ge(S("latT_ready"), 3)
                    for t in range(NT):
                        for k in range(2):
                            last = nc.tensor.matmul(bank[4 + t][:, 0:384], latT[:, k, t * P:(t + 1) * P],
                                                    w_uq[:, k, :], start=(k == 0), stop=(k == 1))
                        last.then_inc(S("lat_up"), 1)
                        nc.tensor.matmul(bank[6 + t][:, :], latT[:, 2, t * P:(t + 1) * P], w_ukv,
                                         start=True, stop=True).then_inc(S("lat_up"), 1)
                    for g, (src, n) in enumerate(groups):
                        if READY[g]:
                            pe.wait_ge(S("qk_source"), READY[g])
                        if g >= 4:
                            pe.wait_ge(S("qk_out_odd" if g % 2 else "qk_out_even"), (g - 4) // 2 + 1)
                        for t in range(NT):
                            last = nc.tensor.transpose(bank[g % 4][0:n, t * P:(t + 1) * P], src(t), ident)
                        last.then_inc(S("qk_turned"), 1)

            heads = []
            for h in range(4):
                p0 = (h % 2) * HD
                heads.append(("na", qkT[p0:p0 + HD, h // 2, :], qkT[p0:p0 + HD, 2 + h // 2, :],
                              lambda t, h=h: z[:, t, A_V + h * HD:A_V + (h + 1) * HD], h * HD, h))
            for h in range(4):
                heads.append(("mla", qkT[0:96, 10 + h, :], qkT[0:96, 14 + h, :],
                              lambda t, h=h: kvb[:, t, h * P + HD:(h + 1) * P], 256 + h * HD, h))
            for kind, g0, v0, o0 in (("ax", 7, C_V, 512), ("sw", 4, D_V, 768)):
                for h in range(4):
                    p0 = (h // 2) * HD
                    heads.append((kind, qkT[p0:p0 + HD, g0 + h % 2, :], qkT[p0:p0 + HD, g0 + 2, :],
                                  lambda t, h=h, v0=v0: z[:, t, v0 + h // 2 * HD:v0 + (h // 2 + 1) * HD],
                                  o0 + h * HD, h))
            NHD = len(heads)
            nmax = view(STAT[:, 32:64], (2, NHD), (1, 2))
            sums = view(STAT[:, 64:96], (2, NHD), (1, 2))
            sinke = view(STAT[:, 96:104], (2, 4), (1, 2))
            nsink = STAT[:, 104:108]
            scale_of = {"na": HD ** -0.5, "mla": 96 ** -0.5, "ax": HD ** -0.5, "sw": HD ** -0.5}

            with nc.Block() as b:
                @b.tensor
                def _(pe):
                    def scores(h):
                        if h >= 2:
                            pe.wait_ge(S("att_scaled"), h - 1)
                        _, qT, kT, _, _, _ = heads[h]
                        for t in range(NT):
                            last = nc.tensor.matmul(bank[h % 2][:, t * T:(t + 1) * T], qT[:, t * P:(t + 1) * P],
                                                    kT, start=True, stop=True)
                        last.then_inc(S("att_scores"), 1)

                    def turn(h):
                        pe.wait_ge(S("att_probs"), h + 1)
                        if h >= 2:
                            pe.wait_ge(S("att_probsT"), h - 1)
                        for t in range(NT):
                            for k in range(2):
                                last = nc.tensor.transpose(bank[2 + h % 2][:, k * T + t * P:k * T + (t + 1) * P],
                                                           p_sb[:, h % 2, t, k * P:(k + 1) * P], ident)
                        last.then_inc(S("att_turned"), 1)

                    def values(h):
                        pe.wait_ge(S("att_probsT"), h + 1)
                        if h >= 2:
                            pe.wait_ge(S("att_out"), h - 1)
                        v = heads[h][3]
                        for t in range(NT):
                            for k in range(2):
                                last = nc.tensor.matmul(bank[4 + h % 2][:, t * HD:(t + 1) * HD],
                                                        pT[:, h % 2, k, t * P:(t + 1) * P], v(k),
                                                        start=(k == 0), stop=(k == 1))
                        last.then_inc(S("att_values"), 1)

                    scores(0)
                    scores(1)
                    for h in range(NHD):
                        turn(h)
                        if h + 2 < NHD:
                            scores(h + 2)
                        values(h)

                @b.vector
                def _(dve):
                    def scaled(h):
                        kind, _, _, _, _, i = heads[h]
                        dve.wait_ge(S("att_scores"), h + 1)
                        if h >= 2:
                            dve.wait_ge(S("att_exp"), h - 1)
                        s = s_sb[:, h % 2, :, :]
                        frm = view(bank[h % 2][:, :], (T, NT), (1, T))
                        sc = scale_of[kind]
                        if kind in ("na", "sw"):
                            add = bias[:, i, :, :] if kind == "na" else const("mask_sw", (T, NT), (1, T))
                            nc.vector.scalar_tensor_tensor(s, frm, sc, add, ALU.mult, ALU.add
                                                           ).then_inc(S("att_scaled"), 1)
                        else:
                            nc.vector.tensor_scalar(s, frm, sc, None, ALU.mult).then_inc(S("att_scaled"), 1)
                        dve.drain()
                        last = nc.vector.tensor_reduce(nmax[:, h, :], s, AX, ALU.max, negate=True)
                        if kind == "sw":
                            dve.drain()
                            last = nc.vector.tensor_scalar(nmax[:, h, :], nmax[:, h, :], nsink[:, i:i + 1], None,
                                                           ALU.min)
                        last.then_inc(S("att_max"), 1)

                    def normalised(h):
                        kind, _, _, _, _, i = heads[h]
                        dve.wait_ge(S("att_exp"), h + 1)
                        if kind == "sw":
                            nc.vector.tensor_tensor(sums[:, h, :], sums[:, h, :], sinke[:, i, :], ALU.add)
                            dve.drain()
                        nc.vector.reciprocal(sums[:, h, :], sums[:, h, :])
                        dve.drain()
                        for t in range(NT):
                            last = nc.vector.tensor_scalar(p_sb[:, h % 2, t, :], p_sb[:, h % 2, t, :],
                                                           sums[:, h, t:t + 1], None, ALU.mult)
                        last.then_inc(S("att_probs"), 1)

                    def store(h):
                        dve.wait_ge(S("att_values"), h + 1)
                        o = heads[h][4]
                        nc.vector.tensor_copy(mixed[:, :, o:o + HD], view(bank[4 + h % 2][:, 0:1], (HD, NT), (1, HD))
                                              ).then_inc(S("att_out"), 1)

                    dve.wait_ge(S("sink_loaded"), 16)
                    nc.vector.tensor_scalar(nsink, sink, -1.0, None, ALU.mult)
                    scaled(0)
                    for h in range(NHD):
                        if h + 1 < NHD:
                            scaled(h + 1)
                        normalised(h)
                        if h >= 1:
                            store(h - 1)
                    store(NHD - 1)

                @b.scalar
                def _(act):
                    def exps(h):
                        kind, _, _, _, _, i = heads[h]
                        act.wait_ge(S("att_max"), h + 1)
                        if h >= 2:
                            act.wait_ge(S("att_turned"), h - 1)
                        if kind == "sw":
                            nc.scalar.activation(sinke[:, i, :], nmax[:, h, :], ACT.Exp, bias=sink[:, i:i + 1])
                        for t in range(NT):
                            last = nc.scalar.activation(p_sb[:, h % 2, t, :], s_sb[:, h % 2, t, :], ACT.Exp,
                                                        bias=nmax[:, h, t:t + 1], accum_out=sums[:, h, t:t + 1])
                        last.then_inc(S("att_exp"), 1)

                    def out_turned(h):
                        act.wait_ge(S("att_turned"), h + 1)
                        if h >= 2:
                            act.wait_ge(S("att_values"), h - 1)
                        nc.scalar.copy(pT[:, h % 2, :, :], view(bank[2 + h % 2][:, :], (T, 2), (1, T))
                                       ).then_inc(S("att_probsT"), 1)

                    exps(0)
                    for h in range(NHD):
                        if h + 1 < NHD:
                            exps(h + 1)
                        out_turned(h)

            turn_to_ht("mixT", mixed)
            m = shaped(mixed_at, NT, D)
            linear("out1", w_out, RING_AT, out_chunks,
                   lambda kind, t, n0, w: m[:, t, n0:n0 + w], preloaded=2)
            add_normed("mix_post", m, mix_post, "mix_post_loaded", shaped(qkT_at, NT, D))

            up_ring = [shaped(RING_AT + s * 2048, 2, KD, P) for s in range(2)]
            down_ring = [arena(RING_AT + 4096 + s * 1024, D) for s in range(2)]
            us = [shaped(RING_AT + 6144 + s * 512, 2, T) for s in range(2)]
            cc = [shaped(RING_AT + 7168 + s * 512, 2, T) for s in range(2)]
            ge = [arena(RING_AT + 8192 + s * T, T) for s in range(2)]
            gg = [arena(RING_AT + 8704 + s * T, T) for s in range(2)]
            conv = shaped(RING_AT + 9216, NF, 8)
            w_up = a["w_up_tiles"]
            w_down = a["w_down"]

            def load_up(sp, j, s):
                sp.dma_start(arena(RING_AT + s * 2048, 2048), w_up[l, j, :, :]).then_inc(S(f"up_loaded{s}"), 16)

            def load_down(sp, j, s):
                sp.dma_start(down_ring[s], w_down[l, bass.ds(j * P, P), :]).then_inc(S(f"down_loaded{s}"), 16)

            def ffn_early(sp):
                sp.dma_start(arena(RING_AT + 9216, NF * 8), a["conv_params"][l, :, :]).then_inc(S("conv_loaded"), 16)
                for s in range(2):
                    load_up(sp, s, s)
                    load_down(sp, s, s)

            norm_to_ht("ffn", l, a["ffn_pre_gain"], mixed_at, gains_at, qkT_at, ffn_early)
            with nc.Block() as b:
                @b.sync
                def _(sp):
                    with sp.Fori(1, NF // 2) as it:
                        for s in range(2):
                            j = it * 2 + s
                            sp.wait_ge(S("up_done"), it * 2 + (s - 1))
                            load_up(sp, j, s)
                            sp.wait_ge(S("down_done"), it * 2 + (s + 1))
                            load_down(sp, j, s)

                @b.tensor
                def _(pe):
                    pe.sem_inc(S("down_done"), 2)
                    for y in range(4):
                        nc.tensor.matmul(bank[y][:, :], ZERO[:, 0:P], ZERO[:, :], start=True, stop=False,
                                         skip_group_check=True)

                    def up(s, turn, j):
                        pe.wait_ge(S(f"up_loaded{s}"), turn)
                        pe.wait_ge(S("ubank_free"), j)
                        for side in range(2):
                            for k in range(KD):
                                last = nc.tensor.matmul(bank[4 + s][:, side * T:(side + 1) * T],
                                                        up_ring[s][:, side, k, :], HT[:, k, :],
                                                        start=(k == 0), stop=(k == KD - 1), skip_group_check=True)
                        last.then_inc(S("up_done"), 1)

                    def down(s, turn, j, stop=False):
                        pe.wait_ge(S(f"down_loaded{s}"), turn)
                        pe.wait_ge(S("g_ready"), j)
                        for t in range(NT):
                            for n in range(2):
                                last = nc.tensor.matmul(bank[2 * t + n][:, :], gg[s][:, t * P:(t + 1) * P],
                                                        down_ring[s][:, n * 512:(n + 1) * 512],
                                                        start=False, stop=stop, skip_group_check=True)
                        last.then_inc(S("down_done"), 1)

                    up(0, 16, 1)
                    with pe.Fori(0, NF // 2 - 1) as it:
                        up(1, it * 16 + 16, it * 2 + 2)
                        down(0, it * 16 + 16, it * 2 + 1)
                        up(0, it * 16 + 32, it * 2 + 3)
                        down(1, it * 16 + 16, it * 2 + 2)
                    up(1, 8 * NF, NF)
                    down(0, 8 * NF, NF - 1)
                    down(1, 8 * NF, NF, stop=True)

                @b.scalar
                def _(act):
                    act.sem_inc(S("ubank_free"), 2)
                    with act.Fori(0, NF // 2) as it:
                        for s in range(2):
                            act.wait_ge(S("up_done"), it * 2 + (s + 1))
                            act.wait_ge(S("us_free"), it * 2 + (s + 1))
                            nc.scalar.copy(us[s], view(bank[4 + s][:, :], (T, 2), (1, T))
                                           ).then_inc(S("ubank_free"), 1)
                            act.wait_ge(S("conv_ready"), it * 2 + (s + 1))
                            nc.scalar.activation(ge[s], cc[s][:, 0, :], ACT.Gelu_apprx_tanh
                                                 ).then_inc(S("gelu_ready"), 1)
                    for t in range(NT):
                        act.wait_ge(S("down_done"), NF + 2)
                        nc.scalar.copy(m[:, t, 0:512], bank[2 * t][:, :])

                @b.vector
                def _(dve):
                    dve.sem_inc(S("us_free"), 2)
                    dve.wait_ge(S("conv_loaded"), 16)
                    with dve.Fori(0, NF // 2) as it:
                        for s in range(2):
                            def w(i):
                                return conv[:, bass.ds(it * 2 + s, 1), i]
                            dve.wait_ge(S("ubank_free"), it * 2 + (s + 3))
                            for side in range(2):
                                u, c, o = us[s][:, side, :], cc[s][:, side, :], 4 * side
                                nc.vector.tensor_scalar(c, u, w(o + 1), w(o + 3), ALU.mult, ALU.add)
                            dve.drain()
                            for side in range(2):
                                u, c, o = us[s][:, side, :], cc[s][:, side, :], 4 * side
                                nc.vector.scalar_tensor_tensor(c[:, 1:T], u[:, 0:T - 1], w(o), c[:, 1:T],
                                                               ALU.mult, ALU.add)
                            dve.drain()
                            for side in range(2):
                                u, c, o = us[s][:, side, :], cc[s][:, side, :], 4 * side
                                last = nc.vector.scalar_tensor_tensor(c[:, 0:T - 1], u[:, 1:T], w(o + 2),
                                                                      c[:, 0:T - 1], ALU.mult, ALU.add)
                            last.then_inc(S("conv_ready"), 1)
                            dve.drain()
                            dve.sem_inc(S("us_free"), 1)
                            dve.wait_ge(S("gelu_ready"), it * 2 + (s + 1))
                            dve.wait_ge(S("down_done"), it * 2 + (s + 1))
                            nc.vector.tensor_tensor(gg[s], ge[s], cc[s][:, 1, :], ALU.mult
                                                    ).then_inc(S("g_ready"), 1)
                    for t in range(NT):
                        dve.wait_ge(S("down_done"), NF + 2)
                        nc.vector.tensor_copy(m[:, t, 512:D], bank[2 * t + 1][:, :])
            add_normed("ffn_post", m, ffn_post, "ffn_post_loaded", shaped(qkT_at, NT, D))
            clear_all()

        def second_layer(l):
            at = 0

            def take(n):
                nonlocal at
                at += n
                return at - n

            z = shaped(take(NT * Z2), NT, Z2)
            RING_AT = take(RING * RING_N)
            qkc_at = take(6 * T)
            qkc = shaped(qkc_at, 6, T)
            qkm = shaped(take(6 * T), 6, T)
            sgm = shaped(take(6 * T), 6, T)
            sbT = shaped(take(6 * T), 6, T)
            sq_at = take(NT * D)
            ycat = shaped(take(NT * D), NT, D)
            xn_at = take(NT * D)
            vaug = shaped(take(NT * NH6 * 65), NT, NH6, 65)
            sgw = shaped(take(SGG * P), SGG, P)
            uv = shaped(take(NT * 512), NT, 512)
            og = shaped(take(NT * 384), NT, 384)
            gain_at = take(16)
            sbg = arena(take(768), 768)
            svg = arena(take(256), 256)
            outg = arena(take(D), D)
            conv = shaped(take(32), 6, 5)
            ifb = arena(take(2), 2)
            sgb = arena(take(4), 4)
            row_at = take(8 * T)
            work_at = take(8 * 512)

            def row(i):
                return ARENA[0:NH6, row_at + i * T:row_at + (i + 1) * T]

            w_in = a["w_in_2"][l].rearrange("(k p) n -> p k n", p=P)
            w_out = a["w_out_2"][l].rearrange("(k p) n -> p k n", p=P)
            in_chunks = [("rows", 0, 512, 0), ("rows", 512, 512, 512), ("rows", 1024, 128, 1024),
                         ("turned", 1152, 384, 0), ("turned", 1536, 384, 3),
                         ("rows", 1920, 512, 1152), ("rows", 2432, 512, 1664), ("rows", 2944, 268, 2176)]
            out_chunks = [("rows", n, 512, n) for n in range(0, D, 512)]

            def early_loads(sp):
                for c in range(RING):
                    linear_load(sp, "in2", w_in, RING_AT, in_chunks, c)
                one = lambda name, n: a[name][bass.ds(l, 1), :].broadcast_to([P, n])
                sp.dma_start(sbg, one("sb_gain", 768)).then_inc(S("mix2_params"), 16)
                sp.dma_start(svg, one("sg_vn_g_2", 256)).then_inc(S("mix2_params"), 16)
                sp.dma_start(outg, one("out_g_2", D)).then_inc(S("mix2_params"), 16)
                sp.dma_start(conv, a["ml_conv"][l]).then_inc(S("mix2_params"), 16)
                sp.dma_start(ifb[0:NH6, :], a["ml_if_b"][l, :, :]).then_inc(S("mix2_params"), 16)
                sp.dma_start(sgb, a["sg_b_t"][l, :, :]).then_inc(S("mix2_params"), 16)
                sp.dma_start(sgw, a["sg_w_t"][l]).then_inc(S("mix2_params"), 16)
            N_PARAMS = 7 * 16

            def pick(kind, t, n0, w):
                return z[:, t, n0:n0 + w] if kind == "rows" else qkc[:, t, :]

            norm_to_ht("pre", l, a["norm1_g_2"], xn_at, gain_at, sq_at, early_loads)
            linear("in2", w_in, RING_AT, in_chunks, pick, preloaded=RING)

            sbqk = view(z[:, 0:1, 0:1], (Z2, NT), (HD, 12), (1, HD))
            sq12 = view(arena(sq_at, 1), (768, NT), (HD, 12), (1, HD))
            sqf = view(arena(sq_at, 1), (768, NT), (1, 768))
            ss12 = view(STAT[:, 0:24], (12, NT), (1, 12))
            ss4 = view(STAT[:, 32:40], (4, NT), (1, 4))
            vsq = view(arena(xn_at, 1), (256, NT), (HD, 4), (1, HD))
            uvv = view(uv[:, 0:1, 256:257], (512, NT), (HD, 4), (1, HD))
            acol = view(STAT[:, 64:76], (6, NT), (1, 6))
            ecol = view(STAT[:, 80:92], (6, NT), (1, 6))
            with nc.Block() as b:
                @b.sync
                def _(sp):
                    for c in range(2):
                        linear_load(sp, "out2", w_out, RING_AT, out_chunks, c)

                @b.scalar
                def _(act):
                    nc.scalar.activation(uv, z[:, :, SG_UV:SG_UV + 512], ACT.Gelu_apprx_tanh
                                         ).then_inc(S("uv_gelu"), 1)
                    nc.scalar.activation(og, z[:, :, ML_O:ML_O + 384], ACT.Sigmoid).then_inc(S("og_ready"), 1)
                    act.wait_ge(S("ml_conv_ready"), 1)
                    nc.scalar.activation(sgm, qkm, ACT.Sigmoid).then_inc(S("ml_sigmoid"), 1)
                    act.wait_ge(S("f_ready"), 1)
                    nc.scalar.activation(row(2), row(1), ACT.Abs)
                    act.drain()
                    nc.scalar.activation(row(2), row(2), ACT.Exp, scale=-1.0)
                    act.drain()
                    nc.scalar.activation(row(2), row(2), ACT.Ln, bias=1.0).then_inc(S("f_log"), 1)
                    act.wait_ge(S("m_ready"), 1)
                    nc.scalar.activation(row(6), row(6), ACT.Exp, scale=-1.0).then_inc(S("em_ready"), 1)
                    for g in range(6):
                        act.wait_ge(S("sb_turned"), g + 1)
                        nc.scalar.copy(sbT[:, g, :], bank[g % 2][:, 0:T]).then_inc(S("sbT_out"), 1)

                @b.gpsimd
                def _(pool):
                    pool.wait_ge(S("mix2_params"), N_PARAMS)
                    nc.gpsimd.tensor_tensor(sgw, sgw, const("tril_t", (0, SGG), (1, P)), ALU.mult)
                    pool.wait_ge(S("sb_squares"), 1)
                    pool_rstd(pool, STAT[:, 0:24], 1.0 / HD, 24).then_inc(S("sb_rstd"), 1)
                    pool.wait_ge(S("sgv_squares"), 1)
                    pool_rstd(pool, STAT[:, 32:40], 1.0 / HD, 8).then_inc(S("sgv_rstd"), 1)
                    nc.gpsimd.memset(vaug, 1.0)
                    pool.drain()
                    nc.gpsimd.tensor_copy(vaug[:, :, :, 0:HD],
                                          view(z[:, 0:1, ML_V:ML_V + 1], (Z2, NT), (HD, NH6), (1, HD)))

                @b.vector
                def _(dve):
                    tt = nc.vector.tensor_tensor
                    tt(sq12, sbqk, sbqk, ALU.mult)
                    dve.drain()
                    nc.vector.reduce_sum(ss12, sq12, AX).then_inc(S("sb_squares"), 1)
                    dve.wait_ge(S("if_turned"), 1)
                    dve.wait_ge(S("mix2_params"), N_PARAMS)
                    nc.vector.tensor_scalar(row(0), bank[7][0:NH6, 0:T], ifb[0:NH6, 0:1], None, ALU.add)
                    nc.vector.tensor_scalar(row(1), bank[7][0:NH6, T:2 * T], ifb[0:NH6, 1:2], None, ALU.add
                                            ).then_inc(S("f_ready"), 1)
                    for f in range(6):
                        nc.vector.tensor_scalar(qkm[:, f, :], qkc[:, f, :], conv[:, f, 3:4], conv[:, f, 4:5],
                                                ALU.mult, ALU.add)
                    for j in range(3):
                        dve.drain()
                        sh = 3 - j
                        for f in range(6):
                            last = nc.vector.scalar_tensor_tensor(
                                qkm[:, f, sh:T], qkc[:, f, 0:T - sh], conv[:, f, j:j + 1], qkm[:, f, sh:T],
                                ALU.mult, ALU.add)
                    last.then_inc(S("ml_conv_ready"), 1)
                    dve.wait_ge(S("sb_rstd"), 1)
                    tt(sq12, sbqk, view(ss12, (12, NT), (1, 12), (0, HD)), ALU.mult)
                    dve.drain()
                    tt(sqf, sqf, view(sbg, (0, NT), (1, 768)), ALU.mult).then_inc(S("sb_ready"), 1)
                    dve.wait_ge(S("f_log"), 1)
                    nc.vector.scalar_tensor_tensor(row(3), row(1), 0.0, row(2), ALU.min, ALU.subtract)
                    nc.vector.memset(row(7), 1.0)
                    dve.drain()
                    nc.vector.tensor_tensor_scan(row(4), row(7), row(3), 0.0, ALU.mult, ALU.add)
                    dve.drain()
                    tt(row(0), row(0), row(4), ALU.subtract)
                    nc.vector.memset(row(7), 0.0)
                    dve.drain()
                    nc.vector.tensor_tensor_scan(row(5), row(7), row(0), 0.0, ALU.max, ALU.max)
                    dve.drain()
                    tt(row(6), row(4), row(5), ALU.add).then_inc(S("m_ready"), 1)
                    dve.wait_ge(S("ml_sigmoid"), 1)
                    tt(qkm, qkm, sgm, ALU.mult)
                    dve.wait_ge(S("uv_gelu"), 1)
                    tt(vsq, uvv, uvv, ALU.mult)
                    dve.drain()
                    nc.vector.reduce_sum(ss4, vsq, AX).then_inc(S("sgv_squares"), 1)
                    dve.wait_ge(S("sgv_rstd"), 1)
                    tt(uvv, uvv, view(ss4, (4, NT), (1, 4), (0, HD)), ALU.mult)
                    dve.drain()
                    uvf = view(uv[:, 0:1, 256:257], (512, NT), (1, 256))
                    tt(uvf, uvf, view(svg, (0, NT), (1, 256)), ALU.mult)
                    dve.wait_ge(S("cols_turned"), 1)
                    nc.vector.tensor_copy(acol, view(bank[6][:, 0:1], (6, NT), (1, 6)))
                    nc.vector.tensor_copy(ecol, view(bank[6][:, 16:17], (6, NT), (1, 6)))

                @b.tensor
                def _(pe):
                    for side in range(2):
                        for t in range(NT):
                            last = nc.tensor.transpose(bank[7][0:NH6, side * T + t * P:side * T + (t + 1) * P],
                                                       z[:, t, ML_IF + side * NH6:ML_IF + (side + 1) * NH6], ident)
                    last.then_inc(S("if_turned"), 1)
                    pe.wait_ge(S("sb_ready"), 1)
                    for g in range(6):
                        if g >= 2:
                            pe.wait_ge(S("sbT_out"), g - 1)
                        for t in range(NT):
                            last = nc.tensor.transpose(bank[g % 2][:, t * P:(t + 1) * P],
                                                       sqf[:, t, g * P:(g + 1) * P], ident)
                        last.then_inc(S("sb_turned"), 1)
                    pe.wait_ge(S("em_ready"), 1)
                    id6 = ident[0:NH6, 0:NH6]
                    for t in range(NT):
                        nc.tensor.transpose(bank[6][:, t * 6:t * 6 + 6], row(0)[:, t * P:(t + 1) * P], id6)
                    for t in range(NT):
                        last = nc.tensor.transpose(bank[6][:, 16 + t * 6:22 + t * 6],
                                                   row(6)[:, t * P:(t + 1) * P], id6)
                    last.then_inc(S("cols_turned"), 1)

            zs = [shaped(work_at + i * 512, 2, T) for i in range(2)]
            lg = [shaped(work_at + 1024 + i * 512, 2, T) for i in range(2)]
            sp_ = [shaped(work_at + 2048 + i * 512, 2, T) for i in range(2)]
            wt = [shaped(work_at + 3072 + i * 512, 2, T) for i in range(2)]
            two = lambda bk: view(bk[:, :], (T, 2), (1, T))
            with nc.Block() as b:
                @b.tensor
                def _(pe):
                    def scores(h):
                        if h >= 2:
                            pe.wait_ge(S("sb_scaled"), h - 1)
                        p0 = (h % 2) * HD
                        qT, kT = sbT[p0:p0 + HD, h // 2, :], sbT[p0:p0 + HD, 3 + h // 2, :]
                        for k in range(2):
                            last = nc.tensor.matmul(bank[h % 2][:, k * T:(k + 1) * T], kT[:, k * P:(k + 1) * P],
                                                    qT, start=True, stop=True)
                        last.then_inc(S("sb_scores"), 1)

                    scores(0)
                    for h in range(NH6):
                        if h + 1 < NH6:
                            scores(h + 1)
                        pe.wait_ge(S("sb_soft"), h + 1)
                        if h >= 2:
                            pe.wait_ge(S("sb_arg"), h - 1)
                        sfx = bank[2 + h % 2]
                        nc.tensor.matmul(sfx[:, 0:T], const("suffix"), sp_[h % 2][:, 0, :], start=True, stop=False)
                        nc.tensor.matmul(sfx[:, 0:T], const("ones"), sp_[h % 2][:, 1, :], start=False, stop=True)
                        nc.tensor.matmul(sfx[:, T:2 * T], const("suffix"), sp_[h % 2][:, 1, :], start=True, stop=True
                                         ).then_inc(S("sb_suffix"), 1)
                        pe.wait_ge(S("sb_weight"), h + 1)
                        if h >= 2:
                            pe.wait_ge(S("sb_out"), h - 1)
                        for t in range(NT):
                            for k in range(t + 1):
                                last = nc.tensor.matmul(bank[4 + h % 2][:, t * HD:(t + 1) * HD],
                                                        wt[h % 2][:, k, t * P:(t + 1) * P],
                                                        z[:, k, SB_V + h * HD:SB_V + (h + 1) * HD],
                                                        start=(k == 0), stop=(k == t))
                        last.then_inc(S("sb_values"), 1)

                @b.vector
                def _(dve):
                    def scaled(h):
                        dve.wait_ge(S("sb_scores"), h + 1)
                        if h >= 2:
                            dve.wait_ge(S("sb_masked"), h - 1)
                        nc.vector.tensor_scalar(zs[h % 2], two(bank[h % 2]), HD ** -0.5, None, ALU.mult
                                                ).then_inc(S("sb_scaled"), 1)
                    scaled(0)
                    for h in range(NH6):
                        dve.wait_ge(S("sb_log"), h + 1)
                        nc.vector.scalar_tensor_tensor(lg[h % 2], zs[h % 2], 0.0, lg[h % 2], ALU.max, ALU.add)
                        dve.drain()
                        nc.vector.tensor_tensor(sp_[h % 2], lg[h % 2], const("strict01", (T, 2), (1, T)), ALU.mult
                                                ).then_inc(S("sb_soft"), 1)
                        if h + 1 < NH6:
                            scaled(h + 1)
                        dve.wait_ge(S("sb_suffix"), h + 1)
                        dve.wait_ge(S("sb_masked"), h + 1)
                        nc.vector.tensor_tensor(lg[h % 2], two(bank[2 + h % 2]), zs[h % 2], ALU.subtract
                                                ).then_inc(S("sb_arg"), 1)
                        dve.wait_ge(S("sb_values"), h + 1)
                        nc.vector.tensor_copy(ycat[:, :, h * HD:(h + 1) * HD],
                                              view(bank[4 + h % 2][:, 0:1], (HD, NT), (1, HD))
                                              ).then_inc(S("sb_out"), 1)

                @b.gpsimd
                def _(pool):
                    for h in range(NH6):
                        pool.wait_ge(S("sb_soft"), h + 1)
                        nc.gpsimd.tensor_tensor(zs[h % 2], zs[h % 2], const("strict_big", (T, 2), (1, T)),
                                                ALU.subtract).then_inc(S("sb_masked"), 1)

                @b.scalar
                def _(act):
                    def logs(h):
                        act.wait_ge(S("sb_scaled"), h + 1)
                        nc.scalar.activation(lg[h % 2], zs[h % 2], ACT.Abs)
                        act.drain()
                        nc.scalar.activation(lg[h % 2], lg[h % 2], ACT.Exp, scale=-1.0)
                        act.drain()
                        nc.scalar.activation(lg[h % 2], lg[h % 2], ACT.Ln, bias=1.0).then_inc(S("sb_log"), 1)
                    logs(0)
                    for h in range(NH6):
                        act.wait_ge(S("sb_arg"), h + 1)
                        nc.scalar.activation(wt[h % 2], lg[h % 2], ACT.Exp, scale=-1.0
                                             ).then_inc(S("sb_weight"), 1)
                        if h + 1 < NH6:
                            logs(h + 1)

            with nc.Block() as b:
                @b.tensor
                def _(pe):
                    def scores(h):
                        if h >= 2:
                            pe.wait_ge(S("ml_arg"), h - 1)
                            pe.wait_ge(S("ml_probs"), h - 1)
                        p0 = (h % 2) * HD
                        qT, kT = qkm[p0:p0 + HD, h // 2, :], qkm[p0:p0 + HD, 3 + h // 2, :]
                        nc.tensor.matmul(bank[h % 2][:, 0:T], const("pick", (1, P), parts=NH6, off=h * P), row(5),
                                         start=True, stop=True).then_inc(S("ml_m"), 1)
                        for k in range(2):
                            last = nc.tensor.matmul(bank[2 + h % 2][:, k * T:(k + 1) * T], kT[:, k * P:(k + 1) * P],
                                                    qT, start=True, stop=True)
                        last.then_inc(S("ml_scores"), 1)
                    scores(0)
                    for h in range(NH6):
                        if h + 1 < NH6:
                            scores(h + 1)
                        pe.wait_ge(S("ml_probs"), h + 1)
                        if h >= 2:
                            pe.wait_ge(S("ml_out"), h - 1)
                        for t in range(NT):
                            for k in range(t + 1):
                                last = nc.tensor.matmul(bank[4 + h % 2][:, t * 65:(t + 1) * 65],
                                                        sp_[h % 2][:, k, t * P:(t + 1) * P], vaug[:, k, h, :],
                                                        start=(k == 0), stop=(k == t))
                        last.then_inc(S("ml_values"), 1)
                    for c in range(NT):
                        for g in range(SGG):
                            last = nc.tensor.matmul(bank[6][:, (c * SGG + g) * HD:(c * SGG + g + 1) * HD],
                                                    sgw[:, g, :], uv[:, c, 256 + g * HD:256 + (g + 1) * HD],
                                                    start=True, stop=True)
                    last.then_inc(S("sg_gate"), 1)

                @b.vector
                def _(dve):
                    def arg(h):
                        dve.wait_ge(S("ml_m"), h + 1)
                        if h >= 2:
                            dve.wait_ge(S("ml_weight"), h - 1)
                        for k in range(2):
                            last = nc.vector.scalar_tensor_tensor(
                                lg[h % 2][:, k, :], bank[h % 2][:, 0:T], acol[:, k, h:h + 1],
                                const("causal_big", (T, 2), (1, T))[:, k, :], ALU.subtract, ALU.add)
                        last.then_inc(S("ml_arg"), 1)
                    arg(0)
                    for h in range(NH6):
                        if h + 1 < NH6:
                            arg(h + 1)
                        dve.wait_ge(S("ml_weight"), h + 1)
                        dve.wait_ge(S("ml_scores"), h + 1)
                        if h >= 2:
                            dve.wait_ge(S("ml_values"), h - 1)
                        nc.vector.scalar_tensor_tensor(sp_[h % 2], two(bank[2 + h % 2]), HD ** -0.5, wt[h % 2],
                                                       ALU.mult, ALU.mult).then_inc(S("ml_probs"), 1)
                        dve.wait_ge(S("ml_values"), h + 1)
                        den = STAT[:, 96 + 2 * h:98 + 2 * h]
                        ov = view(bank[4 + h % 2][:, 0:1], (65, NT), (1, 65))
                        nc.vector.tensor_scalar(den, view(bank[4 + h % 2][:, 64:65], (65, NT)), -1.0, None,
                                                ALU.mult)
                        dve.drain()
                        nc.vector.scalar_tensor_tensor(den, den, -1.0, den, ALU.mult, ALU.max)
                        dve.drain()
                        nc.vector.tensor_tensor(den, den, ecol[:, :, h], ALU.max)
                        dve.drain()
                        nc.vector.reciprocal(den, den)
                        dve.drain()
                        for t in range(NT):
                            o = (NH6 + h) * HD
                            last = nc.vector.tensor_scalar(ycat[:, t, o:o + HD], ov[:, t, 0:HD], den[:, t:t + 1],
                                                           None, ALU.mult)
                        last.then_inc(S("ml_out"), 1)
                    dve.wait_ge(S("sg_gate"), 1)
                    for g in range(SGG):
                        o = (2 * NH6 + g) * HD
                        nc.vector.scalar_tensor_tensor(
                            ycat[:, :, o:o + HD], view(bank[6][:, g * HD:g * HD + 1], (SGG * HD, NT), (1, HD)),
                            sgb[:, g:g + 1], uv[:, :, g * HD:(g + 1) * HD], ALU.add, ALU.mult)

                @b.scalar
                def _(act):
                    for h in range(NH6):
                        act.wait_ge(S("ml_arg"), h + 1)
                        if h >= 2:
                            act.wait_ge(S("ml_probs"), h - 1)
                        nc.scalar.activation(wt[h % 2], lg[h % 2], ACT.Exp, scale=-1.0).then_inc(S("ml_weight"), 1)

            ss16 = view(STAT[:, 128:160], (16, NT), (1, 16))
            sq16 = view(arena(sq_at, 1), (D, NT), (HD, 16), (1, HD))
            y16 = view(ycat, (D, NT), (HD, 16), (1, HD))
            with nc.Block() as b:
                @b.vector
                def _(dve):
                    tt = nc.vector.tensor_tensor
                    tt(sq16, y16, y16, ALU.mult)
                    dve.drain()
                    nc.vector.reduce_sum(ss16, sq16, AX).then_inc(S("y_squares"), 1)
                    dve.wait_ge(S("y_rstd"), 1)
                    tt(y16, y16, view(ss16, (16, NT), (1, 16), (0, HD)), ALU.mult)
                    dve.drain()
                    tt(ycat, ycat, view(outg, (0, NT), (1, D)), ALU.mult)
                    dve.drain()
                    ym = ycat[:, :, NH6 * HD:2 * NH6 * HD]
                    dve.wait_ge(S("og_ready"), 1)
                    tt(ym, ym, og, ALU.mult)

                @b.gpsimd
                def _(pool):
                    pool.wait_ge(S("y_squares"), 1)
                    pool_rstd(pool, STAT[:, 128:160], 1.0 / HD, 32).then_inc(S("y_rstd"), 1)

            turn_to_ht("mixT", ycat)
            m = shaped(xn_at, NT, D)

            def add_x(dve):
                dve.wait_ge(S("out2_taken_act"), 2)
                dve.drain()
                nc.vector.tensor_tensor(X[:, :, :], X[:, :, :], m[:, :, :], ALU.add)
            linear("out2", w_out, RING_AT, out_chunks,
                   lambda kind, t, n0, w: m[:, t, n0:n0 + w], preloaded=2, extra_dve=add_x)
            peer(l)
            clear_all()

        def peer(l):
            G_AT = 0
            G = shaped(G_AT, T, P)
            U_AT = T * P
            V_AT = U_AT + 4 * 1024
            W_AT = V_AT + 4 * 1024
            qT = shaped(0, NSET, T)
            scores = shaped(4096, NT, NSET, NKEY)
            best = shaped(8192, NT, PH, TOPK * TOPK)
            eq_at = 12288
            keys_at = 16384
            keysT = shaped(keys_at, NSET, NKEY)
            wq_at = 18432
            xn_at, junk_at = 22528, 24576
            sv = shaped(26624, NT, NSET, TOPK)
            si = shaped(27136, NT, NSET, TOPK)
            siu = shaped(27648, NT, NSET, TOPK).bitcast(U32)
            bs = shaped(28160, NT, PH, TOPK)
            bpu = shaped(28416, NT, PH, TOPK).bitcast(U32)
            k1u = shaped(28672, NT, PH, TOPK).bitcast(U32)
            k2u = shaped(28928, NT, PH, TOPK).bitcast(U32)
            kf = shaped(29184, 2, NT, PH * TOPK)
            idx = shaped(29696, 2, NT, P)
            gate = shaped(30208, NT, PH, TOPK)
            work_at = 30464
            sel = shaped(U_AT, 3, T)
            hot = shaped(U_AT + 768, 2, 2, 4, P)
            gain_at = W_AT

            def router_loads(sp):
                for s in range(2):
                    sp.dma_start(arena(wq_at + s * 1024, 1024), a["wq_tiles"][l, s, :, :]
                                 ).then_inc(S(f"wq_loaded{s}"), 16)
                sp.dma_start(arena(keys_at, NSET * NKEY), a["keys_t"][l, :, :]).then_inc(S("keys_loaded"), 16)

            norm_to_ht("peer", l, a["norm2_g_2"], xn_at, gain_at, junk_at, router_loads)

            with nc.Block() as b:
                @b.sync
                def _(sp):
                    with sp.Fori(1, NSET // 2) as it:
                        for s in range(2):
                            sp.wait_ge(S("q_filled"), it * 2 + (s - 1))
                            sp.dma_start(arena(wq_at + s * 1024, 1024), a["wq_tiles"][l, it * 2 + s, :, :]
                                         ).then_inc(S(f"wq_loaded{s}"), 16)

                @b.tensor
                def _(pe):
                    with pe.Fori(0, NSET // 2) as it:
                        for s in range(2):
                            w = shaped(wq_at + s * 1024, KD, P)
                            pe.wait_ge(S(f"wq_loaded{s}"), it * 16 + 16)
                            pe.wait_ge(S("q_taken"), it * 2 + (s + 1))
                            for k in range(KD):
                                last = nc.tensor.matmul(bank[s][:, 0:T], w[:, k, :], HT[:, k, :],
                                                        start=(k == 0), stop=(k == KD - 1), skip_group_check=True)
                            last.then_inc(S("q_filled"), 1)
                    pe.wait_ge(S("keys_loaded"), 16)
                    pe.wait_ge(S("q_taken"), NSET + 2)
                    for n in range(NSET // 2):
                        if n >= 4:
                            pe.wait_ge(S("sc_taken"), n - 3)
                        for i in range(4):
                            t, c = (4 * n + i) // NSET, (4 * n + i) % NSET
                            last = nc.tensor.matmul(bank[2 + n % 4][:, i * P:(i + 1) * P],
                                                    qT[:, c, t * P:(t + 1) * P], keysT[:, c, :],
                                                    start=True, stop=True)
                        last.then_inc(S("sc_filled"), 1)

                @b.scalar
                def _(act):
                    act.sem_inc(S("q_taken"), 2)
                    with act.Fori(0, NSET // 2) as it:
                        for s in range(2):
                            act.wait_ge(S("q_filled"), it * 2 + (s + 1))
                            nc.scalar.copy(qT[:, bass.ds(it * 2 + s, 1), :], bank[s][:, 0:T]
                                           ).then_inc(S("q_taken"), 1)
                    sf = arena(4096, NT * NSET * NKEY)
                    for n in range(NSET // 2):
                        act.wait_ge(S("sc_filled"), n + 1)
                        nc.scalar.copy(sf[:, n * 512:(n + 1) * 512], bank[2 + n % 4][:, :]
                                       ).then_inc(S("sc_taken"), 1)
                    act.wait_ge(S("gate_arg"), 1)
                    nc.scalar.activation(view(gate, (1, NT * P)), view(gate, (1, NT * P)), ACT.Exp
                                         ).then_inc(S("gate_exp"), 1)

                @b.vector
                def _(dve):
                    v = nc.vector
                    for t in range(NT):
                        for c in range(NSET):
                            x = scores[:, t, c, :]
                            y = arena(work_at + (c % 2) * P, P)
                            n = t * NSET + c
                            if n % 4 == 0:
                                dve.wait_ge(S("sc_taken"), n // 4 + 1)
                            v.max(sv[:, t, c, 0:8], x)
                            dve.drain()
                            v.max_index(siu[:, t, c, 0:8], sv[:, t, c, 0:8], x)
                            v.match_replace(y, sv[:, t, c, 0:8], x, -3e38)
                            dve.drain()
                            v.max(sv[:, t, c, 8:16], y)
                            dve.drain()
                            v.max_index(siu[:, t, c, 8:16], sv[:, t, c, 8:16], y)
                    dve.drain()
                    v.tensor_copy(view(si, (1, NT * NSET * TOPK)), view(siu, (1, NT * NSET * TOPK)))
                    for t in range(NT):
                        for h in range(PH):
                            v.tensor_tensor(view(best[:, t, h, 0:1], (16, 16), (1, 16)),
                                            view(sv[:, t, 2 * h, 0:1], (1, 16), (0, 16)),
                                            view(sv[:, t, 2 * h + 1, 0:1], (0, 16), (1, 16)), ALU.add)
                    for t in range(NT):
                        for h in range(PH):
                            x = best[:, t, h, :]
                            y = arena(work_at + 256 + (h % 2) * T, T)
                            dve.drain()
                            v.max(bs[:, t, h, 0:8], x)
                            dve.drain()
                            v.max_index(bpu[:, t, h, 0:8], bs[:, t, h, 0:8], x)
                            v.match_replace(y, bs[:, t, h, 0:8], x, -3e38)
                            dve.drain()
                            v.max(bs[:, t, h, 8:16], y)
                            dve.drain()
                            v.max_index(bpu[:, t, h, 8:16], bs[:, t, h, 8:16], y)
                    dve.drain()
                    flat = lambda ap: view(ap, (1, NT * P))
                    v.tensor_scalar(flat(k1u), flat(bpu), 4, None, ALU.logical_shift_right)
                    v.tensor_scalar(flat(k2u), flat(bpu), 15, None, ALU.bitwise_and)
                    dve.drain()
                    v.tensor_copy(view(kf[:, 0, :, :], (1, NT * P)), flat(k1u))
                    v.tensor_copy(view(kf[:, 1, :, :], (1, NT * P)), flat(k2u))
                    for side in range(2):
                        for t in range(NT):
                            eq = view(arena(eq_at, 1), (16, P), (1, 16))
                            dve.drain()
                            v.tensor_tensor(eq, view(kf[:, side, t, :], (1, P), (0, 16)),
                                            const("iota", (0, P), (1, 16)), ALU.is_equal)
                            dve.drain()
                            v.tensor_tensor(view(arena(eq_at, 1), (256, PH), (16, 16), (1, 16)),
                                            view(arena(eq_at, 1), (256, PH), (16, 16), (1, 16)),
                                            view(si[:, t, side, 0:1], (32, PH), (0, 16), (1, 16)), ALU.mult)
                            dve.drain()
                            v.reduce_sum(idx[:, side, t, :], eq, AX)
                    for t in range(NT):
                        v.tensor_tensor(gate[:, t, :, :], bs[:, t, :, :],
                                        view(bs[:, t, 0:1, 0:1], (16, PH), (0, 16)), ALU.subtract)
                    dve.drain()
                    dve.sem_inc(S("gate_arg"), 1)
                    dve.wait_ge(S("gate_exp"), 1)
                    gs = STAT[:, 0:16]
                    v.reduce_sum(gs, view(gate, (16, 16), (1, 16)), AX)
                    dve.drain()
                    v.reciprocal(gs, gs)
                    dve.drain()
                    v.tensor_tensor(view(gate, (16, 16), (1, 16)), view(gate, (16, 16), (1, 16)),
                                    view(gs, (1, 16), (0, 16)), ALU.mult)

            with nc.Block() as b:
                @b.tensor
                def _(pe):
                    srcs = [idx[:, 0, :, :], idx[:, 1, :, :], view(gate, (P, NT), (1, P))]
                    for i, src in enumerate(srcs):
                        for t in range(NT):
                            last = nc.tensor.transpose(bank[i][:, t * P:(t + 1) * P], src[:, t, :], ident)
                        last.then_inc(S("sel_turned"), 1)

                @b.vector
                def _(dve):
                    for i in range(3):
                        dve.wait_ge(S("sel_turned"), i + 1)
                        nc.vector.tensor_copy(sel[:, i, :], bank[i][:, 0:T])

            with nc.Block() as b:
                @b.vector
                def _(dve):
                    dve.sem_inc(S("hot_ready"), 1)
                    with dve.Fori(0, T // 8) as it:
                        for s in range(2):
                            dve.wait_ge(S("hot_free"), it * 2 + (s + 1))
                            for i in range(4):
                                tok = bass.ds(it * 8 + (4 * s + i), 1)
                                nc.vector.tensor_scalar(hot[:, s, 0, i, :], const("iota"), sel[:, 0, tok],
                                                        sel[:, 2, tok], ALU.is_equal, ALU.mult)
                                last = nc.vector.tensor_scalar(hot[:, s, 1, i, :], const("iota"), sel[:, 1, tok],
                                                               None, ALU.is_equal)
                            last.then_inc(S("hot_ready"), 1)

                @b.tensor
                def _(pe):
                    pe.sem_inc(S("hot_free"), 2)
                    with pe.Fori(0, T // 8) as it:
                        for s in range(2):
                            pe.wait_ge(S("hot_ready"), it * 2 + (s + 2))
                            pe.wait_ge(S("g_taken"), it * 2 + (s + 1))
                            for i in range(4):
                                last = nc.tensor.matmul(bank[s][:, i * P:(i + 1) * P], hot[:, s, 0, i, :],
                                                        hot[:, s, 1, i, :], start=True, stop=True,
                                                        skip_group_check=True)
                            last.then_inc(S("hot_free"), 1)

                @b.scalar
                def _(act):
                    act.sem_inc(S("g_taken"), 2)
                    with act.Fori(0, T // 8) as it:
                        for s in range(2):
                            act.wait_ge(S("hot_free"), it * 2 + (s + 3))
                            nc.scalar.copy(G[:, bass.ds(it * 8 + 4 * s, 4), :],
                                           view(bank[s][:, :], (P, 4), (1, P))).then_inc(S("g_taken"), 1)

            R = 4
            NE = NKEY
            u_ring = [shaped(U_AT + s * 1024, KD, P) for s in range(R)]
            v_ring = [arena(V_AT + s * 1024, D) for s in range(R)]
            ga = [arena(W_AT + s * T, T) for s in range(2)]
            wg = [arena(W_AT + 512 + s * T, T) for s in range(2)]

            def load_uv(sp, j, s):
                sp.dma_start(arena(U_AT + s * 1024, 1024), a["u_tiles"][l, j, :, :]).then_inc(S(f"u_loaded{s}"), 16)
                sp.dma_start(v_ring[s], a["v_tiles"][l, j, :, :]).then_inc(S(f"v_loaded{s}"), 16)

            with nc.Block() as b:
                @b.sync
                def _(sp):
                    for s in range(R):
                        load_uv(sp, s, s)
                    with sp.Fori(1, NE // R) as it:
                        for s in range(R):
                            sp.wait_ge(S("y_done"), it * R + (s - R + 1))
                            load_uv(sp, it * R + s, s)

                @b.tensor
                def _(pe):
                    for y in range(4):
                        nc.tensor.matmul(bank[y][:, :], ZERO[:, 0:P], ZERO[:, :], start=True, stop=False,
                                         skip_group_check=True)

                    def acts(s, turn, j):
                        pe.wait_ge(S(f"u_loaded{s}"), turn)
                        pe.wait_ge(S("act_taken"), j)
                        for k in range(KD):
                            last = nc.tensor.matmul(bank[4 + s % 2][:, 0:T], u_ring[s][:, k, :], HT[:, k, :],
                                                    start=(k == 0), stop=(k == KD - 1), skip_group_check=True)
                        last.then_inc(S("act_filled"), 1)

                    def ys(s, turn, j):
                        pe.wait_ge(S(f"v_loaded{s}"), turn)
                        pe.wait_ge(S("weight_ready"), j)
                        for t in range(NT):
                            for n in range(2):
                                last = nc.tensor.matmul(bank[2 * t + n][:, :], wg[s % 2][:, t * P:(t + 1) * P],
                                                        v_ring[s][:, n * 512:(n + 1) * 512],
                                                        start=False, stop=False, skip_group_check=True)
                        last.then_inc(S("y_done"), 1)

                    acts(0, 16, 1)
                    with pe.Fori(0, NE // R - 1) as it:
                        for s in range(R):
                            turn = it * 16 + (16 if s < R - 1 else 32)
                            acts((s + 1) % R, turn, it * R + (s + 2))
                            ys(s, it * 16 + 16, it * R + (s + 1))
                    for s in range(R):
                        if s < R - 1:
                            acts(s + 1, 16 * (NE // R), NE - R + s + 2)
                        ys(s, 16 * (NE // R), NE - R + s + 1)

                @b.scalar
                def _(act):
                    act.sem_inc(S("act_taken"), 2)
                    with act.Fori(0, NE // 2) as it:
                        for s in range(2):
                            act.wait_ge(S("act_filled"), it * 2 + (s + 1))
                            act.wait_ge(S("ga_free"), it * 2 + (s + 1))
                            nc.scalar.activation(ga[s], bank[4 + s][:, 0:T], ACT.Gelu_apprx_tanh
                                                 ).then_inc(S("act_taken"), 1)

                @b.vector
                def _(dve):
                    dve.sem_inc(S("ga_free"), 2)
                    for s in range(2):
                        dve.wait_ge(S("act_taken"), s + 3)
                        nc.vector.tensor_tensor(wg[s], ga[s], G[:, :, s], ALU.mult
                                                ).then_inc(S("weight_ready"), 1)
                        dve.drain()
                        dve.sem_inc(S("ga_free"), 1)
                    with dve.Fori(1, NE // 2) as it:
                        for s in range(2):
                            dve.wait_ge(S("act_taken"), it * 2 + (s + 3))
                            dve.wait_ge(S("y_done"), it * 2 + (s - 1))
                            nc.vector.tensor_tensor(wg[s], ga[s], G[:, :, bass.ds(it * 2 + s, 1)], ALU.mult
                                                    ).then_inc(S("weight_ready"), 1)
                            dve.drain()
                            dve.sem_inc(S("ga_free"), 1)
                    dve.wait_ge(S("y_done"), NE)
                    for t in range(NT):
                        for n in range(2):
                            xx = X[:, t, n * 512:(n + 1) * 512]
                            nc.vector.tensor_tensor(xx, xx, bank[2 * t + n][:, :], ALU.add)

        if 1 in blocks:
            with nc.Fori(0, L) as l:
                first_layer(l)
        if 2 in blocks:
            with nc.Fori(0, L) as l:
                second_layer(l)

        with nc.Block() as b:
            @b.sync
            def _(sp):
                sp.dma_start(out[0].rearrange("(t p) d -> p t d", p=P), X[:, :, :]).then_inc(S("stored"), 16)
                sp.wait_ge(S("stored"), 16)


def constants():
    c = np.zeros((P, NCONST), np.float32)

    def put(name, value):
        at, width = CONST[name]
        c[:, at:at + width] = np.asarray(value, np.float32).reshape(P, width)

    p = np.arange(P)
    tok = (np.arange(2)[None, :] * P + p[:, None])
    keys = np.arange(T)
    put("ident", np.eye(P))
    put("iota", np.broadcast_to(np.arange(P), (P, P)))
    col = tok % GRID
    start = np.clip(col - 8, 0, GRID - 16)[:, :, None]
    kc = keys[None, None, :] % GRID
    put("mask_na", np.where((kc >= start) & (kc < start + 16), 0.0, -BIG))
    put("mask_sw", np.where(np.abs(tok[:, :, None] - keys) <= 128, 0.0, -BIG))
    before = tok[:, :, None] < keys
    put("strict01", before)
    put("strict_big", np.where(before, 0.0, BIG))
    put("causal_big", np.where(tok[:, :, None] <= keys, 0.0, BIG))
    put("tril_t", p[:, None] <= p[None, :])
    put("suffix", p[:, None] >= p[None, :])
    put("ones", np.ones((P, P)))

    def angles(pos, dim):
        inv = np.float32(10000.0) ** (-np.arange(0, dim, 2, dtype=np.float32) / np.float32(dim))
        return (pos.astype(np.float32)[:, :, None] * inv.astype(np.float32)).astype(np.float32)

    for name, pos, dim in (("full", tok, 64), ("mla", tok, 32), ("row", tok // GRID, 32), ("col", tok % GRID, 32)):
        put("cos_" + name, np.cos(angles(pos, dim)))
        put("sin_" + name, np.sin(angles(pos, dim)))
    pick = np.zeros((P, NH6, P))
    for h in range(NH6):
        pick[h, h, :] = 1.0
    put("pick", pick)
    return c


def lay_out(i):
    f = {k: np.asarray(v) for k, v in i.items()}
    cols = lambda g: np.ascontiguousarray(g.reshape(L, -1, P).transpose(0, 2, 1))
    r = {"consts": constants(), "x": f["x"]}
    for k in ("w_in", "w_out", "w_down", "w_in_2", "w_out_2", "mla_w_uq", "mla_w_ukv", "sw_sink",
              "mix_post_gain", "ffn_post_gain", "out_g_2", "sg_vn_g_2"):
        r[k] = f[k]
    for k in ("mix_pre_gain", "ffn_pre_gain", "norm1_g_2", "norm2_g_2"):
        r[k] = cols(f[k])
    r["mla_gain"] = np.concatenate([cols(f["mla_q_gain"]), cols(f["mla_kv_gain"])], axis=2)
    r["ax_gain"] = np.concatenate([np.tile(f["ax_q_gain"], (1, 4)), np.tile(f["ax_k_gain"], (1, 2))], axis=1)
    padded = np.zeros((L, 4, 15, 127), np.float32)
    padded[:, :, :, 48:79] = f["na_rpb"]
    c = np.arange(GRID)
    window = padded[:, :, :, c[None, :] - c[:, None] + 63]
    rows = np.stack([window[:, :, 7 - q:11 - q] for q in range(4)], axis=2)
    r["rpb_rows"] = np.ascontiguousarray(
        rows.reshape(L, 4, NT, 2, 4, GRID, GRID).transpose(0, 3, 5, 1, 2, 4, 6)).reshape(L, P, 4 * NT * T)
    r["w_up_tiles"] = np.ascontiguousarray(
        f["w_up"].reshape(L, KD, P, 2, NF, P).transpose(0, 4, 2, 3, 1, 5)).reshape(L, NF, P, 2 * KD * P)
    conv = np.concatenate([f["conv_w"], f["conv_b"][:, None]], axis=1)
    r["conv_params"] = np.ascontiguousarray(
        conv.reshape(L, 4, 2, NF, P).transpose(0, 4, 3, 2, 1)).reshape(L, P, NF * 8)
    r["sb_gain"] = np.concatenate([np.tile(f["sb_qn_g_2"], (1, NH6)), np.tile(f["sb_kn_g_2"], (1, NH6))], axis=1)
    conv = np.concatenate([f["ml_conv_w_2"], f["ml_conv_b_2"][:, None]], axis=1)
    r["ml_conv"] = np.ascontiguousarray(conv.reshape(L, 5, 6, P).transpose(0, 3, 2, 1))
    r["ml_if_b"] = np.ascontiguousarray(np.stack([f["ml_i_b_2"], f["ml_f_b_2"]], axis=2))
    r["sg_b_t"] = np.ascontiguousarray(f["sg_b_2"].transpose(0, 2, 1))
    r["sg_w_t"] = np.ascontiguousarray(f["sg_w_2"].transpose(0, 3, 1, 2))
    r["wq_tiles"] = np.ascontiguousarray(
        f["peer_wq_2"].reshape(L, KD, P, NSET, P).transpose(0, 3, 2, 1, 4)).reshape(L, NSET, P, KD * P)
    r["keys_t"] = np.ascontiguousarray(
        f["peer_keys_2"].reshape(L, NSET, NKEY, P).transpose(0, 3, 1, 2)).reshape(L, P, NSET * NKEY)
    r["u_tiles"] = np.ascontiguousarray(
        f["peer_u_2"].reshape(L, P, NKEY, KD, P).transpose(0, 2, 4, 3, 1)).reshape(L, NKEY, P, KD * P)
    r["v_tiles"] = np.ascontiguousarray(f["peer_v_2"].reshape(L, P, NKEY, D).transpose(0, 2, 1, 3))
    return r


def kernel(**inputs):
    import concourse.bacc as bacc
    from concourse.bass_utils import run_bass_kernel_spmd

    nc = bacc.Bacc("TRN2", target_bir_lowering=False, num_devices=1)
    arrays, args = {}, {}
    for name, v in lay_out(inputs).items():
        arrays[f"in_{name}"] = v
        args[name] = nc.dram_tensor(f"in_{name}", v.shape, mybir.dt.from_np(v.dtype), kind="ExternalInput").ap()
    out = nc.dram_tensor("out_x", (1, T, D), F32, kind="ExternalOutput").ap()
    build(nc, args, out)
    r = run_bass_kernel_spmd(nc, [arrays], core_ids=[0])
    return r.results[0]["out_x"]
```

```python
from contextlib import ExitStack

import numpy as np
import concourse.bass as bass
from concourse import mybir

F32 = mybir.dt.float32
F32R = mybir.dt.float32r
BF16 = mybir.dt.bfloat16
U32 = mybir.dt.uint32
ALU = mybir.AluOpType
ACT = mybir.ActivationFunctionType
AX = mybir.AxisListType.X

P = 128
T = 256
NT = T // P
D = 1024
KD = D // P
L = 2
HD = 64
EPS = 1e-6
BIG = 1e30
GRID = 64

A_Q, A_K, A_V = 0, 256, 512
B_CQ, B_CKV, B_KR = 768, 1024, 1152
C_Q, C_K, C_V = 1184, 1440, 1568
D_Q, D_K, D_V = 1696, 1952, 2080
IN1 = 2208
FF = 2816
NF = FF // P

MLQK, MLQK_W = 1152, 768
SB_Q, SB_K, SB_V = 0, 384, 768
ML_V, ML_O, ML_IF, SG_UV = 1152, 1536, 1920, 1932
IN2 = 3212
Z2 = IN2 - MLQK_W
NH6 = 6
SGG = 4

NSET = 16
PH = 8
TOPK = 16
NKEY = 128


def plan_of(sizes):
    plan, at = {}, 0
    for name, width in sizes:
        plan[name] = (at, width)
        at += width
    return plan, at


CONST, NCONST = plan_of([("ident", P), ("iota", P), ("tril_t", P), ("suffix", P), ("ones", P)])
CONST1, NCONST1 = plan_of([("mask_na", 2 * T), ("mask_sw", 2 * T), ("cos_full", 2 * 32), ("sin_full", 2 * 32),
                           ("cos_mla", 2 * 16), ("sin_mla", 2 * 16), ("cos_row", 2 * 16), ("sin_row", 2 * 16),
                           ("cos_col", 2 * 16), ("sin_col", 2 * 16)])
CONST2, NCONST2 = plan_of([("strict01", 2 * T), ("strict_big", 2 * T), ("causal_big", 2 * T),
                           ("pick", NH6 * P)])


def build(nc, a, out, dbg=None, blocks=(1, 2)):
    with ExitStack() as ctx:
        sb = lambda name, shape, dt=F32: ctx.enter_context(nc.sbuf_tensor(name, shape, dt))
        X = sb("X", [P, NT, D])
        HT_HI = sb("HT_HI", [P, KD, T], F32R)
        HT_LO = sb("HT_LO", [P, KD, T], F32R)
        CON = sb("CON", [P, NCONST])
        ZERO = sb("ZERO", [P, 512], BF16)
        STAT = sb("STAT", [P, 256])
        HALF = sb("HALF", [P, 64])
        GAINS = sb("GAINS", [P, 4, L, KD])
        ARENA_N = 45696
        arena_bytes = -(-nc.sbuf_base // 32) * 32
        ARENA = sb("ARENA", [P, ARENA_N])
        part_tensors = {}
        bank = [ctx.enter_context(nc.psum_tensor(f"bank{i}", [P, 512], F32)) for i in range(8)]

        semaphores = {}
        numbers_used = set()

        def S(name):
            if name not in semaphores:
                semaphores[name] = nc.alloc_semaphore(name)
                numbers_used.add(semaphores[name].num)
            return semaphores[name]

        def clear_all():
            nums = sorted(numbers_used)
            assert nums == list(range(nums[0], nums[-1] + 1)), nums
            nc.all_engine_barrier(sems_to_clear=range(nums[0], nums[-1] + 1))

        def view(ap, *dims, off=0):
            return bass.AP(ap.tensor, ap.offset + off, [list(ap.ap[0])] + [list(d) for d in dims])

        EXTRA_AT = ARENA_N - max(NCONST1, NCONST2)

        def const(name, *dims, parts=P, off=0):
            for plan, base in ((CONST, None), (CONST1, EXTRA_AT), (CONST2, EXTRA_AT)):
                if name in plan:
                    at, width = plan[name]
                    ap = CON[0:parts, at:at + width] if base is None else ARENA[0:parts, base + at:base + at + width]
                    return view(ap, *dims, off=off) if dims else ap

        ident = const("ident")

        def arena(at, n, parts=P):
            assert at + n <= ARENA_N, (at, n)
            return ARENA[0:parts, at:at + n]

        def shaped(at, *shape):
            n = int(np.prod(shape))
            ap = arena(at, n)
            strides = [int(np.prod(shape[i + 1:])) for i in range(len(shape))]
            return view(ap, *zip(strides, shape))

        def parts(at, n):
            assert at + n <= ARENA_N, (at, n)
            if (at, n) not in part_tensors:
                part_tensors[at, n] = nc.alloc_sbuf_tensor_at(f"PARTS{at}_{n}", [P, n], F32R,
                                                              offset=arena_bytes + 4 * at)
            return part_tensors[at, n][:, :]

        def mm3(out_ap, w_hi, w_lo, x_hi, x_lo, start, stop):
            mm = nc.tensor.matmul
            mm(out_ap, w_hi, x_hi, start=start, stop=False, skip_group_check=True)
            mm(out_ap, w_lo, x_hi, start=False, stop=False, skip_group_check=True)
            return mm(out_ap, w_hi, x_lo, start=False, stop=stop, skip_group_check=True)

        with nc.Block() as b:
            @b.sync
            def _(sp):
                sp.dma_start(CON[:, :], a["consts"][:, :]).then_inc(S("set_up_loaded"), 16)
                sp.dma_start(X[:, :, :], a["x"][0].rearrange("(t p) d -> p t d", p=P)
                             ).then_inc(S("set_up_loaded"), 16)
                sp.dma_start(GAINS[:, :, :, :], a["norm_gains"]).then_inc(S("set_up_loaded"), 16)
                sp.wait_ge(S("set_up_loaded"), 48)

            @b.vector
            def _(dve):
                nc.vector.memset(ZERO[:, :], 0.0)
                nc.vector.memset(HALF[:, :], -0.5)

        def pool_rstd(pool, ss, scale, n):
            nc.gpsimd.tensor_scalar(ss, ss, scale, EPS, ALU.mult, ALU.add)
            pool.drain()
            shape = [c for _, c in list(ss.ap)[1:]]
            h = view(HALF[:, 0:n], *([(shape[1], shape[0]), (1, shape[1])] if len(shape) == 2 else [(1, n)]))
            return nc.gpsimd.tensor_tensor(ss, ss, h, ALU.pow)

        def norm_to_ht(tag, l, which, xn_at, junk_at, extra_loads=None, raw=None):
            xn = shaped(xn_at, NT, D)
            junk = shaped(junk_at, NT, D)
            ss = STAT[:, 0:NT]

            def gain(k):
                return GAINS[:, which, l, k:k + 1]

            with nc.Block() as b:
                if extra_loads:
                    @b.sync
                    def _(sp):
                        extra_loads(sp)

                @b.scalar
                def _(act):
                    for t in range(NT):
                        nc.scalar.activation(junk[:, t, :], X[:, t, :], ACT.Square,
                                             accum_out=ss[:, t:t + 1]).then_inc(S(tag + "_squares"), 1)
                    for k in range(KD):
                        act.wait_ge(S(tag + "_turned"), k + 1)
                        if raw is not None:
                            nc.scalar.mul(raw[:, k, :], bank[k % 4][:, 0:T], gain(k))
                        nc.scalar.mul(HT_HI[:, k, :], bank[k % 4][:, 0:T], gain(k)).then_inc(S(tag + "_hi"), 1)

                @b.gpsimd
                def _(pool):
                    pool.wait_ge(S(tag + "_squares"), NT)
                    pool_rstd(pool, ss, 1.0 / D, NT).then_inc(S(tag + "_rstd"), 1)

                @b.vector
                def _(dve):
                    dve.wait_ge(S(tag + "_rstd"), 1)
                    for t in range(NT):
                        nc.vector.tensor_scalar(xn[:, t, :], X[:, t, :], ss[:, t:t + 1], None, ALU.mult
                                                ).then_inc(S(tag + "_xn"), 1)
                    for k in range(KD):
                        dve.wait_ge(S(tag + "_hi"), k + 1)
                        nc.vector.scalar_tensor_tensor(HT_LO[:, k, :], bank[k % 4][:, 0:T], gain(k), HT_HI[:, k, :],
                                                       ALU.mult, ALU.subtract).then_inc(S(tag + "_lo"), 1)

                @b.tensor
                def _(pe):
                    pe.wait_ge(S(tag + "_xn"), NT)
                    for k in range(KD):
                        if k >= 4:
                            pe.wait_ge(S(tag + "_lo"), k - 3)
                        for t in range(NT):
                            last = nc.tensor.transpose(bank[k % 4][:, t * P:(t + 1) * P],
                                                       xn[:, t, k * P:(k + 1) * P], ident)
                        last.then_inc(S(tag + "_turned"), 1)

        def turn_to_ht(tag, src):
            with nc.Block() as b:
                @b.scalar
                def _(act):
                    for k in range(KD):
                        act.wait_ge(S(tag + "_turned"), k + 1)
                        nc.scalar.copy(HT_HI[:, k, :], bank[k % 4][:, 0:T]).then_inc(S(tag + "_hi"), 1)

                @b.vector
                def _(dve):
                    for k in range(KD):
                        dve.wait_ge(S(tag + "_hi"), k + 1)
                        nc.vector.tensor_tensor(HT_LO[:, k, :], bank[k % 4][:, 0:T], HT_HI[:, k, :], ALU.subtract
                                                ).then_inc(S(tag + "_lo"), 1)

                @b.tensor
                def _(pe):
                    for k in range(KD):
                        if k >= 4:
                            pe.wait_ge(S(tag + "_lo"), k - 3)
                        for t in range(NT):
                            last = nc.tensor.transpose(bank[k % 4][:, t * P:(t + 1) * P],
                                                       src[:, t, k * P:(k + 1) * P], ident)
                        last.then_inc(S(tag + "_turned"), 1)

        PIECES, PIECE_N = 8, 2 * 512
        UNITS, UNIT_N = 8, 2 * 512

        def linear_load(sp, tag, w_view, raw_at, chunks, q):
            c, kp = q // (KD // 2), q % (KD // 2)
            _, n0, w, _ = chunks[c]
            dst = view(arena(raw_at + (q % PIECES) * PIECE_N, PIECE_N), (512, 2), (1, w))
            sp.dma_start(dst, w_view[:, 2 * kp:2 * kp + 2, n0:n0 + w]).then_inc(S(f"{tag}_w_loaded{q % PIECES}"), 16)

        def linear(tag, w_view, raw_at, unit_at, chunks, dst_of, preloaded=0, extra_loads=None, extra_dve=None):
            n_units = KD * len(chunks)
            fills = []
            for c, (kind, n0, w, d0) in enumerate(chunks):
                fills += [(c, i) for i in range(NT if kind == "rows" else w // P)]

            def unit(n):
                u = parts(unit_at + (n % UNITS) * UNIT_N, UNIT_N)
                w = chunks[n // KD][2]
                return u[:, 0:w], u[:, 512:512 + w]

            def raw(n):
                q = n // 2
                at = raw_at + (q % PIECES) * PIECE_N + (n % 2) * 512
                return arena(at, chunks[n // KD][2])

            def empty(eng, copy, who, c):
                mine = [m for m, (cc, _) in enumerate(fills) if cc == c and ("act", "dve")[m % 2] == who]
                if mine:
                    eng.wait_ge(S(tag + "_used"), KD * (c + 1))
                for m in mine:
                    i = fills[m][1]
                    kind, n0, w, d0 = chunks[c]
                    if kind == "rows":
                        to, frm = dst_of(kind, i, d0, w), bank[m % 8][:, 0:w]
                    else:
                        to, frm = dst_of(kind, d0 + i, 0, T), bank[m % 8][:, 0:T]
                    copy(to, frm).then_inc(S(f"{tag}_taken_{who}"), 1)

            with nc.Block() as b:
                @b.sync
                def _(sp):
                    if extra_loads:
                        extra_loads(sp)
                    for q in range(preloaded, n_units // 2):
                        if q >= PIECES:
                            sp.wait_ge(S(tag + "_lo"), 2 * (q - PIECES) + 2)
                        linear_load(sp, tag, w_view, raw_at, chunks, q)

                @b.scalar
                def _(act):
                    for n in range(n_units):
                        c, k = n // KD, n % KD
                        if k % 2 == 0:
                            act.wait_ge(S(f"{tag}_w_loaded{n // 2 % PIECES}"), 16 * (n // 2 // PIECES + 1))
                        if n >= UNITS:
                            act.wait_ge(S(tag + "_used"), n - UNITS + 1)
                        nc.scalar.copy(unit(n)[0], raw(n)).then_inc(S(tag + "_hi"), 1)
                        if k == 3 and c >= 1:
                            empty(act, nc.scalar.copy, "act", c - 1)
                    empty(act, nc.scalar.copy, "act", len(chunks) - 1)

                @b.vector
                def _(dve):
                    for n in range(n_units):
                        c, k = n // KD, n % KD
                        dve.wait_ge(S(tag + "_hi"), n + 1)
                        nc.vector.tensor_tensor(unit(n)[1], raw(n), unit(n)[0], ALU.subtract
                                                ).then_inc(S(tag + "_lo"), 1)
                        if k == 3 and c >= 1:
                            empty(dve, nc.vector.tensor_copy, "dve", c - 1)
                    empty(dve, nc.vector.tensor_copy, "dve", len(chunks) - 1)
                    if extra_dve:
                        extra_dve(dve)

                @b.tensor
                def _(pe):
                    for n in range(n_units):
                        c, k = n // KD, n % KD
                        kind, n0, w, d0 = chunks[c]
                        pe.wait_ge(S(tag + "_lo"), n + 1)
                        hi, lo = unit(n)
                        for m, (cc, i) in enumerate(fills):
                            if cc != c:
                                continue
                            if k == 0 and m >= 8:
                                pe.wait_ge(S(f"{tag}_taken_{('act', 'dve')[m % 2]}"), (m - 8) // 2 + 1)
                            tok = slice(i * P, (i + 1) * P)
                            if kind == "rows":
                                last = mm3(bank[m % 8][:, 0:w], HT_HI[:, k, tok], HT_LO[:, k, tok], hi, lo,
                                           k == 0, k == KD - 1)
                            else:
                                last = mm3(bank[m % 8][:, 0:T], hi[:, tok], lo[:, tok], HT_HI[:, k, :],
                                           HT_LO[:, k, :], k == 0, k == KD - 1)
                        last.then_inc(S(tag + "_used"), 1)

        def add_normed(tag, m, gain, gain_sem, junk, last_x_store=None):
            ss = STAT[:, 0:NT]
            with nc.Block() as b:
                @b.scalar
                def _(act):
                    for t in range(NT):
                        nc.scalar.activation(junk[:, t, :], m[:, t, :], ACT.Square,
                                             accum_out=ss[:, t:t + 1]).then_inc(S(tag + "_squares"), 1)

                @b.gpsimd
                def _(pool):
                    pool.wait_ge(S(tag + "_squares"), NT)
                    pool_rstd(pool, ss, 1.0 / D, NT).then_inc(S(tag + "_rstd"), 1)

                @b.vector
                def _(dve):
                    dve.wait_ge(S(tag + "_rstd"), 1)
                    dve.wait_ge(S(gain_sem), 16)
                    for t in range(NT):
                        nc.vector.scalar_tensor_tensor(m[:, t, :], m[:, t, :], ss[:, t:t + 1], gain,
                                                       ALU.mult, ALU.mult)
                    dve.drain()
                    nc.vector.tensor_tensor(X[:, :, :], X[:, :, :], m[:, :, :], ALU.add)

        def rope(dve, x1, x2, y1, y2, cos, sin, t1, t2):
            tt = nc.vector.tensor_tensor
            dve.drain()
            tt(t1, x1, cos, ALU.mult)
            tt(t2, x2, sin, ALU.mult)
            dve.drain()
            tt(y1, t1, t2, ALU.subtract)
            dve.drain()
            tt(t1, x2, cos, ALU.mult)
            tt(t2, x1, sin, ALU.mult)
            dve.drain()
            return tt(y2, t1, t2, ALU.add)

        def first_layer(l):
            Z_AT = 0
            RING_AT = Z_AT + NT * IN1
            UNIT_AT = RING_AT + PIECES * PIECE_N
            at = UNIT_AT + UNITS * UNIT_N

            def take(n):
                nonlocal at
                at += n
                assert at <= EXTRA_AT, at
                return at - n

            z = shaped(Z_AT, NT, IN1)
            bias_at = take(4 * NT * T)
            bias = shaped(bias_at, 4, NT, T)
            rot_c = shaped(take(NT * 6 * HD), NT, 6 * HD)
            rot_d = shaped(take(NT * 6 * HD), NT, 6 * HD)
            lat = shaped(take(NT * 384), NT, 384)
            latT = shaped(take(3 * T), 3, T)
            qb = shaped(take(NT * 384), NT, 384)
            kvb = shaped(take(NT * 512), NT, 512)
            kb = shaped(take(NT * 384), NT, 384)
            qkT_at = take(18 * T)
            qkT = shaped(qkT_at, 18, T)
            mixed_at = take(NT * D)
            mixed = shaped(mixed_at, NT, D)
            gains_at = take(8 + 4 + 384 + 4)
            post_gain_at = take(2 * D)
            w_uq = shaped(take(2 * 384), 2, 384)
            w_ukv = arena(take(512), 512)
            s_sb = shaped(take(2 * NT * T), 2, NT, T)
            p_at = take(2 * NT * T)
            p_sb = shaped(p_at, 2, NT, T)
            pT = shaped(take(2 * 2 * T), 2, 2, T)
            mla_gain = arena(gains_at + 8, 3)
            ax_gain = arena(gains_at + 12, 384)
            sink = arena(gains_at + 396, 4)
            mix_post = arena(post_gain_at, D)
            ffn_post = arena(post_gain_at + D, D)

            w_in = a["w_in"][l].rearrange("(k p) n -> p k n", p=P)
            w_out = a["w_out"][l].rearrange("(k p) n -> p k n", p=P)
            in_chunks = [("rows", n, min(512, IN1 - n), n) for n in range(0, IN1, 512)]
            out_chunks = [("rows", n, 512, n) for n in range(0, D, 512)]

            def early_loads(sp):
                for q in range(PIECES):
                    linear_load(sp, "in1", w_in, RING_AT, in_chunks, q)
                sp.dma_start(ARENA[:, EXTRA_AT:EXTRA_AT + NCONST1], a["consts1"][:, :]).then_inc(S("prep_params"), 16)
                sp.dma_start(mla_gain, a["mla_gain"][l, :, :]).then_inc(S("prep_params"), 16)
                sp.dma_start(ax_gain, a["ax_gain"][bass.ds(l, 1), :].broadcast_to([P, 384])).then_inc(S("prep_params"), 16)
                sp.dma_start(w_uq, a["mla_w_uq"][l].rearrange("(k p) n -> p k n", p=P)).then_inc(S("prep_params"), 16)
                sp.dma_start(w_ukv, a["mla_w_ukv"][l, :, :]).then_inc(S("prep_params"), 16)
                sp.dma_start(sink, a["sw_sink"][bass.ds(l, 1), :].broadcast_to([P, 4])).then_inc(S("sink_loaded"), 16)
                sp.dma_start(mix_post, a["mix_post_gain"][bass.ds(l, 1), :].broadcast_to([P, D])
                             ).then_inc(S("mix_post_loaded"), 16)
                sp.dma_start(ffn_post, a["ffn_post_gain"][bass.ds(l, 1), :].broadcast_to([P, D])
                             ).then_inc(S("ffn_post_loaded"), 16)
                sp.dma_start(arena(bias_at, 4 * NT * T), a["rpb_rows"][l, :, :]).then_inc(S("rpb_loaded"), 16)

            norm_to_ht("pre", l, 0, mixed_at, qkT_at, early_loads)
            linear("in1", w_in, RING_AT, UNIT_AT, in_chunks,
                   lambda kind, t, n0, w: z[:, t, n0:n0 + w], preloaded=PIECES)

            ssB = STAT[:, 0:4]
            ssC = view(STAT[:, 16:28], (6, NT), (1, 6))
            sq = shaped(mixed_at, NT, 6 * HD)
            c_in = shaped(p_at, NT, 6 * HD)
            t1_at = mixed_at + 768
            t2_at = t1_at + 400
            groups = []
            for g in range(2):
                groups.append((lambda t, g=g: z[:, t, A_Q + g * P:A_Q + (g + 1) * P], P))
            for g in range(2):
                groups.append((lambda t, g=g: z[:, t, A_K + g * P:A_K + (g + 1) * P], P))
            for rot in (rot_d, rot_c):
                for g in range(3):
                    groups.append((lambda t, g=g, rot=rot: rot[:, t, g * P:(g + 1) * P], P))
            for h in range(4):
                groups.append((lambda t, h=h: qb[:, t, h * 96:(h + 1) * 96], 96))
            for h in range(4):
                groups.append((lambda t, h=h: kb[:, t, h * 96:(h + 1) * 96], 96))
            READY = [0] * 4 + [1] * 3 + [2] * 3 + [3] * 8

            with nc.Block() as b:
                @b.sync
                def _(sp):
                    for q in range(PIECES):
                        linear_load(sp, "out1", w_out, RING_AT, out_chunks, q)

                @b.scalar
                def _(act):
                    junk = shaped(mixed_at + 1600, 256)
                    for t in range(NT):
                        nc.scalar.activation(junk, z[:, t, B_CQ:B_CQ + 256], ACT.Square,
                                             accum_out=ssB[:, t:t + 1])
                        act.drain()
                        nc.scalar.activation(junk[:, 0:128], z[:, t, B_CKV:B_CKV + 128], ACT.Square,
                                             accum_out=ssB[:, 2 + t:3 + t])
                        act.drain()
                    act.sem_inc(S("lat_squares"), 1)
                    act.wait_ge(S("prep_params"), 80)
                    for i in range(3):
                        act.wait_ge(S("lat_turned"), i + 1)
                        nc.scalar.mul(latT[:, i, :], bank[i][:, 0:T], mla_gain[:, i:i + 1]
                                      ).then_inc(S("latT_ready"), 1)
                    for t in range(NT):
                        act.wait_ge(S("lat_up"), 2 * t + 1)
                        nc.scalar.copy(qb[:, t, :], bank[4 + t][:, 0:384])
                        act.wait_ge(S("lat_up"), 2 * t + 2)
                        nc.scalar.copy(kvb[:, t, :], bank[6 + t][:, :]).then_inc(S("up_ready"), 1)
                    for g in range(0, 18, 2):
                        act.wait_ge(S("qk_turned"), g + 1)
                        n = groups[g][1]
                        nc.scalar.copy(qkT[0:n, g, :], bank[g % 4][0:n, 0:T]).then_inc(S("qk_out_even"), 1)

                @b.gpsimd
                def _(pool):
                    pool.wait_ge(S("rpb_loaded"), 16)
                    pool.wait_ge(S("prep_params"), 80)
                    for h in range(4):
                        nc.gpsimd.tensor_tensor(bias[:, h, :, :], bias[:, h, :, :],
                                                const("mask_na", (T, NT), (1, T)), ALU.add)
                    pool.wait_ge(S("lat_squares"), 1)
                    nc.gpsimd.tensor_scalar(ssB[:, 0:2], ssB[:, 0:2], 1.0 / 256, EPS, ALU.mult, ALU.add)
                    nc.gpsimd.tensor_scalar(ssB[:, 2:4], ssB[:, 2:4], 1.0 / 128, EPS, ALU.mult, ALU.add)
                    pool.drain()
                    nc.gpsimd.tensor_tensor(ssB, ssB, HALF[:, 0:4], ALU.pow).then_inc(S("lat_rstd"), 1)
                    pool.wait_ge(S("ax_squares"), 1)
                    pool_rstd(pool, STAT[:, 16:28], 1.0 / HD, 12).then_inc(S("ax_rstd"), 1)

                @b.vector
                def _(dve):
                    tt = nc.vector.tensor_tensor
                    dve.wait_ge(S("prep_params"), 80)
                    cqk = z[:, :, C_Q:C_Q + 384]
                    tt(sq, cqk, cqk, ALU.mult)
                    dve.drain()
                    nc.vector.reduce_sum(ssC, view(sq, (384, NT), (HD, 6), (1, HD)), AX
                                         ).then_inc(S("ax_squares"), 1)
                    dve.wait_ge(S("lat_rstd"), 1)
                    for t in range(NT):
                        nc.vector.tensor_scalar(lat[:, t, 0:256], z[:, t, B_CQ:B_CQ + 256], ssB[:, t:t + 1],
                                                None, ALU.mult)
                        nc.vector.tensor_scalar(lat[:, t, 256:384], z[:, t, B_CKV:B_CKV + 128],
                                                ssB[:, 2 + t:3 + t], None, ALU.mult).then_inc(S("lat_ready"), 1)
                    def half(src, stride, base, heads, width, w):
                        return view(src[:, 0:1, base:base + 1], (stride, NT), (width, heads), (1, w))
                    def tmp(base, heads, w):
                        return view(arena(base, 400), (heads * w, NT), (w, heads), (1, w))
                    def angle(name, heads, w):
                        return const(name, (w, NT), (0, heads), (1, w))
                    pairs = ((0, 2 * HD), (HD, 2 * HD), (4 * HD, HD))
                    for g, (c0, step) in enumerate(pairs):
                        rope(dve, half(z, IN1, D_Q + c0, 2, step, 32), half(z, IN1, D_Q + c0 + 32, 2, step, 32),
                             half(rot_d, 384, g * P, 2, HD, 32), half(rot_d, 384, g * P + 32, 2, HD, 32),
                             angle("cos_full", 2, 32), angle("sin_full", 2, 32),
                             tmp(t1_at, 2, 32), tmp(t2_at, 2, 32))
                    dve.drain()
                    dve.sem_inc(S("qk_source"), 1)
                    dve.wait_ge(S("ax_rstd"), 1)
                    c3 = view(cqk, (IN1, NT), (HD, 6), (1, HD))
                    tt(view(sq, (384, NT), (HD, 6), (1, HD)), c3, view(ssC, (6, NT), (1, 6), (0, HD)), ALU.mult)
                    dve.drain()
                    for g, (c0, step) in enumerate(pairs):
                        tt(half(c_in, 384, g * P, 2, HD, HD), half(sq, 384, c0, 2, step, HD),
                           view(ax_gain, (0, NT), (step, 2), (1, HD), off=c0), ALU.mult)
                    for base, ang in ((0, "row"), (32, "col")):
                        rope(dve, half(c_in, 384, base, 6, HD, 16), half(c_in, 384, base + 16, 6, HD, 16),
                             half(rot_c, 384, base, 6, HD, 16), half(rot_c, 384, base + 16, 6, HD, 16),
                             angle("cos_" + ang, 6, 16), angle("sin_" + ang, 6, 16),
                             tmp(t1_at, 6, 16), tmp(t2_at, 6, 16))
                    dve.drain()
                    dve.sem_inc(S("qk_source"), 1)
                    dve.wait_ge(S("up_ready"), NT)
                    rope(dve, half(qb, 384, 64, 4, 96, 16), half(qb, 384, 80, 4, 96, 16),
                         half(sq, 384, 0, 4, 32, 16), half(sq, 384, 16, 4, 32, 16),
                         angle("cos_mla", 4, 16), angle("sin_mla", 4, 16), tmp(t1_at, 4, 16), tmp(t2_at, 4, 16))
                    dve.drain()
                    nc.vector.tensor_copy(half(qb, 384, 64, 4, 96, 32), half(sq, 384, 0, 4, 32, 32))
                    rope(dve, half(z, IN1, B_KR, 1, 32, 16), half(z, IN1, B_KR + 16, 1, 32, 16),
                         half(sq, 384, 128, 1, 32, 16), half(sq, 384, 144, 1, 32, 16),
                         angle("cos_mla", 1, 16), angle("sin_mla", 1, 16), tmp(t1_at, 1, 16), tmp(t2_at, 1, 16))
                    dve.drain()
                    nc.vector.tensor_copy(half(kb, 384, 64, 4, 96, 32), view(sq[:, 0:1, 128:129], (384, NT), (0, 4), (1, 32)))
                    nc.vector.tensor_copy(half(kb, 384, 0, 4, 96, HD), half(kvb, 512, 0, 4, P, HD)
                                          )
                    dve.drain()
                    dve.sem_inc(S("qk_source"), 1)
                    for g in range(1, 18, 2):
                        dve.wait_ge(S("qk_turned"), g + 1)
                        n = groups[g][1]
                        nc.vector.tensor_copy(qkT[0:n, g, :], bank[g % 4][0:n, 0:T]).then_inc(S("qk_out_odd"), 1)

                @b.tensor
                def _(pe):
                    pe.wait_ge(S("lat_ready"), NT)
                    for i in range(3):
                        for t in range(NT):
                            last = nc.tensor.transpose(bank[i][:, t * P:(t + 1) * P],
                                                       lat[:, t, i * P:(i + 1) * P], ident)
                        last.then_inc(S("lat_turned"), 1)
                    pe.wait_ge(S("prep_params"), 80)
                    pe.wait_ge(S("latT_ready"), 3)
                    for t in range(NT):
                        for k in range(2):
                            last = nc.tensor.matmul(bank[4 + t][:, 0:384], latT[:, k, t * P:(t + 1) * P],
                                                    w_uq[:, k, :], start=(k == 0), stop=(k == 1))
                        last.then_inc(S("lat_up"), 1)
                        nc.tensor.matmul(bank[6 + t][:, :], latT[:, 2, t * P:(t + 1) * P], w_ukv,
                                         start=True, stop=True).then_inc(S("lat_up"), 1)
                    for g, (src, n) in enumerate(groups):
                        if READY[g]:
                            pe.wait_ge(S("qk_source"), READY[g])
                        if g >= 4:
                            pe.wait_ge(S("qk_out_odd" if g % 2 else "qk_out_even"), (g - 4) // 2 + 1)
                        for t in range(NT):
                            last = nc.tensor.transpose(bank[g % 4][0:n, t * P:(t + 1) * P], src(t), ident)
                        last.then_inc(S("qk_turned"), 1)

            heads = []
            for h in range(4):
                p0 = (h % 2) * HD
                heads.append(("na", qkT[p0:p0 + HD, h // 2, :], qkT[p0:p0 + HD, 2 + h // 2, :],
                              lambda t, h=h: z[:, t, A_V + h * HD:A_V + (h + 1) * HD], h * HD, h))
            for h in range(4):
                heads.append(("mla", qkT[0:96, 10 + h, :], qkT[0:96, 14 + h, :],
                              lambda t, h=h: kvb[:, t, h * P + HD:(h + 1) * P], 256 + h * HD, h))
            for kind, g0, v0, o0 in (("ax", 7, C_V, 512), ("sw", 4, D_V, 768)):
                for h in range(4):
                    p0 = (h // 2) * HD
                    heads.append((kind, qkT[p0:p0 + HD, g0 + h % 2, :], qkT[p0:p0 + HD, g0 + 2, :],
                                  lambda t, h=h, v0=v0: z[:, t, v0 + h // 2 * HD:v0 + (h // 2 + 1) * HD],
                                  o0 + h * HD, h))
            NHD = len(heads)
            nmax = view(STAT[:, 32:64], (2, NHD), (1, 2))
            sums = view(STAT[:, 64:96], (2, NHD), (1, 2))
            sinke = view(STAT[:, 96:104], (2, 4), (1, 2))
            nsink = STAT[:, 104:108]
            scale_of = {"na": HD ** -0.5, "mla": 96 ** -0.5, "ax": HD ** -0.5, "sw": HD ** -0.5}

            with nc.Block() as b:
                @b.tensor
                def _(pe):
                    def scores(h):
                        if h >= 2:
                            pe.wait_ge(S("att_scaled"), h - 1)
                        _, qT, kT, _, _, _ = heads[h]
                        for t in range(NT):
                            last = nc.tensor.matmul(bank[h % 2][:, t * T:(t + 1) * T], qT[:, t * P:(t + 1) * P],
                                                    kT, start=True, stop=True)
                        last.then_inc(S("att_scores"), 1)

                    def turn(h):
                        pe.wait_ge(S("att_probs"), h + 1)
                        if h >= 2:
                            pe.wait_ge(S("att_probsT"), h - 1)
                        for t in range(NT):
                            for k in range(2):
                                last = nc.tensor.transpose(bank[2 + h % 2][:, k * T + t * P:k * T + (t + 1) * P],
                                                           p_sb[:, h % 2, t, k * P:(k + 1) * P], ident)
                        last.then_inc(S("att_turned"), 1)

                    def values(h):
                        pe.wait_ge(S("att_probsT"), h + 1)
                        if h >= 2:
                            pe.wait_ge(S("att_out"), h - 1)
                        v = heads[h][3]
                        for t in range(NT):
                            for k in range(2):
                                last = nc.tensor.matmul(bank[4 + h % 2][:, t * HD:(t + 1) * HD],
                                                        pT[:, h % 2, k, t * P:(t + 1) * P], v(k),
                                                        start=(k == 0), stop=(k == 1))
                        last.then_inc(S("att_values"), 1)

                    scores(0)
                    scores(1)
                    for h in range(NHD):
                        turn(h)
                        if h + 2 < NHD:
                            scores(h + 2)
                        values(h)

                @b.vector
                def _(dve):
                    def scaled(h):
                        kind, _, _, _, _, i = heads[h]
                        dve.wait_ge(S("att_scores"), h + 1)
                        if h >= 2:
                            dve.wait_ge(S("att_exp"), h - 1)
                        s = s_sb[:, h % 2, :, :]
                        frm = view(bank[h % 2][:, :], (T, NT), (1, T))
                        sc = scale_of[kind]
                        if kind in ("na", "sw"):
                            add = bias[:, i, :, :] if kind == "na" else const("mask_sw", (T, NT), (1, T))
                            nc.vector.scalar_tensor_tensor(s, frm, sc, add, ALU.mult, ALU.add
                                                           ).then_inc(S("att_scaled"), 1)
                        else:
                            nc.vector.tensor_scalar(s, frm, sc, None, ALU.mult).then_inc(S("att_scaled"), 1)
                        dve.drain()
                        last = nc.vector.tensor_reduce(nmax[:, h, :], s, AX, ALU.max, negate=True)
                        if kind == "sw":
                            dve.drain()
                            last = nc.vector.tensor_scalar(nmax[:, h, :], nmax[:, h, :], nsink[:, i:i + 1], None,
                                                           ALU.min)
                        last.then_inc(S("att_max"), 1)

                    def normalised(h):
                        kind, _, _, _, _, i = heads[h]
                        dve.wait_ge(S("att_exp"), h + 1)
                        if kind == "sw":
                            nc.vector.tensor_tensor(sums[:, h, :], sums[:, h, :], sinke[:, i, :], ALU.add)
                            dve.drain()
                        nc.vector.reciprocal(sums[:, h, :], sums[:, h, :])
                        dve.drain()
                        for t in range(NT):
                            last = nc.vector.tensor_scalar(p_sb[:, h % 2, t, :], p_sb[:, h % 2, t, :],
                                                           sums[:, h, t:t + 1], None, ALU.mult)
                        last.then_inc(S("att_probs"), 1)

                    def store(h):
                        dve.wait_ge(S("att_values"), h + 1)
                        o = heads[h][4]
                        nc.vector.tensor_copy(mixed[:, :, o:o + HD], view(bank[4 + h % 2][:, 0:1], (HD, NT), (1, HD))
                                              ).then_inc(S("att_out"), 1)

                    dve.wait_ge(S("sink_loaded"), 16)
                    nc.vector.tensor_scalar(nsink, sink, -1.0, None, ALU.mult)
                    scaled(0)
                    for h in range(NHD):
                        if h + 1 < NHD:
                            scaled(h + 1)
                        normalised(h)
                        if h >= 1:
                            store(h - 1)
                    store(NHD - 1)

                @b.scalar
                def _(act):
                    def exps(h):
                        kind, _, _, _, _, i = heads[h]
                        act.wait_ge(S("att_max"), h + 1)
                        if h >= 2:
                            act.wait_ge(S("att_turned"), h - 1)
                        if kind == "sw":
                            nc.scalar.activation(sinke[:, i, :], nmax[:, h, :], ACT.Exp, bias=sink[:, i:i + 1])
                        for t in range(NT):
                            last = nc.scalar.activation(p_sb[:, h % 2, t, :], s_sb[:, h % 2, t, :], ACT.Exp,
                                                        bias=nmax[:, h, t:t + 1], accum_out=sums[:, h, t:t + 1])
                        last.then_inc(S("att_exp"), 1)

                    def out_turned(h):
                        act.wait_ge(S("att_turned"), h + 1)
                        if h >= 2:
                            act.wait_ge(S("att_values"), h - 1)
                        nc.scalar.copy(pT[:, h % 2, :, :], view(bank[2 + h % 2][:, :], (T, 2), (1, T))
                                       ).then_inc(S("att_probsT"), 1)

                    exps(0)
                    for h in range(NHD):
                        if h + 1 < NHD:
                            exps(h + 1)
                        out_turned(h)

            turn_to_ht("mixT", mixed)
            m = shaped(mixed_at, NT, D)
            linear("out1", w_out, RING_AT, UNIT_AT, out_chunks,
                   lambda kind, t, n0, w: m[:, t, n0:n0 + w], preloaded=PIECES)
            add_normed("mix_post", m, mix_post, "mix_post_loaded", shaped(qkT_at, NT, D))

            up_raw_at, down_raw_at = RING_AT, RING_AT + 2 * 2048
            g_at = RING_AT + 6144
            up_raw = [shaped(up_raw_at + s * 2048, 4, 512) for s in range(2)]
            down_raw = [shaped(down_raw_at + s * 1024, 2, 512) for s in range(2)]
            up_hi = [[parts(UNIT_AT + (4 * s + u) * 1024, 512) for u in range(4)] for s in range(2)]
            up_lo = [[parts(UNIT_AT + (4 * s + u) * 1024 + 512, 512) for u in range(4)] for s in range(2)]
            down_hi = [[parts(qkT_at + (2 * s + u) * 1024, 512) for u in range(2)] for s in range(2)]
            down_lo = [[parts(qkT_at + (2 * s + u) * 1024 + 512, 512) for u in range(2)] for s in range(2)]
            g_hi = [parts(g_at + s * 512, T) for s in range(2)]
            g_lo = [parts(g_at + s * 512 + T, T) for s in range(2)]
            us = [shaped(Z_AT + s * 512, 2, T) for s in range(2)]
            cc = [shaped(Z_AT + 1024 + s * 512, 2, T) for s in range(2)]
            ge = [arena(Z_AT + 2048 + s * T, T) for s in range(2)]
            conv = shaped(Z_AT + 2560, NF, 8)
            w_up = a["w_up_tiles"]
            w_down = a["w_down"]

            def load_up(sp, j, s):
                sp.dma_start(arena(up_raw_at + s * 2048, 2048), w_up[l, j, :, :]).then_inc(S(f"up_loaded{s}"), 16)

            def load_down(sp, j, s):
                sp.dma_start(arena(down_raw_at + s * 1024, D), w_down[l, bass.ds(j * P, P), :]
                             ).then_inc(S(f"down_loaded{s}"), 16)

            def ffn_early(sp):
                for s in range(2):
                    load_up(sp, s, s)
                    load_down(sp, s, s)
                sp.dma_start(arena(Z_AT + 2560, NF * 8), a["conv_params"][l, :, :]).then_inc(S("conv_loaded"), 16)

            norm_to_ht("ffn", l, 1, mixed_at, qkT_at, ffn_early)
            with nc.Block() as b:
                @b.sync
                def _(sp):
                    with sp.Fori(1, NF // 2) as it:
                        for s in range(2):
                            j = it * 2 + s
                            sp.wait_ge(S("up_lo"), it * 8 + 4 * (s - 1))
                            load_up(sp, j, s)
                            sp.wait_ge(S("down_lo"), it * 4 + 2 * (s - 1))
                            load_down(sp, j, s)

                @b.tensor
                def _(pe):
                    pe.sem_inc(S("up_used"), 2)
                    pe.sem_inc(S("down_used"), 2)
                    for y in range(4):
                        nc.tensor.matmul(bank[y][:, :], ZERO[:, 0:P], ZERO[:, :], start=True, stop=False,
                                         skip_group_check=True)

                    def up(s, j):
                        pe.wait_ge(S("ubank_free"), j)
                        for u in range(4):
                            pe.wait_ge(S("up_lo"), j * 4 + (u - 3))
                            side, half = u // 2, u % 2
                            for k in range(4):
                                c = slice(k * P, (k + 1) * P)
                                last = mm3(bank[4 + s][:, side * T:(side + 1) * T], up_hi[s][u][:, c],
                                           up_lo[s][u][:, c], HT_HI[:, 4 * half + k, :], HT_LO[:, 4 * half + k, :],
                                           u % 2 == 0 and k == 0, u % 2 == 1 and k == 3)
                        last.then_inc(S("up_used"), 1)

                    def down(s, j, stop=False):
                        pe.wait_ge(S("g_ready"), j)
                        for n in range(2):
                            pe.wait_ge(S("down_lo"), j * 2 + (n - 1))
                            for t in range(NT):
                                c = slice(t * P, (t + 1) * P)
                                last = mm3(bank[2 * t + n][:, :], g_hi[s][:, c], g_lo[s][:, c], down_hi[s][n],
                                           down_lo[s][n], False, stop)
                        last.then_inc(S("down_used"), 1)

                    up(0, 1)
                    with pe.Fori(0, NF // 2 - 1) as it:
                        up(1, it * 2 + 2)
                        down(0, it * 2 + 1)
                        up(0, it * 2 + 3)
                        down(1, it * 2 + 2)
                    up(1, NF)
                    down(0, NF - 1)
                    down(1, NF, stop=True)

                @b.scalar
                def _(act):
                    act.sem_inc(S("ubank_free"), 2)
                    act.wait_ge(S("conv_loaded"), 16)

                    def split_up(s, j, turn):
                        act.wait_ge(S(f"up_loaded{s}"), turn)
                        act.wait_ge(S("up_used"), j)
                        for u in range(4):
                            nc.scalar.copy(up_hi[s][u], up_raw[s][:, u, :]).then_inc(S("up_hi"), 1)

                    def split_down(s, j, turn):
                        act.wait_ge(S(f"down_loaded{s}"), turn)
                        act.wait_ge(S("down_used"), j)
                        for n in range(2):
                            nc.scalar.copy(down_hi[s][n], down_raw[s][:, n, :]).then_inc(S("down_hi"), 1)

                    def take_u(s, j, j0):
                        act.wait_ge(S("up_used"), j + 2)
                        act.wait_ge(S("us_free"), j)
                        nc.scalar.copy(us[s], view(bank[4 + s][:, :], (T, 2), (1, T)))
                        for side in range(2):
                            w1 = conv[:, j0, 4 * side + 1:4 * side + 2]
                            b1 = conv[:, j0, 4 * side + 3:4 * side + 4]
                            last = nc.scalar.activation(cc[s][:, side, :], bank[4 + s][:, side * T:(side + 1) * T],
                                                        ACT.Identity, bias=b1, scale=w1)
                        last.then_inc(S("ubank_free"), 1)

                    def gelu(s, j):
                        act.wait_ge(S("conv_ready"), j)
                        nc.scalar.activation(ge[s], cc[s][:, 0, :], ACT.Gelu_apprx_tanh).then_inc(S("gelu_ready"), 1)

                    split_up(0, 1, 16)
                    split_up(1, 2, 16)
                    split_down(0, 1, 16)
                    take_u(0, 1, 0)
                    split_up(0, 3, 32)
                    with act.Fori(0, NF // 2 - 2) as it:
                        for s in range(2):
                            gelu(s, it * 2 + (s + 1))
                            split_down(1 - s, it * 2 + (s + 2), it * 16 + 16 * (s + 1))
                            take_u(1 - s, it * 2 + (s + 2), it * 2 + (s + 1))
                            split_up(1 - s, it * 2 + (s + 4), it * 16 + 16 * (s + 2))
                    for j in range(NF - 4, NF):
                        s = j % 2
                        gelu(s, j + 1)
                        if j + 1 < NF:
                            split_down(1 - s, j + 2, 16 * ((j + 1) // 2 + 1))
                            take_u(1 - s, j + 2, j + 1)
                        if j + 3 < NF:
                            split_up(1 - s, j + 4, 16 * ((j + 3) // 2 + 1))
                    for t in range(NT):
                        act.wait_ge(S("down_used"), NF + 2)
                        nc.scalar.copy(m[:, t, 0:512], bank[2 * t][:, :])

                @b.vector
                def _(dve):
                    dve.sem_inc(S("us_free"), 2)
                    dve.wait_ge(S("conv_loaded"), 16)

                    def split_up(s, j):
                        for u in range(4):
                            dve.wait_ge(S("up_hi"), j * 4 + (u - 3))
                            nc.vector.tensor_tensor(up_lo[s][u], up_raw[s][:, u, :], up_hi[s][u], ALU.subtract
                                                    ).then_inc(S("up_lo"), 1)

                    def split_down(s, j):
                        for n in range(2):
                            dve.wait_ge(S("down_hi"), j * 2 + (n - 1))
                            nc.vector.tensor_tensor(down_lo[s][n], down_raw[s][:, n, :], down_hi[s][n],
                                                    ALU.subtract).then_inc(S("down_lo"), 1)

                    def convolve(s, j, j0):
                        dve.wait_ge(S("ubank_free"), j + 2)
                        for tap, to, frm in ((0, slice(1, T), slice(0, T - 1)), (2, slice(0, T - 1), slice(1, T))):
                            for side in range(2):
                                u, c = us[s][:, side, :], cc[s][:, side, :]
                                w = conv[:, j0, 4 * side + tap:4 * side + tap + 1]
                                last = nc.vector.scalar_tensor_tensor(c[:, to], u[:, frm], w, c[:, to],
                                                                      ALU.mult, ALU.add)
                            if tap == 0:
                                dve.drain()
                        last.then_inc(S("conv_ready"), 1)

                    def gated(s, j):
                        dve.wait_ge(S("gelu_ready"), j)
                        nc.vector.tensor_tensor(ge[s], ge[s], cc[s][:, 1, :], ALU.mult)
                        dve.drain()
                        dve.wait_ge(S("down_used"), j)
                        nc.vector.tensor_copy(g_hi[s], ge[s])
                        dve.drain()
                        nc.vector.tensor_tensor(g_lo[s], ge[s], g_hi[s], ALU.subtract).then_inc(S("g_ready"), 1)
                        dve.drain()
                        dve.sem_inc(S("us_free"), 1)

                    split_up(0, 1)
                    split_up(1, 2)
                    split_down(0, 1)
                    with dve.Fori(0, NF // 2 - 1) as it:
                        for s in range(2):
                            convolve(s, it * 2 + (s + 1), it * 2 + s)
                            split_up(s, it * 2 + (s + 3))
                            gated(s, it * 2 + (s + 1))
                            split_down(1 - s, it * 2 + (s + 2))
                    convolve(0, NF - 1, NF - 2)
                    gated(0, NF - 1)
                    split_down(1, NF)
                    convolve(1, NF, NF - 1)
                    gated(1, NF)
                    for t in range(NT):
                        dve.wait_ge(S("down_used"), NF + 2)
                        nc.vector.tensor_copy(m[:, t, 512:D], bank[2 * t + 1][:, :])
            add_normed("ffn_post", m, ffn_post, "ffn_post_loaded", shaped(qkT_at, NT, D))
            clear_all()

        def second_layer(l):
            at = 0

            def take(n):
                nonlocal at
                at += n
                assert at <= EXTRA_AT, at
                return at - n

            z = shaped(take(NT * Z2), NT, Z2)
            RING_AT = take(PIECES * PIECE_N)
            UNIT_AT = take(UNITS * UNIT_N)
            qkc_at = take(6 * T)
            qkc = shaped(qkc_at, 6, T)
            qkm = shaped(take(6 * T), 6, T)
            sbT = shaped(take(6 * T), 6, T)
            sq_at = take(NT * D)
            ycat = shaped(take(NT * D), NT, D)
            xn_at = take(4096)
            sgm = shaped(xn_at + NT * D, 6, T)
            work_at = xn_at
            vaug = shaped(take(NT * NH6 * 65), NT, NH6, 65)
            sgw = shaped(take(SGG * P), SGG, P)
            uv = shaped(take(NT * 512), NT, 512)
            og = shaped(take(NT * 384), NT, 384)
            sbg = arena(take(768), 768)
            svg = arena(take(256), 256)
            outg = arena(take(D), D)
            conv = shaped(take(32), 6, 5)
            ifb = arena(take(2), 2)
            sgb = arena(take(4), 4)
            row_at = take(8 * T)

            def row(i):
                return ARENA[0:NH6, row_at + i * T:row_at + (i + 1) * T]

            w_in = a["w_in_2"][l].rearrange("(k p) n -> p k n", p=P)
            w_out = a["w_out_2"][l].rearrange("(k p) n -> p k n", p=P)
            in_chunks = [("rows", 0, 512, 0), ("rows", 512, 512, 512), ("rows", 1024, 128, 1024),
                         ("turned", 1152, 384, 0), ("turned", 1536, 384, 3),
                         ("rows", 1920, 512, 1152), ("rows", 2432, 512, 1664), ("rows", 2944, 268, 2176)]
            out_chunks = [("rows", n, 512, n) for n in range(0, D, 512)]

            def early_loads(sp):
                for q in range(PIECES):
                    linear_load(sp, "in2", w_in, RING_AT, in_chunks, q)
                sp.dma_start(ARENA[:, EXTRA_AT:EXTRA_AT + NCONST2], a["consts2"][:, :]).then_inc(S("mix2_params"), 16)
                one = lambda name, n: a[name][bass.ds(l, 1), :].broadcast_to([P, n])
                sp.dma_start(sbg, one("sb_gain", 768)).then_inc(S("mix2_params"), 16)
                sp.dma_start(svg, one("sg_vn_g_2", 256)).then_inc(S("mix2_params"), 16)
                sp.dma_start(outg, one("out_g_2", D)).then_inc(S("mix2_params"), 16)
                sp.dma_start(conv, a["ml_conv"][l]).then_inc(S("mix2_params"), 16)
                sp.dma_start(ifb[0:NH6, :], a["ml_if_b"][l, :, :]).then_inc(S("mix2_params"), 16)
                sp.dma_start(sgb, a["sg_b_t"][l, :, :]).then_inc(S("mix2_params"), 16)
                sp.dma_start(sgw, a["sg_w_t"][l]).then_inc(S("mix2_params"), 16)
            N_PARAMS = 8 * 16

            def pick(kind, t, n0, w):
                return z[:, t, n0:n0 + w] if kind == "rows" else qkc[:, t, :]

            norm_to_ht("pre", l, 2, xn_at, sq_at, early_loads)
            linear("in2", w_in, RING_AT, UNIT_AT, in_chunks, pick, preloaded=PIECES)

            sbqk = view(z[:, 0:1, 0:1], (Z2, NT), (HD, 12), (1, HD))
            sq12 = view(arena(sq_at, 1), (768, NT), (HD, 12), (1, HD))
            sqf = view(arena(sq_at, 1), (768, NT), (1, 768))
            ss12 = view(STAT[:, 0:24], (12, NT), (1, 12))
            ss4 = view(STAT[:, 32:40], (4, NT), (1, 4))
            vsq = view(arena(xn_at, 1), (256, NT), (HD, 4), (1, HD))
            uvv = view(uv[:, 0:1, 256:257], (512, NT), (HD, 4), (1, HD))
            acol = view(STAT[:, 64:76], (6, NT), (1, 6))
            ecol = view(STAT[:, 80:92], (6, NT), (1, 6))
            with nc.Block() as b:
                @b.sync
                def _(sp):
                    for q in range(PIECES):
                        linear_load(sp, "out2", w_out, RING_AT, out_chunks, q)

                @b.scalar
                def _(act):
                    nc.scalar.activation(uv, z[:, :, SG_UV:SG_UV + 512], ACT.Gelu_apprx_tanh
                                         ).then_inc(S("uv_gelu"), 1)
                    nc.scalar.activation(og, z[:, :, ML_O:ML_O + 384], ACT.Sigmoid).then_inc(S("og_ready"), 1)
                    act.wait_ge(S("ml_conv_ready"), 1)
                    nc.scalar.activation(sgm, qkm, ACT.Sigmoid).then_inc(S("ml_sigmoid"), 1)
                    act.wait_ge(S("f_ready"), 1)
                    nc.scalar.activation(row(2), row(1), ACT.Abs)
                    act.drain()
                    nc.scalar.activation(row(2), row(2), ACT.Exp, scale=-1.0)
                    act.drain()
                    nc.scalar.activation(row(2), row(2), ACT.Ln, bias=1.0).then_inc(S("f_log"), 1)
                    act.wait_ge(S("m_ready"), 1)
                    nc.scalar.activation(row(6), row(6), ACT.Exp, scale=-1.0).then_inc(S("em_ready"), 1)
                    for g in range(6):
                        act.wait_ge(S("sb_turned"), g + 1)
                        nc.scalar.copy(sbT[:, g, :], bank[g % 2][:, 0:T]).then_inc(S("sbT_out"), 1)

                @b.gpsimd
                def _(pool):
                    pool.wait_ge(S("mix2_params"), N_PARAMS)
                    nc.gpsimd.tensor_tensor(sgw, sgw, const("tril_t", (0, SGG), (1, P)), ALU.mult)
                    pool.wait_ge(S("sb_squares"), 1)
                    pool_rstd(pool, STAT[:, 0:24], 1.0 / HD, 24).then_inc(S("sb_rstd"), 1)
                    pool.wait_ge(S("sgv_squares"), 1)
                    pool_rstd(pool, STAT[:, 32:40], 1.0 / HD, 8).then_inc(S("sgv_rstd"), 1)
                    nc.gpsimd.memset(vaug, 1.0)
                    pool.drain()
                    nc.gpsimd.tensor_copy(vaug[:, :, :, 0:HD],
                                          view(z[:, 0:1, ML_V:ML_V + 1], (Z2, NT), (HD, NH6), (1, HD)))

                @b.vector
                def _(dve):
                    tt = nc.vector.tensor_tensor
                    tt(sq12, sbqk, sbqk, ALU.mult)
                    dve.drain()
                    nc.vector.reduce_sum(ss12, sq12, AX).then_inc(S("sb_squares"), 1)
                    dve.wait_ge(S("if_turned"), 1)
                    dve.wait_ge(S("mix2_params"), N_PARAMS)
                    nc.vector.tensor_scalar(row(0), bank[7][0:NH6, 0:T], ifb[0:NH6, 0:1], None, ALU.add)
                    nc.vector.tensor_scalar(row(1), bank[7][0:NH6, T:2 * T], ifb[0:NH6, 1:2], None, ALU.add
                                            ).then_inc(S("f_ready"), 1)
                    for f in range(6):
                        nc.vector.tensor_scalar(qkm[:, f, :], qkc[:, f, :], conv[:, f, 3:4], conv[:, f, 4:5],
                                                ALU.mult, ALU.add)
                    for j in range(3):
                        dve.drain()
                        sh = 3 - j
                        for f in range(6):
                            last = nc.vector.scalar_tensor_tensor(
                                qkm[:, f, sh:T], qkc[:, f, 0:T - sh], conv[:, f, j:j + 1], qkm[:, f, sh:T],
                                ALU.mult, ALU.add)
                    last.then_inc(S("ml_conv_ready"), 1)
                    dve.wait_ge(S("sb_rstd"), 1)
                    tt(sq12, sbqk, view(ss12, (12, NT), (1, 12), (0, HD)), ALU.mult)
                    dve.drain()
                    tt(sqf, sqf, view(sbg, (0, NT), (1, 768)), ALU.mult).then_inc(S("sb_ready"), 1)
                    dve.wait_ge(S("f_log"), 1)
                    nc.vector.scalar_tensor_tensor(row(3), row(1), 0.0, row(2), ALU.min, ALU.subtract)
                    nc.vector.memset(row(7), 1.0)
                    dve.drain()
                    nc.vector.tensor_tensor_scan(row(4), row(7), row(3), 0.0, ALU.mult, ALU.add)
                    dve.drain()
                    tt(row(0), row(0), row(4), ALU.subtract)
                    nc.vector.memset(row(7), 0.0)
                    dve.drain()
                    nc.vector.tensor_tensor_scan(row(5), row(7), row(0), 0.0, ALU.max, ALU.max)
                    dve.drain()
                    tt(row(6), row(4), row(5), ALU.add).then_inc(S("m_ready"), 1)
                    dve.wait_ge(S("ml_sigmoid"), 1)
                    tt(qkm, qkm, sgm, ALU.mult)
                    dve.wait_ge(S("uv_gelu"), 1)
                    tt(vsq, uvv, uvv, ALU.mult)
                    dve.drain()
                    nc.vector.reduce_sum(ss4, vsq, AX).then_inc(S("sgv_squares"), 1)
                    dve.wait_ge(S("sgv_rstd"), 1)
                    tt(uvv, uvv, view(ss4, (4, NT), (1, 4), (0, HD)), ALU.mult)
                    dve.drain()
                    uvf = view(uv[:, 0:1, 256:257], (512, NT), (1, 256))
                    tt(uvf, uvf, view(svg, (0, NT), (1, 256)), ALU.mult)
                    dve.wait_ge(S("cols_turned"), 1)
                    nc.vector.tensor_copy(acol, view(bank[6][:, 0:1], (6, NT), (1, 6)))
                    nc.vector.tensor_copy(ecol, view(bank[6][:, 16:17], (6, NT), (1, 6)))

                @b.tensor
                def _(pe):
                    for side in range(2):
                        for t in range(NT):
                            last = nc.tensor.transpose(bank[7][0:NH6, side * T + t * P:side * T + (t + 1) * P],
                                                       z[:, t, ML_IF + side * NH6:ML_IF + (side + 1) * NH6], ident)
                    last.then_inc(S("if_turned"), 1)
                    pe.wait_ge(S("sb_ready"), 1)
                    for g in range(6):
                        if g >= 2:
                            pe.wait_ge(S("sbT_out"), g - 1)
                        for t in range(NT):
                            last = nc.tensor.transpose(bank[g % 2][:, t * P:(t + 1) * P],
                                                       sqf[:, t, g * P:(g + 1) * P], ident)
                        last.then_inc(S("sb_turned"), 1)
                    pe.wait_ge(S("em_ready"), 1)
                    id6 = ident[0:NH6, 0:NH6]
                    for t in range(NT):
                        nc.tensor.transpose(bank[6][:, t * 6:t * 6 + 6], row(0)[:, t * P:(t + 1) * P], id6)
                    for t in range(NT):
                        last = nc.tensor.transpose(bank[6][:, 16 + t * 6:22 + t * 6],
                                                   row(6)[:, t * P:(t + 1) * P], id6)
                    last.then_inc(S("cols_turned"), 1)

            zs = [shaped(work_at + i * 512, 2, T) for i in range(2)]
            lg = [shaped(work_at + 1024 + i * 512, 2, T) for i in range(2)]
            sp_ = [shaped(work_at + 2048 + i * 512, 2, T) for i in range(2)]
            wt = [shaped(work_at + 3072 + i * 512, 2, T) for i in range(2)]
            two = lambda bk: view(bk[:, :], (T, 2), (1, T))
            with nc.Block() as b:
                @b.tensor
                def _(pe):
                    def scores(h):
                        if h >= 2:
                            pe.wait_ge(S("sb_scaled"), h - 1)
                        p0 = (h % 2) * HD
                        qT, kT = sbT[p0:p0 + HD, h // 2, :], sbT[p0:p0 + HD, 3 + h // 2, :]
                        for k in range(2):
                            last = nc.tensor.matmul(bank[h % 2][:, k * T:(k + 1) * T], kT[:, k * P:(k + 1) * P],
                                                    qT, start=True, stop=True)
                        last.then_inc(S("sb_scores"), 1)

                    scores(0)
                    for h in range(NH6):
                        if h + 1 < NH6:
                            scores(h + 1)
                        pe.wait_ge(S("sb_soft"), h + 1)
                        if h >= 2:
                            pe.wait_ge(S("sb_arg"), h - 1)
                        sfx = bank[2 + h % 2]
                        nc.tensor.matmul(sfx[:, 0:T], const("suffix"), sp_[h % 2][:, 0, :], start=True, stop=False)
                        nc.tensor.matmul(sfx[:, 0:T], const("ones"), sp_[h % 2][:, 1, :], start=False, stop=True)
                        nc.tensor.matmul(sfx[:, T:2 * T], const("suffix"), sp_[h % 2][:, 1, :], start=True, stop=True
                                         ).then_inc(S("sb_suffix"), 1)
                        pe.wait_ge(S("sb_weight"), h + 1)
                        if h >= 2:
                            pe.wait_ge(S("sb_out"), h - 1)
                        for t in range(NT):
                            for k in range(t + 1):
                                last = nc.tensor.matmul(bank[4 + h % 2][:, t * HD:(t + 1) * HD],
                                                        wt[h % 2][:, k, t * P:(t + 1) * P],
                                                        z[:, k, SB_V + h * HD:SB_V + (h + 1) * HD],
                                                        start=(k == 0), stop=(k == t))
                        last.then_inc(S("sb_values"), 1)

                @b.vector
                def _(dve):
                    def scaled(h):
                        dve.wait_ge(S("sb_scores"), h + 1)
                        if h >= 2:
                            dve.wait_ge(S("sb_masked"), h - 1)
                        nc.vector.tensor_scalar(zs[h % 2], two(bank[h % 2]), HD ** -0.5, None, ALU.mult
                                                ).then_inc(S("sb_scaled"), 1)
                    scaled(0)
                    for h in range(NH6):
                        dve.wait_ge(S("sb_log"), h + 1)
                        nc.vector.scalar_tensor_tensor(lg[h % 2], zs[h % 2], 0.0, lg[h % 2], ALU.max, ALU.add)
                        dve.drain()
                        nc.vector.tensor_tensor(sp_[h % 2], lg[h % 2], const("strict01", (T, 2), (1, T)), ALU.mult
                                                ).then_inc(S("sb_soft"), 1)
                        if h + 1 < NH6:
                            scaled(h + 1)
                        dve.wait_ge(S("sb_suffix"), h + 1)
                        dve.wait_ge(S("sb_masked"), h + 1)
                        nc.vector.tensor_tensor(lg[h % 2], two(bank[2 + h % 2]), zs[h % 2], ALU.subtract
                                                ).then_inc(S("sb_arg"), 1)
                        dve.wait_ge(S("sb_values"), h + 1)
                        nc.vector.tensor_copy(ycat[:, :, h * HD:(h + 1) * HD],
                                              view(bank[4 + h % 2][:, 0:1], (HD, NT), (1, HD))
                                              ).then_inc(S("sb_out"), 1)

                @b.gpsimd
                def _(pool):
                    for h in range(NH6):
                        pool.wait_ge(S("sb_soft"), h + 1)
                        nc.gpsimd.tensor_tensor(zs[h % 2], zs[h % 2], const("strict_big", (T, 2), (1, T)),
                                                ALU.subtract).then_inc(S("sb_masked"), 1)

                @b.scalar
                def _(act):
                    def logs(h):
                        act.wait_ge(S("sb_scaled"), h + 1)
                        nc.scalar.activation(lg[h % 2], zs[h % 2], ACT.Abs)
                        act.drain()
                        nc.scalar.activation(lg[h % 2], lg[h % 2], ACT.Exp, scale=-1.0)
                        act.drain()
                        nc.scalar.activation(lg[h % 2], lg[h % 2], ACT.Ln, bias=1.0).then_inc(S("sb_log"), 1)
                    logs(0)
                    for h in range(NH6):
                        act.wait_ge(S("sb_arg"), h + 1)
                        nc.scalar.activation(wt[h % 2], lg[h % 2], ACT.Exp, scale=-1.0
                                             ).then_inc(S("sb_weight"), 1)
                        if h + 1 < NH6:
                            logs(h + 1)

            with nc.Block() as b:
                @b.tensor
                def _(pe):
                    def scores(h):
                        if h >= 2:
                            pe.wait_ge(S("ml_arg"), h - 1)
                            pe.wait_ge(S("ml_probs"), h - 1)
                        p0 = (h % 2) * HD
                        qT, kT = qkm[p0:p0 + HD, h // 2, :], qkm[p0:p0 + HD, 3 + h // 2, :]
                        nc.tensor.matmul(bank[h % 2][:, 0:T], const("pick", (1, P), parts=NH6, off=h * P), row(5),
                                         start=True, stop=True).then_inc(S("ml_m"), 1)
                        for k in range(2):
                            last = nc.tensor.matmul(bank[2 + h % 2][:, k * T:(k + 1) * T], kT[:, k * P:(k + 1) * P],
                                                    qT, start=True, stop=True)
                        last.then_inc(S("ml_scores"), 1)
                    scores(0)
                    for h in range(NH6):
                        if h + 1 < NH6:
                            scores(h + 1)
                        pe.wait_ge(S("ml_probs"), h + 1)
                        if h >= 2:
                            pe.wait_ge(S("ml_out"), h - 1)
                        for t in range(NT):
                            for k in range(t + 1):
                                last = nc.tensor.matmul(bank[4 + h % 2][:, t * 65:(t + 1) * 65],
                                                        sp_[h % 2][:, k, t * P:(t + 1) * P], vaug[:, k, h, :],
                                                        start=(k == 0), stop=(k == t))
                        last.then_inc(S("ml_values"), 1)
                    for c in range(NT):
                        for g in range(SGG):
                            last = nc.tensor.matmul(bank[6][:, (c * SGG + g) * HD:(c * SGG + g + 1) * HD],
                                                    sgw[:, g, :], uv[:, c, 256 + g * HD:256 + (g + 1) * HD],
                                                    start=True, stop=True)
                    last.then_inc(S("sg_gate"), 1)

                @b.vector
                def _(dve):
                    def arg(h):
                        dve.wait_ge(S("ml_m"), h + 1)
                        if h >= 2:
                            dve.wait_ge(S("ml_weight"), h - 1)
                        for k in range(2):
                            last = nc.vector.scalar_tensor_tensor(
                                lg[h % 2][:, k, :], bank[h % 2][:, 0:T], acol[:, k, h:h + 1],
                                const("causal_big", (T, 2), (1, T))[:, k, :], ALU.subtract, ALU.add)
                        last.then_inc(S("ml_arg"), 1)
                    arg(0)
                    for h in range(NH6):
                        if h + 1 < NH6:
                            arg(h + 1)
                        dve.wait_ge(S("ml_weight"), h + 1)
                        dve.wait_ge(S("ml_scores"), h + 1)
                        if h >= 2:
                            dve.wait_ge(S("ml_values"), h - 1)
                        nc.vector.scalar_tensor_tensor(sp_[h % 2], two(bank[2 + h % 2]), HD ** -0.5, wt[h % 2],
                                                       ALU.mult, ALU.mult).then_inc(S("ml_probs"), 1)
                        dve.wait_ge(S("ml_values"), h + 1)
                        den = STAT[:, 96 + 2 * h:98 + 2 * h]
                        ov = view(bank[4 + h % 2][:, 0:1], (65, NT), (1, 65))
                        nc.vector.tensor_scalar(den, view(bank[4 + h % 2][:, 64:65], (65, NT)), -1.0, None,
                                                ALU.mult)
                        dve.drain()
                        nc.vector.scalar_tensor_tensor(den, den, -1.0, den, ALU.mult, ALU.max)
                        dve.drain()
                        nc.vector.tensor_tensor(den, den, ecol[:, :, h], ALU.max)
                        dve.drain()
                        nc.vector.reciprocal(den, den)
                        dve.drain()
                        for t in range(NT):
                            o = (NH6 + h) * HD
                            last = nc.vector.tensor_scalar(ycat[:, t, o:o + HD], ov[:, t, 0:HD], den[:, t:t + 1],
                                                           None, ALU.mult)
                        last.then_inc(S("ml_out"), 1)
                    dve.wait_ge(S("sg_gate"), 1)
                    for g in range(SGG):
                        o = (2 * NH6 + g) * HD
                        nc.vector.scalar_tensor_tensor(
                            ycat[:, :, o:o + HD], view(bank[6][:, g * HD:g * HD + 1], (SGG * HD, NT), (1, HD)),
                            sgb[:, g:g + 1], uv[:, :, g * HD:(g + 1) * HD], ALU.add, ALU.mult)

                @b.scalar
                def _(act):
                    for h in range(NH6):
                        act.wait_ge(S("ml_arg"), h + 1)
                        if h >= 2:
                            act.wait_ge(S("ml_probs"), h - 1)
                        nc.scalar.activation(wt[h % 2], lg[h % 2], ACT.Exp, scale=-1.0).then_inc(S("ml_weight"), 1)

            ss16 = view(STAT[:, 128:160], (16, NT), (1, 16))
            sq16 = view(arena(sq_at, 1), (D, NT), (HD, 16), (1, HD))
            y16 = view(ycat, (D, NT), (HD, 16), (1, HD))
            with nc.Block() as b:
                @b.vector
                def _(dve):
                    tt = nc.vector.tensor_tensor
                    tt(sq16, y16, y16, ALU.mult)
                    dve.drain()
                    nc.vector.reduce_sum(ss16, sq16, AX).then_inc(S("y_squares"), 1)
                    dve.wait_ge(S("y_rstd"), 1)
                    tt(y16, y16, view(ss16, (16, NT), (1, 16), (0, HD)), ALU.mult)
                    dve.drain()
                    tt(ycat, ycat, view(outg, (0, NT), (1, D)), ALU.mult)
                    dve.drain()
                    ym = ycat[:, :, NH6 * HD:2 * NH6 * HD]
                    dve.wait_ge(S("og_ready"), 1)
                    tt(ym, ym, og, ALU.mult)

                @b.gpsimd
                def _(pool):
                    pool.wait_ge(S("y_squares"), 1)
                    pool_rstd(pool, STAT[:, 128:160], 1.0 / HD, 32).then_inc(S("y_rstd"), 1)

            turn_to_ht("mixT", ycat)
            m = shaped(xn_at, NT, D)

            def add_x(dve):
                dve.wait_ge(S("out2_taken_act"), 2)
                dve.drain()
                nc.vector.tensor_tensor(X[:, :, :], X[:, :, :], m[:, :, :], ALU.add)
            linear("out2", w_out, RING_AT, UNIT_AT, out_chunks,
                   lambda kind, t, n0, w: m[:, t, n0:n0 + w], preloaded=PIECES, extra_dve=add_x)
            peer(l)
            clear_all()

        def peer(l):
            G = shaped(0, T, P)
            GEND = T * P
            U_RAW, V_RAW = GEND, GEND + 2048
            U_PART, V_PART = GEND + 4096, GEND + 6144
            W_PART = GEND + 8192
            GA_AT = GEND + 9216
            SEL_AT = U_PART
            HOT_AT = SEL_AT + 3 * T
            sel = shaped(SEL_AT, 3, T)
            hot = shaped(HOT_AT, 2, 2, 4, P)
            bare = shaped(HOT_AT + 2048, 2, 2, P)
            two_numbers = shaped(HOT_AT + 2560, 2, 2)
            at = 0

            def take(n):
                nonlocal at
                at += n
                assert at <= GEND, at
                return at - n

            HT = shaped(take(KD * T), KD, T)
            q_ring = [shaped(take(2 * T), 2, T) for _ in range(2)]
            wq_at = take(4 * 1024)
            keys_at = take(NSET * NKEY)
            keysT = shaped(keys_at, PH, 2, NKEY)
            sc = [shaped(take(4 * NKEY), 2, NT, NKEY) for _ in range(2)]
            rest = shaped(take(4 * NKEY), 2, NT, NKEY)
            sv = shaped(take(64), 2, NT, TOPK)
            siu = shaped(take(64), 2, NT, TOPK).bitcast(U32)
            si = [shaped(take(64), 2, NT, TOPK) for _ in range(2)]
            best = shaped(take(2 * T), NT, T)
            rest2 = shaped(take(2 * T), NT, T)
            bv = shaped(take(32), NT, TOPK)
            bpu = shaped(take(32), NT, TOPK).bitcast(U32)
            ku = shaped(take(64), 2, NT, TOPK).bitcast(U32)
            kf = [shaped(take(64), 2, NT, TOPK) for _ in range(2)]
            eq = [shaped(take(1024), 2, NT * TOPK, TOPK) for _ in range(2)]
            idx = shaped(take(2 * NT * (PH + 1) * TOPK), 2, NT, PH + 1, TOPK)
            gate = shaped(take(T), NT, PH, TOPK)
            pad = arena(take(16), 1)
            xn_at, junk_at = take(NT * D), take(NT * D)

            def load_wq(sp, c, s):
                sp.dma_start(arena(wq_at + s * 1024, 1024), a["wq_tiles"][l, c, :, :]).then_inc(S(f"wq_loaded{s}"), 16)

            def router_loads(sp):
                for s in range(4):
                    load_wq(sp, s, s)
                sp.dma_start(arena(keys_at, NSET * NKEY), a["keys_t"][l, :, :]).then_inc(S("keys_loaded"), 16)

            norm_to_ht("peer", l, 3, xn_at, junk_at, router_loads, raw=HT)

            with nc.Block() as b:
                @b.sync
                def _(sp):
                    with sp.Fori(1, PH // 2) as it:
                        for s in range(4):
                            sp.wait_ge(S("q_filled"), it * 2 + (s // 2 - 1))
                            load_wq(sp, it * 4 + s, s)

                @b.tensor
                def _(pe):
                    pe.wait_ge(S("keys_loaded"), 16)

                    def queries(s, turn, h):
                        pe.wait_ge(S("q_taken"), h)
                        for side in range(2):
                            w = shaped(wq_at + (2 * s + side) * 1024, KD, P)
                            pe.wait_ge(S(f"wq_loaded{2 * s + side}"), turn)
                            for k in range(KD):
                                last = nc.tensor.matmul(bank[s][:, side * T:(side + 1) * T], w[:, k, :], HT[:, k, :],
                                                        start=(k == 0), stop=(k == KD - 1), skip_group_check=True)
                        last.then_inc(S("q_filled"), 1)

                    def score(s, h, h0):
                        pe.wait_ge(S("q_taken"), h + 2)
                        pe.wait_ge(S("sc_taken"), h)
                        for side in range(2):
                            for t in range(NT):
                                last = nc.tensor.matmul(bank[2 + s][:, (2 * side + t) * P:(2 * side + t + 1) * P],
                                                        q_ring[s][:, side, t * P:(t + 1) * P],
                                                        keysT[:, h0, side, :], start=True, stop=True,
                                                        skip_group_check=True)
                        last.then_inc(S("sc_filled"), 1)

                    queries(0, 16, 1)
                    with pe.Fori(0, PH // 2 - 1) as it:
                        queries(1, it * 16 + 16, it * 2 + 2)
                        score(0, it * 2 + 1, it * 2)
                        queries(0, it * 16 + 32, it * 2 + 3)
                        score(1, it * 2 + 2, it * 2 + 1)
                    queries(1, 8 * PH, PH)
                    score(0, PH - 1, PH - 2)
                    score(1, PH, PH - 1)

                @b.scalar
                def _(act):
                    act.sem_inc(S("q_taken"), 2)
                    act.sem_inc(S("sc_taken"), 2)
                    with act.Fori(0, PH // 2) as it:
                        for s in range(2):
                            act.wait_ge(S("q_filled"), it * 2 + (s + 1))
                            nc.scalar.copy(q_ring[s], view(bank[s][:, :], (T, 2), (1, T))).then_inc(S("q_taken"), 1)
                            act.wait_ge(S("sc_filled"), it * 2 + (s + 1))
                            act.wait_ge(S("sc_free"), it * 2 + (s + 1))
                            nc.scalar.copy(view(sc[s], (1, 4 * NKEY)), bank[2 + s][:, :]).then_inc(S("sc_taken"), 1)
                    act.wait_ge(S("gate_arg"), 1)
                    nc.scalar.activation(view(gate, (1, NT * P)), view(gate, (1, NT * P)), ACT.Exp
                                         ).then_inc(S("gate_exp"), 1)

                @b.vector
                def _(dve):
                    v = nc.vector
                    four = [(side, t) for side in range(2) for t in range(NT)]
                    dve.sem_inc(S("sc_free"), 2)

                    def sum_up(s, done, h1):
                        dve.wait_ge(S("si_free"), done)
                        for a_ in range(2):
                            v.reduce_sum(view(idx[:, a_, :, h1, :], ((PH + 1) * TOPK, NT), (1, TOPK)),
                                         view(eq[s][:, a_, :, :], (256, NT), (16, 16), (1, 16)), AX)

                    v.memset(view(eq[1], (1, 1024)), 0.0)
                    with dve.Fori(0, PH // 2) as it:
                        for s in range(2):
                            h = it * 2 + s
                            dve.wait_ge(S("sc_taken"), it * 2 + (s + 3))
                            v.memset(pad, 0.0)
                            for a_, t in four:
                                v.max(sv[:, a_, t, 0:8], sc[s][:, a_, t, :])
                            dve.drain()
                            for a_, t in four:
                                v.max_index(siu[:, a_, t, 0:8], sv[:, a_, t, 0:8], sc[s][:, a_, t, :])
                                v.match_replace(rest[:, a_, t, :], sv[:, a_, t, 0:8], sc[s][:, a_, t, :], -3e38)
                            dve.drain()
                            dve.sem_inc(S("sc_free"), 1)
                            for a_, t in four:
                                v.max(sv[:, a_, t, 8:16], rest[:, a_, t, :])
                            dve.drain()
                            for a_, t in four:
                                v.max_index(siu[:, a_, t, 8:16], sv[:, a_, t, 8:16], rest[:, a_, t, :])
                            for t in range(NT):
                                v.tensor_tensor(view(best[:, t, 0:1], (16, 16), (1, 16)),
                                                view(sv[:, 0, t, 0:1], (1, 16), (0, 16)),
                                                view(sv[:, 1, t, 0:1], (0, 16), (1, 16)), ALU.add)
                            dve.drain()
                            dve.wait_ge(S("si_free"), it * 2 + (s + 1))
                            v.tensor_copy(view(si[s], (1, 64)), view(siu, (1, 64)))
                            for t in range(NT):
                                v.max(bv[:, t, 0:8], best[:, t, :])
                            dve.drain()
                            for t in range(NT):
                                v.max_index(bpu[:, t, 0:8], bv[:, t, 0:8], best[:, t, :])
                                v.match_replace(rest2[:, t, :], bv[:, t, 0:8], best[:, t, :], -3e38)
                            dve.drain()
                            for t in range(NT):
                                v.max(bv[:, t, 8:16], rest2[:, t, :])
                            dve.drain()
                            for t in range(NT):
                                v.max_index(bpu[:, t, 8:16], bv[:, t, 8:16], rest2[:, t, :])
                            v.tensor_tensor(view(gate[:, :, h, 0:1], (P, NT), (1, 16)), bv,
                                            view(bv, (TOPK, NT), (0, 16)), ALU.subtract)
                            dve.drain()
                            flat = view(bpu, (1, 32))
                            v.tensor_scalar(view(ku[:, 0, :, :], (1, 32)), flat, 4, None, ALU.logical_shift_right)
                            v.tensor_scalar(view(ku[:, 1, :, :], (1, 32)), flat, 15, None, ALU.bitwise_and)
                            dve.drain()
                            v.tensor_copy(view(kf[s], (1, 64)), view(ku, (1, 64)))
                            dve.drain()
                            sum_up(1 - s, it * 2 + (s + 2), h)
                            for a_ in range(2):
                                last = v.tensor_tensor(eq[s][:, a_, :, :], view(kf[s][:, a_, :, :], (1, 32), (0, 16)),
                                                       const("iota", (0, 32), (1, 16)), ALU.is_equal)
                            last.then_inc(S("eq_ready"), 1)
                    sum_up(1, PH + 2, PH)
                    dve.sem_inc(S("gate_arg"), 1)
                    dve.wait_ge(S("gate_exp"), 1)
                    gs = STAT[:, 0:16]
                    g16 = view(gate, (16, 16), (1, 16))
                    v.reduce_sum(gs, g16, AX)
                    dve.drain()
                    v.reciprocal(gs, gs)
                    dve.drain()
                    v.tensor_tensor(g16, g16, view(gs, (1, 16), (0, 16)), ALU.mult)

                @b.gpsimd
                def _(pool):
                    pool.sem_inc(S("si_free"), 2)
                    with pool.Fori(0, PH // 2) as it:
                        for s in range(2):
                            pool.wait_ge(S("eq_ready"), it * 2 + (s + 1))
                            for a_ in range(2):
                                e = view(eq[s][:, a_, :, :], (256, NT), (16, 16), (1, 16))
                                last = nc.gpsimd.tensor_tensor(e, e, view(si[s][:, a_, :, :], (TOPK, NT), (0, 16), (1, 16)),
                                                               ALU.mult)
                            last.then_inc(S("si_free"), 1)

            def load_u(sp, j, s):
                sp.dma_start(arena(U_RAW + s * 1024, 1024), a["u_tiles"][l, j, :, :]).then_inc(S(f"u_loaded{s}"), 16)

            def load_v(sp, j, s):
                sp.dma_start(arena(V_RAW + s * 1024, 1024), a["v_tiles"][l, j, :, :]).then_inc(S(f"v_loaded{s}"), 16)

            with nc.Block() as b:
                @b.sync
                def _(sp):
                    for s in range(2):
                        load_u(sp, s, s)
                        load_v(sp, s, s)

                @b.tensor
                def _(pe):
                    srcs = [view(idx[:, a_, :, 1, :], ((PH + 1) * TOPK, NT), (1, P)) for a_ in range(2)] + [
                        view(gate, (P, NT), (1, P))]
                    for i, src in enumerate(srcs):
                        for t in range(NT):
                            last = nc.tensor.transpose(bank[i][:, t * P:(t + 1) * P], src[:, t, :], ident)
                        last.then_inc(S("sel_turned"), 1)

                @b.vector
                def _(dve):
                    for i in range(3):
                        dve.wait_ge(S("sel_turned"), i + 1)
                        nc.vector.tensor_copy(sel[:, i, :], bank[i][:, 0:T])

            with nc.Block() as b:
                def numbers(side, tok):
                    return sel[:, side, bass.ds(tok, 2)].unsqueeze(2).broadcast_to([P, 2, P])

                @b.vector
                def _(dve):
                    with dve.Fori(0, T // 8) as it:
                        for s in range(2):
                            tok = it * 8 + 4 * s
                            dve.wait_ge(S("hot_free"), it * 2 + (s + 1))
                            nc.vector.tensor_tensor(bare[:, s, :, :], const("iota", (0, 2), (1, P)),
                                                    numbers(0, tok + 2), ALU.is_equal).then_inc(S("hot_bare"), 1)
                            nc.vector.tensor_tensor(hot[:, s, 1, 0:2, :], const("iota", (0, 2), (1, P)),
                                                    numbers(1, tok), ALU.is_equal)
                            for i in range(2):
                                one = bass.ds(tok + i, 1)
                                last = nc.vector.tensor_scalar(hot[:, s, 0, i, :], const("iota"), sel[:, 0, one],
                                                               sel[:, 2, one], ALU.is_equal, ALU.mult)
                            last.then_inc(S("hot_ready"), 1)

                @b.gpsimd
                def _(pool):
                    with pool.Fori(0, T // 8) as it:
                        for s in range(2):
                            pool.wait_ge(S("hot_free"), it * 2 + (s + 1))
                            nc.gpsimd.tensor_copy(two_numbers[:, s, :], sel[:, 1, bass.ds(it * 8 + 4 * s + 2, 2)])
                            pool.drain()
                            for i in range(2):
                                last = nc.gpsimd.tensor_scalar(hot[:, s, 1, 2 + i, :], const("iota"),
                                                               two_numbers[:, s, i:i + 1], None, ALU.is_equal)
                            last.then_inc(S("hot_ready_pool"), 1)

                @b.tensor
                def _(pe):
                    pe.sem_inc(S("hot_free"), 2)
                    with pe.Fori(0, T // 8) as it:
                        for s in range(2):
                            pe.wait_ge(S("g_taken"), it * 2 + (s + 1))
                            pe.wait_ge(S("hot_ready"), it * 2 + (s + 1))
                            pe.wait_ge(S("hot_ready_pool"), it * 2 + (s + 1))
                            pe.wait_ge(S("hot_ready_act"), it * 2 + (s + 1))
                            for i in range(4):
                                last = nc.tensor.matmul(bank[s][:, i * P:(i + 1) * P], hot[:, s, 0, i, :],
                                                        hot[:, s, 1, i, :], start=True, stop=True,
                                                        skip_group_check=True)
                            last.then_inc(S("hot_free"), 1)

                @b.scalar
                def _(act):
                    act.sem_inc(S("g_taken"), 2)

                    def gates(s, n, tok):
                        act.wait_ge(S("hot_bare"), n)
                        for i in range(2):
                            last = nc.scalar.mul(hot[:, s, 0, 2 + i, :], bare[:, s, i, :],
                                                 sel[:, 2, bass.ds(tok + 2 + i, 1)])
                        last.then_inc(S("hot_ready_act"), 1)

                    def take_g(s, n, tok):
                        act.wait_ge(S("hot_free"), n + 2)
                        nc.scalar.copy(G[:, bass.ds(tok, 4), :], view(bank[s][:, :], (P, 4), (1, P))
                                       ).then_inc(S("g_taken"), 1)

                    gates(0, 1, 0)
                    with act.Fori(0, T // 8 - 1) as it:
                        gates(1, it * 2 + 2, it * 8 + 4)
                        take_g(0, it * 2 + 1, it * 8)
                        gates(0, it * 2 + 3, it * 8 + 8)
                        take_g(1, it * 2 + 2, it * 8 + 4)
                    gates(1, T // 4, T - 4)
                    take_g(0, T // 4 - 1, T - 8)
                    take_g(1, T // 4, T - 4)

            NE = NKEY
            u_raw = [shaped(U_RAW + s * 1024, 2, 512) for s in range(2)]
            v_raw = [shaped(V_RAW + s * 1024, 2, 512) for s in range(2)]
            u_hi = [parts(U_PART + i * 1024, 512) for i in range(2)]
            u_lo = [parts(U_PART + i * 1024 + 512, 512) for i in range(2)]
            v_hi = [parts(V_PART + i * 1024, 512) for i in range(2)]
            v_lo = [parts(V_PART + i * 1024 + 512, 512) for i in range(2)]
            w_hi = [parts(W_PART + s * 512, T) for s in range(2)]
            w_lo = [parts(W_PART + s * 512 + T, T) for s in range(2)]
            ga = [arena(GA_AT + s * T, T) for s in range(2)]

            with nc.Block() as b:
                @b.sync
                def _(sp):
                    for s in range(2):
                        sp.wait_ge(S("u_lo"), 2 * s + 2)
                        load_u(sp, s + 2, s)
                    with sp.Fori(1, NE // 2 - 1) as it:
                        for s in range(2):
                            j = it * 2 + s
                            sp.wait_ge(S("v_lo"), it * 4 + 2 * (s - 1))
                            load_v(sp, j, s)
                            sp.wait_ge(S("u_lo"), it * 4 + 2 * (s + 1))
                            load_u(sp, j + 2, s)
                    for s in range(2):
                        sp.wait_ge(S("v_lo"), 2 * (NE - 3 + s))
                        load_v(sp, NE - 2 + s, s)

                @b.tensor
                def _(pe):
                    pe.sem_inc(S("u_used"), 2)
                    pe.sem_inc(S("v_used"), 4)
                    for y in range(4):
                        nc.tensor.matmul(bank[y][:, :], ZERO[:, 0:P], ZERO[:, :], start=True, stop=False,
                                         skip_group_check=True)

                    def acts(s, j):
                        pe.wait_ge(S("act_taken"), j)
                        for i in range(2):
                            pe.wait_ge(S("u_lo"), j * 2 + (i - 1))
                            for k in range(4):
                                c = slice(k * P, (k + 1) * P)
                                last = mm3(bank[4 + s][:, 0:T], u_hi[i][:, c], u_lo[i][:, c],
                                           HT_HI[:, 4 * i + k, :], HT_LO[:, 4 * i + k, :],
                                           i == 0 and k == 0, i == 1 and k == 3)
                            last.then_inc(S("u_used"), 1)

                    def ys(s, j, stop=False):
                        pe.wait_ge(S("weight_ready"), j)
                        for n in range(2):
                            pe.wait_ge(S("v_lo"), j * 2 + (n - 1))
                            for t in range(NT):
                                c = slice(t * P, (t + 1) * P)
                                last = mm3(bank[2 * t + n][:, :], w_hi[s][:, c], w_lo[s][:, c], v_hi[n], v_lo[n],
                                           False, stop)
                            last.then_inc(S("v_used"), 1)

                    acts(0, 1)
                    with pe.Fori(0, NE // 2 - 1) as it:
                        acts(1, it * 2 + 2)
                        ys(0, it * 2 + 1)
                        acts(0, it * 2 + 3)
                        ys(1, it * 2 + 2)
                    acts(1, NE)
                    ys(0, NE - 1)
                    ys(1, NE, stop=True)

                @b.scalar
                def _(act):
                    act.sem_inc(S("act_taken"), 2)

                    def split_u(s, j, turn):
                        act.wait_ge(S(f"u_loaded{s}"), turn)
                        for i in range(2):
                            act.wait_ge(S("u_used"), j * 2 + (i - 1))
                            nc.scalar.copy(u_hi[i], u_raw[s][:, i, :]).then_inc(S("u_hi"), 1)

                    def gelu(s, j):
                        act.wait_ge(S("u_used"), j * 2 + 2)
                        act.wait_ge(S("ga_free"), j)
                        nc.scalar.activation(ga[s], bank[4 + s][:, 0:T], ACT.Gelu_apprx_tanh
                                             ).then_inc(S("act_taken"), 1)

                    def split_v(s, j, turn):
                        act.wait_ge(S(f"v_loaded{s}"), turn)
                        for i in range(2):
                            act.wait_ge(S("v_used"), j * 2 + (i + 1))
                            nc.scalar.copy(v_hi[i], v_raw[s][:, i, :]).then_inc(S("v_hi"), 1)

                    split_u(0, 1, 16)
                    split_u(1, 2, 16)
                    with act.Fori(0, NE // 2 - 1) as it:
                        for s in range(2):
                            gelu(s, it * 2 + (s + 1))
                            split_v(s, it * 2 + (s + 1), it * 16 + 16)
                            split_u(s, it * 2 + (s + 3), it * 16 + 32)
                    for s in range(2):
                        gelu(s, NE - 1 + s)
                        split_v(s, NE - 1 + s, 8 * NE)

                @b.vector
                def _(dve):
                    dve.sem_inc(S("ga_free"), 2)

                    def split_u(s, j):
                        for i in range(2):
                            dve.wait_ge(S("u_hi"), j * 2 + (i - 1))
                            nc.vector.tensor_tensor(u_lo[i], u_raw[s][:, i, :], u_hi[i], ALU.subtract
                                                    ).then_inc(S("u_lo"), 1)

                    def split_v(s, j):
                        for i in range(2):
                            dve.wait_ge(S("v_hi"), j * 2 + (i - 1))
                            nc.vector.tensor_tensor(v_lo[i], v_raw[s][:, i, :], v_hi[i], ALU.subtract
                                                    ).then_inc(S("v_lo"), 1)

                    def weight(s, j, j0):
                        dve.wait_ge(S("act_taken"), j + 2)
                        nc.vector.tensor_tensor(ga[s], ga[s], G[:, :, j0], ALU.mult)
                        dve.drain()
                        dve.wait_ge(S("v_used"), j * 2)
                        nc.vector.tensor_copy(w_hi[s], ga[s])
                        dve.drain()
                        nc.vector.tensor_tensor(w_lo[s], ga[s], w_hi[s], ALU.subtract).then_inc(S("weight_ready"), 1)
                        dve.drain()
                        dve.sem_inc(S("ga_free"), 1)

                    split_u(0, 1)
                    split_u(1, 2)
                    with dve.Fori(0, NE // 2 - 1) as it:
                        for s in range(2):
                            weight(s, it * 2 + (s + 1), it * 2 + s)
                            split_v(s, it * 2 + (s + 1))
                            split_u(s, it * 2 + (s + 3))
                    for s in range(2):
                        weight(s, NE - 1 + s, NE - 2 + s)
                        split_v(s, NE - 1 + s)
                    dve.wait_ge(S("v_used"), 2 * NE + 4)
                    for t in range(NT):
                        for n in range(2):
                            xx = X[:, t, n * 512:(n + 1) * 512]
                            nc.vector.tensor_tensor(xx, xx, bank[2 * t + n][:, :], ALU.add)

        if 1 in blocks:
            with nc.Fori(0, L) as l:
                first_layer(l)
            for semaphore in semaphores.values():
                nc.release_semaphore(semaphore)
            semaphores.clear()
        if 2 in blocks:
            with nc.Fori(0, L) as l:
                second_layer(l)

        with nc.Block() as b:
            @b.sync
            def _(sp):
                sp.dma_start(out[0].rearrange("(t p) d -> p t d", p=P), X[:, :, :]).then_inc(S("stored"), 16)
                sp.wait_ge(S("stored"), 16)


def constants():
    c = [np.zeros((P, n), np.float32) for n in (NCONST, NCONST1, NCONST2)]

    def put(name, value):
        for array, plan in zip(c, (CONST, CONST1, CONST2)):
            if name in plan:
                at, width = plan[name]
                array[:, at:at + width] = np.asarray(value, np.float32).reshape(P, width)

    p = np.arange(P)
    tok = (np.arange(2)[None, :] * P + p[:, None])
    keys = np.arange(T)
    put("ident", np.eye(P))
    put("iota", np.broadcast_to(np.arange(P), (P, P)))
    col = tok % GRID
    start = np.clip(col - 8, 0, GRID - 16)[:, :, None]
    kc = keys[None, None, :] % GRID
    put("mask_na", np.where((kc >= start) & (kc < start + 16), 0.0, -BIG))
    put("mask_sw", np.where(np.abs(tok[:, :, None] - keys) <= 128, 0.0, -BIG))
    before = tok[:, :, None] < keys
    put("strict01", before)
    put("strict_big", np.where(before, 0.0, BIG))
    put("causal_big", np.where(tok[:, :, None] <= keys, 0.0, BIG))
    put("tril_t", p[:, None] <= p[None, :])
    put("suffix", p[:, None] >= p[None, :])
    put("ones", np.ones((P, P)))

    def angles(pos, dim):
        inv = np.float32(10000.0) ** (-np.arange(0, dim, 2, dtype=np.float32) / np.float32(dim))
        return (pos.astype(np.float32)[:, :, None] * inv.astype(np.float32)).astype(np.float32)

    for name, pos, dim in (("full", tok, 64), ("mla", tok, 32), ("row", tok // GRID, 32), ("col", tok % GRID, 32)):
        put("cos_" + name, np.cos(angles(pos, dim)))
        put("sin_" + name, np.sin(angles(pos, dim)))
    pick = np.zeros((P, NH6, P))
    for h in range(NH6):
        pick[h, h, :] = 1.0
    put("pick", pick)
    return c


def lay_out(i):
    f = {k: np.asarray(v) for k, v in i.items()}
    cols = lambda g: np.ascontiguousarray(g.reshape(L, -1, P).transpose(0, 2, 1))
    r = dict(zip(("consts", "consts1", "consts2"), constants()), x=f["x"])
    for k in ("w_in", "w_out", "w_down", "w_in_2", "w_out_2", "mla_w_uq", "mla_w_ukv", "sw_sink",
              "mix_post_gain", "ffn_post_gain", "out_g_2", "sg_vn_g_2"):
        r[k] = f[k]
    r["norm_gains"] = np.ascontiguousarray(np.stack(
        [f[k].reshape(L, KD, P) for k in ("mix_pre_gain", "ffn_pre_gain", "norm1_g_2", "norm2_g_2")]
    ).transpose(3, 0, 1, 2))
    r["mla_gain"] = np.concatenate([cols(f["mla_q_gain"]), cols(f["mla_kv_gain"])], axis=2)
    r["ax_gain"] = np.concatenate([np.tile(f["ax_q_gain"], (1, 4)), np.tile(f["ax_k_gain"], (1, 2))], axis=1)
    padded = np.zeros((L, 4, 15, 127), np.float32)
    padded[:, :, :, 48:79] = f["na_rpb"]
    c = np.arange(GRID)
    window = padded[:, :, :, c[None, :] - c[:, None] + 63]
    rows = np.stack([window[:, :, 7 - q:11 - q] for q in range(4)], axis=2)
    r["rpb_rows"] = np.ascontiguousarray(
        rows.reshape(L, 4, NT, 2, 4, GRID, GRID).transpose(0, 3, 5, 1, 2, 4, 6)).reshape(L, P, 4 * NT * T)
    r["w_up_tiles"] = np.ascontiguousarray(
        f["w_up"].reshape(L, KD, P, 2, NF, P).transpose(0, 4, 2, 3, 1, 5)).reshape(L, NF, P, 2 * KD * P)
    conv = np.concatenate([f["conv_w"], f["conv_b"][:, None]], axis=1)
    r["conv_params"] = np.ascontiguousarray(
        conv.reshape(L, 4, 2, NF, P).transpose(0, 4, 3, 2, 1)).reshape(L, P, NF * 8)
    r["sb_gain"] = np.concatenate([np.tile(f["sb_qn_g_2"], (1, NH6)), np.tile(f["sb_kn_g_2"], (1, NH6))], axis=1)
    conv = np.concatenate([f["ml_conv_w_2"], f["ml_conv_b_2"][:, None]], axis=1)
    r["ml_conv"] = np.ascontiguousarray(conv.reshape(L, 5, 6, P).transpose(0, 3, 2, 1))
    r["ml_if_b"] = np.ascontiguousarray(np.stack([f["ml_i_b_2"], f["ml_f_b_2"]], axis=2))
    r["sg_b_t"] = np.ascontiguousarray(f["sg_b_2"].transpose(0, 2, 1))
    r["sg_w_t"] = np.ascontiguousarray(f["sg_w_2"].transpose(0, 3, 1, 2))
    r["wq_tiles"] = np.ascontiguousarray(
        f["peer_wq_2"].reshape(L, KD, P, NSET, P).transpose(0, 3, 2, 1, 4)).reshape(L, NSET, P, KD * P)
    r["keys_t"] = np.ascontiguousarray(
        f["peer_keys_2"].reshape(L, NSET, NKEY, P).transpose(0, 3, 1, 2)).reshape(L, P, NSET * NKEY)
    r["u_tiles"] = np.ascontiguousarray(
        f["peer_u_2"].reshape(L, P, NKEY, KD, P).transpose(0, 2, 4, 3, 1)).reshape(L, NKEY, P, KD * P)
    r["v_tiles"] = np.ascontiguousarray(f["peer_v_2"].reshape(L, P, NKEY, D).transpose(0, 2, 1, 3))
    return r


def kernel(**inputs):
    import concourse.bacc as bacc
    from concourse.bass_utils import run_bass_kernel_spmd

    nc = bacc.Bacc("TRN2", target_bir_lowering=False, num_devices=1)
    arrays, args = {}, {}
    for name, v in lay_out(inputs).items():
        arrays[f"in_{name}"] = v
        args[name] = nc.dram_tensor(f"in_{name}", v.shape, mybir.dt.from_np(v.dtype), kind="ExternalInput").ap()
    out = nc.dram_tensor("out_x", (1, T, D), F32, kind="ExternalOutput").ap()
    build(nc, args, out)
    r = run_bass_kernel_spmd(nc, [arrays], core_ids=[0])
    return r.results[0]["out_x"]
```

```python
from contextlib import ExitStack

import numpy as np
import concourse.bass as bass
from concourse import mybir

F32 = mybir.dt.float32
F32R = mybir.dt.float32r
BF16 = mybir.dt.bfloat16
U32 = mybir.dt.uint32
ALU = mybir.AluOpType
ACT = mybir.ActivationFunctionType
AX = mybir.AxisListType.X

P = 128
T = 256
NT = T // P
D = 1024
KD = D // P
L = 2
HD = 64
EPS = 1e-6
BIG = 1e30
GRID = 64

A_Q, A_K, A_V = 0, 256, 512
B_CQ, B_CKV, B_KR = 768, 1024, 1152
C_Q, C_K, C_V = 1184, 1440, 1568
D_Q, D_K, D_V = 1696, 1952, 2080
IN1 = 2208
FF = 2816
NF = FF // P

MLQK, MLQK_W = 1152, 768
SB_Q, SB_K, SB_V = 0, 384, 768
ML_V, ML_O, ML_IF, SG_UV = 1152, 1536, 1920, 1932
IN2 = 3212
Z2 = IN2 - MLQK_W
NH6 = 6
SGG = 4

NSET = 16
PH = 8
TOPK = 16
NKEY = 128


def plan_of(sizes):
    plan, at = {}, 0
    for name, width in sizes:
        plan[name] = (at, width)
        at += width
    return plan, at


CONST, NCONST = plan_of([("ident", P), ("iota", P), ("tril_t", P), ("suffix", P), ("ones", P)])
CONST1, NCONST1 = plan_of([("mask_na", 2 * T), ("mask_sw", 2 * T), ("cos_full", 2 * 32), ("sin_full", 2 * 32),
                           ("cos_mla", 2 * 16), ("sin_mla", 2 * 16), ("cos_row", 2 * 16), ("sin_row", 2 * 16),
                           ("cos_col", 2 * 16), ("sin_col", 2 * 16)])
CONST2, NCONST2 = plan_of([("strict01", 2 * T), ("strict_big", 2 * T), ("causal_big", 2 * T),
                           ("pick", NH6 * P)])


def build(nc, a, out, blocks=(1, 2)):
    with ExitStack() as ctx:
        sb = lambda name, shape, dt=F32: ctx.enter_context(nc.sbuf_tensor(name, shape, dt))
        X = sb("X", [P, NT, D])
        HT_HI = sb("HT_HI", [P, KD, T], F32R)
        HT_LO = sb("HT_LO", [P, KD, T], F32R)
        CON = sb("CON", [P, NCONST])
        ZERO = sb("ZERO", [P, 512], BF16)
        STAT = sb("STAT", [P, 192])
        HALF = sb("HALF", [P, 64])
        GAINS = sb("GAINS", [P, 5, L, KD])
        ARENA_N = 45824
        arena_bytes = -(-nc.sbuf_base // 32) * 32
        ARENA = sb("ARENA", [P, ARENA_N])
        part_tensors = {}
        bank = [ctx.enter_context(nc.psum_tensor(f"bank{i}", [P, 512], F32)) for i in range(8)]

        semaphores = {}
        numbers_used = set()

        def S(name):
            if name not in semaphores:
                semaphores[name] = nc.alloc_semaphore(name)
                numbers_used.add(semaphores[name].num)
            return semaphores[name]

        def clear_all():
            nums = sorted(numbers_used)
            assert nums == list(range(nums[0], nums[-1] + 1)), nums
            nc.all_engine_barrier(sems_to_clear=range(nums[0], nums[-1] + 1))

        def view(ap, *dims, off=0):
            return bass.AP(ap.tensor, ap.offset + off, [list(ap.ap[0])] + [list(d) for d in dims])

        EXTRA_AT = ARENA_N - max(NCONST1, NCONST2)

        def const(name, *dims, parts=P, off=0):
            for plan, base in ((CONST, None), (CONST1, EXTRA_AT), (CONST2, EXTRA_AT)):
                if name in plan:
                    at, width = plan[name]
                    ap = CON[0:parts, at:at + width] if base is None else ARENA[0:parts, base + at:base + at + width]
                    return view(ap, *dims, off=off) if dims else ap

        ident = const("ident")

        def arena(at, n, parts=P):
            assert at + n <= ARENA_N, (at, n)
            return ARENA[0:parts, at:at + n]

        def shaped(at, *shape):
            n = int(np.prod(shape))
            ap = arena(at, n)
            strides = [int(np.prod(shape[i + 1:])) for i in range(len(shape))]
            return view(ap, *zip(strides, shape))

        def parts(at, n):
            assert at + n <= ARENA_N, (at, n)
            if (at, n) not in part_tensors:
                part_tensors[at, n] = nc.alloc_sbuf_tensor_at(f"PARTS{at}_{n}", [P, n], F32R,
                                                              offset=arena_bytes + 4 * at)
            return part_tensors[at, n][:, :]

        def mm3(out_ap, w_hi, w_lo, x_hi, x_lo, start, stop):
            mm = nc.tensor.matmul
            mm(out_ap, w_hi, x_hi, start=start, stop=False, skip_group_check=True)
            mm(out_ap, w_lo, x_hi, start=False, stop=False, skip_group_check=True)
            return mm(out_ap, w_hi, x_lo, start=False, stop=stop, skip_group_check=True)

        with nc.Block() as b:
            @b.sync
            def _(sp):
                sp.dma_start(CON[:, :], a["consts"][:, :]).then_inc(S("set_up_loaded"), 16)
                sp.dma_start(X[:, :, :], a["x"][0].rearrange("(t p) d -> p t d", p=P)
                             ).then_inc(S("set_up_loaded"), 16)
                sp.dma_start(GAINS[:, :, :, :], a["norm_gains"]).then_inc(S("set_up_loaded"), 16)
                sp.wait_ge(S("set_up_loaded"), 48)

            @b.vector
            def _(dve):
                nc.vector.memset(ZERO[:, :], 0.0)
                nc.vector.memset(HALF[:, :], -0.5)

        def pool_rstd(pool, ss, scale, n):
            nc.gpsimd.tensor_scalar(ss, ss, scale, EPS, ALU.mult, ALU.add)
            pool.drain()
            shape = [c for _, c in list(ss.ap)[1:]]
            h = view(HALF[:, 0:n], *([(shape[1], shape[0]), (1, shape[1])] if len(shape) == 2 else [(1, n)]))
            return nc.gpsimd.tensor_tensor(ss, ss, h, ALU.pow)

        def norm_to_ht(tag, l, which, xn_at, junk_at, extra_loads=None, raw=None):
            xn = shaped(xn_at, NT, D)
            junk = shaped(junk_at, NT, D)
            ss = STAT[:, 0:NT]

            def gain(k):
                return GAINS[:, which, l, k:k + 1]

            with nc.Block() as b:
                if extra_loads:
                    @b.sync
                    def _(sp):
                        extra_loads(sp)

                @b.scalar
                def _(act):
                    for t in range(NT):
                        nc.scalar.activation(junk[:, t, :], X[:, t, :], ACT.Square,
                                             accum_out=ss[:, t:t + 1]).then_inc(S(tag + "_squares"), 1)
                    for k in range(KD):
                        act.wait_ge(S(tag + "_turned"), k + 1)
                        if raw is not None and k % 2 == 0:
                            nc.scalar.mul(raw[:, k, :], bank[k][:, 0:T], gain(k))
                        nc.scalar.mul(HT_HI[:, k, :], bank[k][:, 0:T], gain(k)).then_inc(S(tag + "_hi"), 1)

                @b.gpsimd
                def _(pool):
                    for t in range(NT):
                        pool.wait_ge(S(tag + "_squares"), t + 1)
                        pool_rstd(pool, ss[:, t:t + 1], 1.0 / D, 1).then_inc(S(tag + "_rstd"), 1)

                @b.vector
                def _(dve):
                    for t in range(NT):
                        dve.wait_ge(S(tag + "_rstd"), t + 1)
                        nc.vector.tensor_scalar(xn[:, t, :], X[:, t, :], ss[:, t:t + 1], None, ALU.mult
                                                ).then_inc(S(tag + "_xn"), 1)
                    for k in range(KD):
                        dve.wait_ge(S(tag + "_hi"), k + 1)
                        if raw is not None and k % 2 == 1:
                            nc.vector.tensor_scalar(raw[:, k, :], bank[k][:, 0:T], gain(k), None, ALU.mult)
                        nc.vector.scalar_tensor_tensor(HT_LO[:, k, :], bank[k][:, 0:T], gain(k), HT_HI[:, k, :],
                                                       ALU.mult, ALU.subtract)

                @b.tensor
                def _(pe):
                    turn_all(pe, tag, xn)

        def turn_all(pe, tag, src):
            for t in range(NT):
                pe.wait_ge(S(tag + "_xn"), t + 1)
                for k in range(KD):
                    last = nc.tensor.transpose(bank[k][:, t * P:(t + 1) * P], src[:, t, k * P:(k + 1) * P], ident)
                    if t == NT - 1:
                        last.then_inc(S(tag + "_turned"), 1)

        PIECES, PIECE_N = 8, 2 * 512
        UNITS, UNIT_N = 8, 2 * 512

        def linear_load(sp, tag, w_view, raw_at, chunks, q):
            c, kp = q // (KD // 2), q % (KD // 2)
            _, n0, w, _ = chunks[c]
            dst = view(arena(raw_at + (q % PIECES) * PIECE_N, PIECE_N), (512, 2), (1, w))
            sp.dma_start(dst, w_view[:, 2 * kp:2 * kp + 2, n0:n0 + w]).then_inc(S(f"{tag}_w_loaded{q % PIECES}"), 16)

        def linear(tag, w_view, raw_at, unit_at, chunks, dst_of, preloaded=0, extra_loads=None, extra_dve=None):
            n_units = KD * len(chunks)
            fills = []
            for c, (kind, n0, w, d0) in enumerate(chunks):
                fills += [(c, i) for i in range(NT if kind == "rows" else w // P)]

            def unit(n):
                u = parts(unit_at + (n % UNITS) * UNIT_N, UNIT_N)
                w = chunks[n // KD][2]
                return u[:, 0:w], u[:, 512:512 + w]

            def raw(n):
                q = n // 2
                at = raw_at + (q % PIECES) * PIECE_N + (n % 2) * 512
                return arena(at, chunks[n // KD][2])

            def empty(eng, copy, who, c):
                mine = [m for m, (cc, _) in enumerate(fills) if cc == c and ("act", "dve")[m % 2] == who]
                if mine:
                    eng.wait_ge(S(tag + "_used"), KD * (c + 1))
                for m in mine:
                    i = fills[m][1]
                    kind, n0, w, d0 = chunks[c]
                    if kind == "rows":
                        to, frm = dst_of(kind, i, d0, w), bank[m % 8][:, 0:w]
                    else:
                        to, frm = dst_of(kind, d0 + i, 0, T), bank[m % 8][:, 0:T]
                    copy(to, frm).then_inc(S(f"{tag}_taken_{who}"), 1)

            with nc.Block() as b:
                @b.sync
                def _(sp):
                    if extra_loads:
                        extra_loads(sp)
                    for q in range(preloaded, n_units // 2):
                        if q >= PIECES:
                            sp.wait_ge(S(tag + "_lo"), 2 * (q - PIECES) + 2)
                        linear_load(sp, tag, w_view, raw_at, chunks, q)

                @b.scalar
                def _(act):
                    for n in range(n_units):
                        c, k = n // KD, n % KD
                        if k % 2 == 0:
                            act.wait_ge(S(f"{tag}_w_loaded{n // 2 % PIECES}"), 16 * (n // 2 // PIECES + 1))
                        if n >= UNITS:
                            act.wait_ge(S(tag + "_used"), n - UNITS + 1)
                        nc.scalar.copy(unit(n)[0], raw(n)).then_inc(S(tag + "_hi"), 1)
                        if k == 3 and c >= 1:
                            empty(act, nc.scalar.copy, "act", c - 1)
                    empty(act, nc.scalar.copy, "act", len(chunks) - 1)

                @b.vector
                def _(dve):
                    for n in range(n_units):
                        c, k = n // KD, n % KD
                        dve.wait_ge(S(tag + "_hi"), n + 1)
                        nc.vector.tensor_tensor(unit(n)[1], raw(n), unit(n)[0], ALU.subtract
                                                ).then_inc(S(tag + "_lo"), 1)
                        if k == 3 and c >= 1:
                            empty(dve, nc.vector.tensor_copy, "dve", c - 1)
                    empty(dve, nc.vector.tensor_copy, "dve", len(chunks) - 1)
                    if extra_dve:
                        extra_dve(dve)

                @b.tensor
                def _(pe):
                    for n in range(n_units):
                        c, k = n // KD, n % KD
                        kind, n0, w, d0 = chunks[c]
                        pe.wait_ge(S(tag + "_lo"), n + 1)
                        hi, lo = unit(n)
                        for m, (cc, i) in enumerate(fills):
                            if cc != c:
                                continue
                            if k == 0 and m >= 8:
                                pe.wait_ge(S(f"{tag}_taken_{('act', 'dve')[m % 2]}"), (m - 8) // 2 + 1)
                            tok = slice(i * P, (i + 1) * P)
                            if kind == "rows":
                                last = mm3(bank[m % 8][:, 0:w], HT_HI[:, k, tok], HT_LO[:, k, tok], hi, lo,
                                           k == 0, k == KD - 1)
                            else:
                                last = mm3(bank[m % 8][:, 0:T], hi[:, tok], lo[:, tok], HT_HI[:, k, :],
                                           HT_LO[:, k, :], k == 0, k == KD - 1)
                        last.then_inc(S(tag + "_used"), 1)

        def add_normed(tag, m, gain, gain_sem, junk):
            ss = STAT[:, 0:NT]
            with nc.Block() as b:
                @b.scalar
                def _(act):
                    for t in range(NT):
                        nc.scalar.activation(junk[:, t, :], m[:, t, :], ACT.Square,
                                             accum_out=ss[:, t:t + 1]).then_inc(S(tag + "_squares"), 1)

                @b.gpsimd
                def _(pool):
                    pool.wait_ge(S(tag + "_squares"), NT)
                    pool_rstd(pool, ss, 1.0 / D, NT).then_inc(S(tag + "_rstd"), 1)

                @b.vector
                def _(dve):
                    dve.wait_ge(S(tag + "_rstd"), 1)
                    dve.wait_ge(S(gain_sem), 16)
                    for t in range(NT):
                        nc.vector.scalar_tensor_tensor(m[:, t, :], m[:, t, :], ss[:, t:t + 1], gain,
                                                       ALU.mult, ALU.mult)
                    dve.drain()
                    nc.vector.tensor_tensor(X[:, :, :], X[:, :, :], m[:, :, :], ALU.add)

        def rope(dve, x1, x2, y1, y2, cos, sin, t1, t2):
            tt = nc.vector.tensor_tensor
            dve.drain()
            tt(t1, x1, cos, ALU.mult)
            tt(t2, x2, sin, ALU.mult)
            dve.drain()
            tt(y1, t1, t2, ALU.subtract)
            dve.drain()
            tt(t1, x2, cos, ALU.mult)
            tt(t2, x1, sin, ALU.mult)
            dve.drain()
            return tt(y2, t1, t2, ALU.add)

        def first_layer(l):
            Z_AT = 0
            RING_AT = Z_AT + NT * IN1
            UNIT_AT = RING_AT + PIECES * PIECE_N
            at = UNIT_AT + UNITS * UNIT_N

            def take(n):
                nonlocal at
                at += n
                assert at <= EXTRA_AT, at
                return at - n

            z = shaped(Z_AT, NT, IN1)
            bias_at = take(4 * NT * T)
            bias = shaped(bias_at, 4, NT, T)
            rot_c = shaped(take(NT * 6 * HD), NT, 6 * HD)
            rot_d = shaped(take(NT * 6 * HD), NT, 6 * HD)
            lat = shaped(take(NT * 384), NT, 384)
            latT = shaped(take(3 * T), 3, T)
            qb = shaped(take(NT * 384), NT, 384)
            kvb = shaped(take(NT * 512), NT, 512)
            kb = shaped(take(NT * 384), NT, 384)
            qkT_at = take(18 * T)
            qk_hi = view(parts(qkT_at, 18 * T), (T, 18), (1, T))
            qk_lo = view(parts(UNIT_AT, 18 * T), (T, 18), (1, T))
            mixed_at = take(NT * D)
            gains_at = take(8 + 4 + 384 + 4)
            post_gain_at = take(2 * D)
            w_uq = shaped(take(2 * 384), 2, 384)
            w_ukv = arena(take(512), 512)
            c_in_at = take(3 * NT * T)
            s_sb = shaped(c_in_at, 3, NT, T)
            p_sb = shaped(mixed_at, 3, NT, T)
            pT = shaped(take(2 * 2 * T), 2, 2, T)
            mla_gain = arena(gains_at + 8, 3)
            ax_gain = arena(gains_at + 12, 384)
            sink = arena(gains_at + 396, 4)
            mix_post = arena(post_gain_at, D)
            ffn_post = arena(post_gain_at + D, D)

            w_in = a["w_in"][l].rearrange("(k p) n -> p k n", p=P)
            w_out = a["w_out"][l].rearrange("(k p) n -> p k n", p=P)
            in_chunks = [("rows", n, min(512, IN1 - n), n) for n in range(0, IN1, 512)]
            out_chunks = [("rows", n, 512, n) for n in range(0, D, 512)]

            def early_loads(sp):
                for q in range(PIECES):
                    linear_load(sp, "in1", w_in, RING_AT, in_chunks, q)
                sp.dma_start(ARENA[:, EXTRA_AT:EXTRA_AT + NCONST1], a["consts1"][:, :]).then_inc(S("prep_params"), 16)
                sp.dma_start(mla_gain, a["mla_gain"][l, :, :]).then_inc(S("prep_params"), 16)
                sp.dma_start(ax_gain, a["ax_gain"][bass.ds(l, 1), :].broadcast_to([P, 384])).then_inc(S("prep_params"), 16)
                sp.dma_start(w_uq, a["mla_w_uq"][l].rearrange("(k p) n -> p k n", p=P)).then_inc(S("prep_params"), 16)
                sp.dma_start(w_ukv, a["mla_w_ukv"][l, :, :]).then_inc(S("prep_params"), 16)
                sp.dma_start(sink, a["sw_sink"][bass.ds(l, 1), :].broadcast_to([P, 4])).then_inc(S("sink_loaded"), 16)
                sp.dma_start(mix_post, a["mix_post_gain"][bass.ds(l, 1), :].broadcast_to([P, D])
                             ).then_inc(S("mix_post_loaded"), 16)
                sp.dma_start(ffn_post, a["ffn_post_gain"][bass.ds(l, 1), :].broadcast_to([P, D])
                             ).then_inc(S("ffn_post_loaded"), 16)
                sp.dma_start(arena(bias_at, 4 * NT * T), a["rpb_rows"][l, :, :]).then_inc(S("rpb_loaded"), 16)

            norm_to_ht("pre", l, 0, mixed_at, qkT_at, early_loads)
            linear("in1", w_in, RING_AT, UNIT_AT, in_chunks,
                   lambda kind, t, n0, w: z[:, t, n0:n0 + w], preloaded=PIECES)

            ssB = STAT[:, 0:4]
            ssC = view(STAT[:, 16:28], (6, NT), (1, 6))
            sq = shaped(mixed_at, NT, 6 * HD)
            c_in = shaped(c_in_at, NT, 6 * HD)
            t1_at = mixed_at + 768
            t2_at = t1_at + 400
            groups = []
            for g in range(2):
                groups.append((lambda t, g=g: z[:, t, A_Q + g * P:A_Q + (g + 1) * P], P))
            for g in range(2):
                groups.append((lambda t, g=g: z[:, t, A_K + g * P:A_K + (g + 1) * P], P))
            for rot in (rot_d, rot_c):
                for g in range(3):
                    groups.append((lambda t, g=g, rot=rot: rot[:, t, g * P:(g + 1) * P], P))
            for h in range(4):
                groups.append((lambda t, h=h: qb[:, t, h * 96:(h + 1) * 96], 96))
            for h in range(4):
                groups.append((lambda t, h=h: kb[:, t, h * 96:(h + 1) * 96], 96))
            READY = [0] * 4 + [1] * 3 + [2] * 3 + [3] * 8

            with nc.Block() as b:
                @b.sync
                def _(sp):
                    for q in range(PIECES):
                        linear_load(sp, "out1", w_out, RING_AT, out_chunks, q)

                @b.scalar
                def _(act):
                    junk = shaped(mixed_at + 1600, 256)
                    for t in range(NT):
                        nc.scalar.activation(junk, z[:, t, B_CQ:B_CQ + 256], ACT.Square,
                                             accum_out=ssB[:, t:t + 1])
                        act.drain()
                        nc.scalar.activation(junk[:, 0:128], z[:, t, B_CKV:B_CKV + 128], ACT.Square,
                                             accum_out=ssB[:, 2 + t:3 + t])
                        act.drain()
                    act.sem_inc(S("lat_squares"), 1)
                    act.wait_ge(S("prep_params"), 80)
                    for i in range(3):
                        act.wait_ge(S("lat_turned"), i + 1)
                        nc.scalar.mul(latT[:, i, :], bank[i][:, 0:T], mla_gain[:, i:i + 1]
                                      ).then_inc(S("latT_ready"), 1)
                    for t in range(NT):
                        act.wait_ge(S("lat_up"), 2 * t + 1)
                        nc.scalar.copy(qb[:, t, :], bank[4 + t][:, 0:384])
                        act.wait_ge(S("lat_up"), 2 * t + 2)
                        nc.scalar.copy(kvb[:, t, :], bank[6 + t][:, :]).then_inc(S("up_ready"), 1)
                    for g, (_, n) in enumerate(groups):
                        act.wait_ge(S("qk_turned"), g + 1)
                        nc.scalar.copy(qk_hi[0:n, g, :], bank[g % 4][0:n, 0:T]).then_inc(S("qk_hi"), 1)

                @b.gpsimd
                def _(pool):
                    pool.wait_ge(S("lat_squares"), 1)
                    nc.gpsimd.tensor_scalar(ssB[:, 0:2], ssB[:, 0:2], 1.0 / 256, EPS, ALU.mult, ALU.add)
                    nc.gpsimd.tensor_scalar(ssB[:, 2:4], ssB[:, 2:4], 1.0 / 128, EPS, ALU.mult, ALU.add)
                    pool.drain()
                    nc.gpsimd.tensor_tensor(ssB, ssB, HALF[:, 0:4], ALU.pow).then_inc(S("lat_rstd"), 1)
                    pool.wait_ge(S("ax_squares"), 1)
                    pool_rstd(pool, STAT[:, 16:28], 1.0 / HD, 12).then_inc(S("ax_rstd"), 1)
                    pool.wait_ge(S("rpb_loaded"), 16)
                    pool.wait_ge(S("prep_params"), 80)
                    for h in range(4):
                        nc.gpsimd.tensor_tensor(bias[:, h, :, :], bias[:, h, :, :],
                                                const("mask_na", (T, NT), (1, T)), ALU.add)

                @b.vector
                def _(dve):
                    tt = nc.vector.tensor_tensor

                    def low_parts(g0, g1):
                        for g in range(g0, g1):
                            n = groups[g][1]
                            dve.wait_ge(S("qk_hi"), g + 1)
                            tt(qk_lo[0:n, g, :], bank[g % 4][0:n, 0:T], qk_hi[0:n, g, :], ALU.subtract
                               ).then_inc(S("qk_lo"), 1)

                    dve.wait_ge(S("prep_params"), 80)
                    cqk = z[:, :, C_Q:C_Q + 384]
                    tt(sq, cqk, cqk, ALU.mult)
                    dve.drain()
                    nc.vector.reduce_sum(ssC, view(sq, (384, NT), (HD, 6), (1, HD)), AX
                                         ).then_inc(S("ax_squares"), 1)
                    dve.wait_ge(S("lat_rstd"), 1)
                    for t in range(NT):
                        nc.vector.tensor_scalar(lat[:, t, 0:256], z[:, t, B_CQ:B_CQ + 256], ssB[:, t:t + 1],
                                                None, ALU.mult)
                        nc.vector.tensor_scalar(lat[:, t, 256:384], z[:, t, B_CKV:B_CKV + 128],
                                                ssB[:, 2 + t:3 + t], None, ALU.mult).then_inc(S("lat_ready"), 1)
                    def half(src, stride, base, heads, width, w):
                        return view(src[:, 0:1, base:base + 1], (stride, NT), (width, heads), (1, w))
                    def tmp(base, heads, w):
                        return view(arena(base, 400), (heads * w, NT), (w, heads), (1, w))
                    def angle(name, heads, w):
                        return const(name, (w, NT), (0, heads), (1, w))
                    pairs = ((0, 2 * HD), (HD, 2 * HD), (4 * HD, HD))
                    for g, (c0, step) in enumerate(pairs):
                        rope(dve, half(z, IN1, D_Q + c0, 2, step, 32), half(z, IN1, D_Q + c0 + 32, 2, step, 32),
                             half(rot_d, 384, g * P, 2, HD, 32), half(rot_d, 384, g * P + 32, 2, HD, 32),
                             angle("cos_full", 2, 32), angle("sin_full", 2, 32),
                             tmp(t1_at, 2, 32), tmp(t2_at, 2, 32))
                    dve.drain()
                    dve.sem_inc(S("qk_source"), 1)
                    dve.wait_ge(S("ax_rstd"), 1)
                    c3 = view(cqk, (IN1, NT), (HD, 6), (1, HD))
                    tt(view(sq, (384, NT), (HD, 6), (1, HD)), c3, view(ssC, (6, NT), (1, 6), (0, HD)), ALU.mult)
                    dve.drain()
                    for g, (c0, step) in enumerate(pairs):
                        tt(half(c_in, 384, g * P, 2, HD, HD), half(sq, 384, c0, 2, step, HD),
                           view(ax_gain, (0, NT), (step, 2), (1, HD), off=c0), ALU.mult)
                    for base, ang in ((0, "row"), (32, "col")):
                        rope(dve, half(c_in, 384, base, 6, HD, 16), half(c_in, 384, base + 16, 6, HD, 16),
                             half(rot_c, 384, base, 6, HD, 16), half(rot_c, 384, base + 16, 6, HD, 16),
                             angle("cos_" + ang, 6, 16), angle("sin_" + ang, 6, 16),
                             tmp(t1_at, 6, 16), tmp(t2_at, 6, 16))
                    dve.drain()
                    dve.sem_inc(S("qk_source"), 1)
                    low_parts(0, 7)
                    dve.wait_ge(S("up_ready"), NT)
                    rope(dve, half(qb, 384, 64, 4, 96, 16), half(qb, 384, 80, 4, 96, 16),
                         half(sq, 384, 0, 4, 32, 16), half(sq, 384, 16, 4, 32, 16),
                         angle("cos_mla", 4, 16), angle("sin_mla", 4, 16), tmp(t1_at, 4, 16), tmp(t2_at, 4, 16))
                    dve.drain()
                    nc.vector.tensor_copy(half(qb, 384, 64, 4, 96, 32), half(sq, 384, 0, 4, 32, 32))
                    rope(dve, half(z, IN1, B_KR, 1, 32, 16), half(z, IN1, B_KR + 16, 1, 32, 16),
                         half(sq, 384, 128, 1, 32, 16), half(sq, 384, 144, 1, 32, 16),
                         angle("cos_mla", 1, 16), angle("sin_mla", 1, 16), tmp(t1_at, 1, 16), tmp(t2_at, 1, 16))
                    dve.drain()
                    nc.vector.tensor_copy(half(kb, 384, 64, 4, 96, 32), view(sq[:, 0:1, 128:129], (384, NT), (0, 4), (1, 32)))
                    nc.vector.tensor_copy(half(kb, 384, 0, 4, 96, HD), half(kvb, 512, 0, 4, P, HD)
                                          )
                    dve.drain()
                    dve.sem_inc(S("qk_source"), 1)
                    low_parts(7, 18)

                @b.tensor
                def _(pe):
                    pe.wait_ge(S("lat_ready"), NT)
                    for i in range(3):
                        for t in range(NT):
                            last = nc.tensor.transpose(bank[i][:, t * P:(t + 1) * P],
                                                       lat[:, t, i * P:(i + 1) * P], ident)
                        last.then_inc(S("lat_turned"), 1)
                    pe.wait_ge(S("prep_params"), 80)
                    pe.wait_ge(S("latT_ready"), 3)
                    for t in range(NT):
                        for k in range(2):
                            last = nc.tensor.matmul(bank[4 + t][:, 0:384], latT[:, k, t * P:(t + 1) * P],
                                                    w_uq[:, k, :], start=(k == 0), stop=(k == 1))
                        last.then_inc(S("lat_up"), 1)
                        nc.tensor.matmul(bank[6 + t][:, :], latT[:, 2, t * P:(t + 1) * P], w_ukv,
                                         start=True, stop=True).then_inc(S("lat_up"), 1)
                    for g, (src, n) in enumerate(groups):
                        if READY[g]:
                            pe.wait_ge(S("qk_source"), READY[g])
                        if g >= 4:
                            pe.wait_ge(S("qk_lo"), g - 3)
                        for t in range(NT):
                            last = nc.tensor.transpose(bank[g % 4][0:n, t * P:(t + 1) * P], src(t), ident)
                        last.then_inc(S("qk_turned"), 1)

            heads = []
            for h in range(4):
                heads.append(("na", h // 2, 2 + h // 2, (h % 2) * HD, HD,
                              lambda t, h=h: z[:, t, A_V + h * HD:A_V + (h + 1) * HD], h))
            for h in range(4):
                heads.append(("mla", 10 + h, 14 + h, 0, 96,
                              lambda t, h=h: kvb[:, t, h * P + HD:(h + 1) * P], h))
            for kind, g0, v0 in (("ax", 7, C_V), ("sw", 4, D_V)):
                for h in range(4):
                    heads.append((kind, g0 + h % 2, g0 + 2, (h // 2) * HD, HD,
                                  lambda t, h=h, v0=v0: z[:, t, v0 + h // 2 * HD:v0 + (h // 2 + 1) * HD], h))
            NHD = len(heads)
            nmax = view(STAT[:, 32:64], (2, NHD), (1, 2))
            sums = view(STAT[:, 64:96], (2, NHD), (1, 2))
            sinke = view(STAT[:, 96:104], (2, 4), (1, 2))
            nsink = STAT[:, 104:108]
            scale_of = {"na": HD ** -0.5, "mla": 96 ** -0.5, "ax": HD ** -0.5, "sw": HD ** -0.5}
            score_bank = [bank[0], bank[1], bank[6]]

            with nc.Block() as b:
                @b.tensor
                def _(pe):
                    def scores(h):
                        if h >= 3:
                            pe.wait_ge(S("att_scaled"), h - 2)
                        _, gq, gk, p0, n, _, _ = heads[h]
                        for t in range(NT):
                            tok = slice(t * P, (t + 1) * P)
                            last = mm3(score_bank[h % 3][:, t * T:(t + 1) * T],
                                       qk_hi[p0:p0 + n, gq, tok], qk_lo[p0:p0 + n, gq, tok],
                                       qk_hi[p0:p0 + n, gk, :], qk_lo[p0:p0 + n, gk, :], True, True)
                        last.then_inc(S("att_scores"), 1)

                    def turn(h):
                        pe.wait_ge(S("att_probs"), h + 1)
                        pe.wait_ge(S("att_probs_pool"), h + 1)
                        if h >= 2:
                            pe.wait_ge(S("att_probsT"), h - 1)
                        for t in range(NT):
                            for k in range(2):
                                last = nc.tensor.transpose(bank[2 + h % 2][:, k * T + t * P:k * T + (t + 1) * P],
                                                           p_sb[:, h % 3, t, k * P:(k + 1) * P], ident)
                        last.then_inc(S("att_turned"), 1)

                    def values(h):
                        pe.wait_ge(S("att_probsT"), h + 1)
                        if h >= 4 and h % 2 == 0:
                            pe.wait_ge(S("att_lo"), h // 2 - 1)
                        v, p0 = heads[h][5], (h % 2) * HD
                        for k in range(2):
                            last = nc.tensor.matmul(bank[4 + h // 2 % 2][p0:p0 + HD, 0:T], v(k), pT[:, h % 2, k, :],
                                                    start=(k == 0), stop=(k == 1), skip_group_check=True)
                        last.then_inc(S("att_values"), 1)

                    for h in range(3):
                        scores(h)
                    for h in range(NHD):
                        turn(h)
                        if h + 3 < NHD:
                            scores(h + 3)
                        values(h)

                @b.vector
                def _(dve):
                    def scaled(h):
                        kind, i = heads[h][0], heads[h][6]
                        dve.wait_ge(S("att_scores"), h + 1)
                        if h >= 3:
                            dve.wait_ge(S("att_exp"), h - 2)
                        s = s_sb[:, h % 3, :, :]
                        frm = view(score_bank[h % 3][:, :], (T, NT), (1, T))
                        sc = scale_of[kind]
                        if kind in ("na", "sw"):
                            add = bias[:, i, :, :] if kind == "na" else const("mask_sw", (T, NT), (1, T))
                            nc.vector.scalar_tensor_tensor(s, frm, sc, add, ALU.mult, ALU.add
                                                           ).then_inc(S("att_scaled"), 1)
                        else:
                            nc.vector.tensor_scalar(s, frm, sc, None, ALU.mult).then_inc(S("att_scaled"), 1)
                        dve.drain()
                        last = nc.vector.tensor_reduce(nmax[:, h, :], s, AX, ALU.max, negate=True)
                        if kind == "sw":
                            dve.drain()
                            last = nc.vector.tensor_scalar(nmax[:, h, :], nmax[:, h, :], nsink[:, i:i + 1], None,
                                                           ALU.min)
                        last.then_inc(S("att_max"), 1)

                    def normalised(h):
                        kind, i = heads[h][0], heads[h][6]
                        dve.wait_ge(S("att_exp"), h + 1)
                        if kind == "sw":
                            nc.vector.tensor_tensor(sums[:, h, :], sums[:, h, :], sinke[:, i, :], ALU.add)
                            dve.drain()
                        nc.vector.reciprocal(sums[:, h, :], sums[:, h, :]).then_inc(S("att_recip"), 1)
                        dve.drain()
                        nc.vector.tensor_scalar(p_sb[:, h % 3, 0, :], p_sb[:, h % 3, 0, :], sums[:, h, 0:1], None,
                                                ALU.mult).then_inc(S("att_probs"), 1)

                    def low_part(pair):
                        dve.wait_ge(S("att_hi"), pair + 1)
                        nc.vector.tensor_tensor(HT_LO[:, pair, :], bank[4 + pair % 2][:, 0:T], HT_HI[:, pair, :],
                                                ALU.subtract).then_inc(S("att_lo"), 1)

                    dve.wait_ge(S("sink_loaded"), 16)
                    nc.vector.tensor_scalar(nsink, sink, -1.0, None, ALU.mult)
                    for h in range(3):
                        scaled(h)
                    normalised(0)
                    for h in range(NHD):
                        if h + 1 < NHD:
                            normalised(h + 1)
                        if h + 3 < NHD:
                            scaled(h + 3)
                        if h >= 2 and h % 2 == 0:
                            low_part(h // 2 - 1)
                    low_part(NHD // 2 - 1)

                @b.gpsimd
                def _(pool):
                    for h in range(NHD):
                        pool.wait_ge(S("att_recip"), h + 1)
                        nc.gpsimd.tensor_scalar(p_sb[:, h % 3, 1, :], p_sb[:, h % 3, 1, :], sums[:, h, 1:2], None,
                                                ALU.mult).then_inc(S("att_probs_pool"), 1)

                @b.scalar
                def _(act):
                    def exps(h):
                        kind, i = heads[h][0], heads[h][6]
                        act.wait_ge(S("att_max"), h + 1)
                        if h >= 3:
                            act.wait_ge(S("att_turned"), h - 2)
                        if kind == "sw":
                            nc.scalar.activation(sinke[:, i, :], nmax[:, h, :], ACT.Exp, bias=sink[:, i:i + 1])
                        for t in range(NT):
                            last = nc.scalar.activation(p_sb[:, h % 3, t, :], s_sb[:, h % 3, t, :], ACT.Exp,
                                                        bias=nmax[:, h, t:t + 1], accum_out=sums[:, h, t:t + 1])
                        last.then_inc(S("att_exp"), 1)

                    def out_turned(h):
                        act.wait_ge(S("att_turned"), h + 1)
                        if h >= 2:
                            act.wait_ge(S("att_values"), h - 1)
                        nc.scalar.copy(pT[:, h % 2, :, :], view(bank[2 + h % 2][:, :], (T, 2), (1, T))
                                       ).then_inc(S("att_probsT"), 1)

                    def high_part(pair):
                        act.wait_ge(S("att_values"), 2 * pair + 2)
                        nc.scalar.copy(HT_HI[:, pair, :], bank[4 + pair % 2][:, 0:T]).then_inc(S("att_hi"), 1)

                    exps(0)
                    exps(1)
                    for h in range(NHD):
                        out_turned(h)
                        if h >= 2 and h % 2 == 0:
                            high_part(h // 2 - 1)
                        if h + 2 < NHD:
                            exps(h + 2)
                    high_part(NHD // 2 - 1)

            m = shaped(mixed_at, NT, D)
            linear("out1", w_out, RING_AT, UNIT_AT, out_chunks,
                   lambda kind, t, n0, w: m[:, t, n0:n0 + w], preloaded=PIECES)
            add_normed("mix_post", m, mix_post, "mix_post_loaded", shaped(qkT_at, NT, D))

            up_raw_at, down_raw_at = RING_AT, RING_AT + 2 * 2048
            g_at = RING_AT + 6144
            up_raw = [shaped(up_raw_at + s * 2048, 4, 512) for s in range(2)]
            down_raw = [shaped(down_raw_at + s * 1024, 2, 512) for s in range(2)]
            up_hi = [[parts(UNIT_AT + (4 * s + u) * 1024, 512) for u in range(4)] for s in range(2)]
            up_lo = [[parts(UNIT_AT + (4 * s + u) * 1024 + 512, 512) for u in range(4)] for s in range(2)]
            down_hi = [[parts(qkT_at + (2 * s + u) * 1024, 512) for u in range(2)] for s in range(2)]
            down_lo = [[parts(qkT_at + (2 * s + u) * 1024 + 512, 512) for u in range(2)] for s in range(2)]
            g_hi = [parts(g_at + s * 512, T) for s in range(2)]
            g_lo = [parts(g_at + s * 512 + T, T) for s in range(2)]
            us = [shaped(Z_AT + s * 512, 2, T) for s in range(2)]
            cc = [shaped(Z_AT + 1024 + s * 512, 2, T) for s in range(2)]
            ge = [arena(Z_AT + 2048 + s * T, T) for s in range(2)]
            conv = shaped(Z_AT + 2560, NF, 8)
            w_up = a["w_up_tiles"]
            w_down = a["w_down"]

            def load_up(sp, j, s):
                sp.dma_start(arena(up_raw_at + s * 2048, 2048), w_up[l, j, :, :]).then_inc(S(f"up_loaded{s}"), 16)

            def load_down(sp, j, s):
                sp.dma_start(arena(down_raw_at + s * 1024, D), w_down[l, bass.ds(j * P, P), :]
                             ).then_inc(S(f"down_loaded{s}"), 16)

            def ffn_early(sp):
                for s in range(2):
                    load_up(sp, s, s)
                    load_down(sp, s, s)
                sp.dma_start(arena(Z_AT + 2560, NF * 8), a["conv_params"][l, :, :]).then_inc(S("conv_loaded"), 16)

            norm_to_ht("ffn", l, 1, mixed_at, qkT_at, ffn_early)
            with nc.Block() as b:
                @b.sync
                def _(sp):
                    with sp.Fori(1, NF // 2) as it:
                        for s in range(2):
                            j = it * 2 + s
                            sp.wait_ge(S("up_lo"), it * 8 + 4 * (s - 1))
                            load_up(sp, j, s)
                            sp.wait_ge(S("down_lo"), it * 4 + 2 * (s - 1))
                            load_down(sp, j, s)

                @b.tensor
                def _(pe):
                    pe.sem_inc(S("up_used"), 2)
                    pe.sem_inc(S("down_used"), 2)
                    for y in range(4):
                        nc.tensor.matmul(bank[y][:, :], ZERO[:, 0:P], ZERO[:, :], start=True, stop=False,
                                         skip_group_check=True)

                    def up(s, j):
                        pe.wait_ge(S("ubank_free"), j)
                        for u in range(4):
                            pe.wait_ge(S("up_lo"), j * 4 + (u - 3))
                            side, half = u // 2, u % 2
                            for k in range(4):
                                c = slice(k * P, (k + 1) * P)
                                last = mm3(bank[4 + s][:, side * T:(side + 1) * T], up_hi[s][u][:, c],
                                           up_lo[s][u][:, c], HT_HI[:, 4 * half + k, :], HT_LO[:, 4 * half + k, :],
                                           u % 2 == 0 and k == 0, u % 2 == 1 and k == 3)
                        last.then_inc(S("up_used"), 1)

                    def down(s, j, stop=False):
                        pe.wait_ge(S("g_ready"), j)
                        for n in range(2):
                            pe.wait_ge(S("down_lo"), j * 2 + (n - 1))
                            for t in range(NT):
                                c = slice(t * P, (t + 1) * P)
                                last = mm3(bank[2 * t + n][:, :], g_hi[s][:, c], g_lo[s][:, c], down_hi[s][n],
                                           down_lo[s][n], False, stop)
                        last.then_inc(S("down_used"), 1)

                    up(0, 1)
                    with pe.Fori(0, NF // 2 - 1) as it:
                        up(1, it * 2 + 2)
                        down(0, it * 2 + 1)
                        up(0, it * 2 + 3)
                        down(1, it * 2 + 2)
                    up(1, NF)
                    down(0, NF - 1)
                    down(1, NF, stop=True)

                @b.scalar
                def _(act):
                    act.sem_inc(S("ubank_free"), 2)
                    act.wait_ge(S("conv_loaded"), 16)

                    def split_up(s, j, turn):
                        act.wait_ge(S(f"up_loaded{s}"), turn)
                        act.wait_ge(S("up_used"), j)
                        for u in range(4):
                            nc.scalar.copy(up_hi[s][u], up_raw[s][:, u, :]).then_inc(S("up_hi"), 1)

                    def split_down(s, j, turn):
                        act.wait_ge(S(f"down_loaded{s}"), turn)
                        act.wait_ge(S("down_used"), j)
                        for n in range(2):
                            nc.scalar.copy(down_hi[s][n], down_raw[s][:, n, :]).then_inc(S("down_hi"), 1)

                    def take_u(s, j, j0):
                        act.wait_ge(S("up_used"), j + 2)
                        act.wait_ge(S("us_free"), j)
                        nc.scalar.copy(us[s], view(bank[4 + s][:, :], (T, 2), (1, T)))
                        for side in range(2):
                            w1 = conv[:, j0, 4 * side + 1:4 * side + 2]
                            b1 = conv[:, j0, 4 * side + 3:4 * side + 4]
                            last = nc.scalar.activation(cc[s][:, side, :], bank[4 + s][:, side * T:(side + 1) * T],
                                                        ACT.Identity, bias=b1, scale=w1)
                        last.then_inc(S("ubank_free"), 1)

                    def gelu(s, j):
                        act.wait_ge(S("conv_ready"), j)
                        nc.scalar.activation(ge[s], cc[s][:, 0, :], ACT.Gelu_apprx_tanh).then_inc(S("gelu_ready"), 1)

                    split_up(0, 1, 16)
                    split_up(1, 2, 16)
                    split_down(0, 1, 16)
                    take_u(0, 1, 0)
                    split_up(0, 3, 32)
                    with act.Fori(0, NF // 2 - 2) as it:
                        for s in range(2):
                            gelu(s, it * 2 + (s + 1))
                            split_down(1 - s, it * 2 + (s + 2), it * 16 + 16 * (s + 1))
                            take_u(1 - s, it * 2 + (s + 2), it * 2 + (s + 1))
                            split_up(1 - s, it * 2 + (s + 4), it * 16 + 16 * (s + 2))
                    for j in range(NF - 4, NF):
                        s = j % 2
                        gelu(s, j + 1)
                        if j + 1 < NF:
                            split_down(1 - s, j + 2, 16 * ((j + 1) // 2 + 1))
                            take_u(1 - s, j + 2, j + 1)
                        if j + 3 < NF:
                            split_up(1 - s, j + 4, 16 * ((j + 3) // 2 + 1))
                    for t in range(NT):
                        act.wait_ge(S("down_used"), NF + 2)
                        nc.scalar.copy(m[:, t, 0:512], bank[2 * t][:, :])

                @b.vector
                def _(dve):
                    dve.sem_inc(S("us_free"), 2)
                    dve.wait_ge(S("conv_loaded"), 16)

                    def split_up(s, j):
                        for u in range(4):
                            dve.wait_ge(S("up_hi"), j * 4 + (u - 3))
                            nc.vector.tensor_tensor(up_lo[s][u], up_raw[s][:, u, :], up_hi[s][u], ALU.subtract
                                                    ).then_inc(S("up_lo"), 1)

                    def split_down(s, j):
                        for n in range(2):
                            dve.wait_ge(S("down_hi"), j * 2 + (n - 1))
                            nc.vector.tensor_tensor(down_lo[s][n], down_raw[s][:, n, :], down_hi[s][n],
                                                    ALU.subtract).then_inc(S("down_lo"), 1)

                    def convolve(s, j, j0):
                        dve.wait_ge(S("ubank_free"), j + 2)
                        for tap, to, frm in ((0, slice(1, T), slice(0, T - 1)), (2, slice(0, T - 1), slice(1, T))):
                            for side in range(2):
                                u, c = us[s][:, side, :], cc[s][:, side, :]
                                w = conv[:, j0, 4 * side + tap:4 * side + tap + 1]
                                last = nc.vector.scalar_tensor_tensor(c[:, to], u[:, frm], w, c[:, to],
                                                                      ALU.mult, ALU.add)
                            if tap == 0:
                                dve.drain()
                        last.then_inc(S("conv_ready"), 1)

                    def gated(s, j):
                        dve.wait_ge(S("gelu_ready"), j)
                        nc.vector.tensor_tensor(ge[s], ge[s], cc[s][:, 1, :], ALU.mult)
                        dve.drain()
                        dve.wait_ge(S("down_used"), j)
                        nc.vector.tensor_copy(g_hi[s], ge[s])
                        dve.drain()
                        nc.vector.tensor_tensor(g_lo[s], ge[s], g_hi[s], ALU.subtract).then_inc(S("g_ready"), 1)
                        dve.drain()
                        dve.sem_inc(S("us_free"), 1)

                    split_up(0, 1)
                    split_up(1, 2)
                    split_down(0, 1)
                    with dve.Fori(0, NF // 2 - 1) as it:
                        for s in range(2):
                            convolve(s, it * 2 + (s + 1), it * 2 + s)
                            split_up(s, it * 2 + (s + 3))
                            gated(s, it * 2 + (s + 1))
                            split_down(1 - s, it * 2 + (s + 2))
                    convolve(0, NF - 1, NF - 2)
                    gated(0, NF - 1)
                    split_down(1, NF)
                    convolve(1, NF, NF - 1)
                    gated(1, NF)
                    for t in range(NT):
                        dve.wait_ge(S("down_used"), NF + 2)
                        nc.vector.tensor_copy(m[:, t, 512:D], bank[2 * t + 1][:, :])
            add_normed("ffn_post", m, ffn_post, "ffn_post_loaded", shaped(qkT_at, NT, D))
            clear_all()

        def second_layer(l):
            at = 0

            def take(n):
                nonlocal at
                at += n
                assert at <= EXTRA_AT, at
                return at - n

            z = shaped(take(NT * Z2), NT, Z2)
            RING_AT = take(PIECES * PIECE_N)
            UNIT_AT = take(UNITS * UNIT_N)
            qkc_at = take(6 * T)
            qkc = shaped(qkc_at, 6, T)
            qkm = shaped(take(6 * T), 6, T)
            sb_hi = view(parts(take(6 * T), 6 * T), (T, 6), (1, T))
            sb_lo = view(parts(qkc_at, 6 * T), (T, 6), (1, T))
            sq_at = take(NT * D)
            ycat = shaped(take(NT * D), NT, D)
            xn_at = take(4096)
            sgm = shaped(xn_at + NT * D, 6, T)
            work_at = xn_at
            vaug = shaped(take(NT * NH6 * 65), NT, NH6, 65)
            sgw = shaped(take(SGG * P), SGG, P)
            uv = shaped(take(NT * 512), NT, 512)
            og = shaped(take(NT * 384), NT, 384)
            sbg = arena(take(768), 768)
            svg = arena(take(256), 256)
            conv = shaped(take(32), 6, 5)
            ifb = arena(take(2), 2)
            sgb = arena(take(4), 4)
            row_at = take(8 * T)

            def row(i):
                return ARENA[0:NH6, row_at + i * T:row_at + (i + 1) * T]

            w_in = a["w_in_2"][l].rearrange("(k p) n -> p k n", p=P)
            w_out = a["w_out_2"][l].rearrange("(k p) n -> p k n", p=P)
            in_chunks = [("rows", 0, 512, 0), ("rows", 512, 512, 512), ("rows", 1024, 128, 1024),
                         ("turned", 1152, 384, 0), ("turned", 1536, 384, 3),
                         ("rows", 1920, 512, 1152), ("rows", 2432, 512, 1664), ("rows", 2944, 268, 2176)]
            out_chunks = [("rows", n, 512, n) for n in range(0, D, 512)]

            def early_loads(sp):
                for q in range(PIECES):
                    linear_load(sp, "in2", w_in, RING_AT, in_chunks, q)
                sp.dma_start(ARENA[:, EXTRA_AT:EXTRA_AT + NCONST2], a["consts2"][:, :]).then_inc(S("mix2_params"), 16)
                one = lambda name, n: a[name][bass.ds(l, 1), :].broadcast_to([P, n])
                sp.dma_start(sbg, one("sb_gain", 768)).then_inc(S("mix2_params"), 16)
                sp.dma_start(svg, one("sg_vn_g_2", 256)).then_inc(S("mix2_params"), 16)
                sp.dma_start(conv, a["ml_conv"][l]).then_inc(S("mix2_params"), 16)
                sp.dma_start(ifb[0:NH6, :], a["ml_if_b"][l, :, :]).then_inc(S("mix2_params"), 16)
                sp.dma_start(sgb, a["sg_b_t"][l, :, :]).then_inc(S("mix2_params"), 16)
                sp.dma_start(sgw, a["sg_w_t"][l]).then_inc(S("mix2_params"), 16)
            N_PARAMS = 7 * 16

            def pick(kind, t, n0, w):
                return z[:, t, n0:n0 + w] if kind == "rows" else qkc[:, t, :]

            norm_to_ht("pre", l, 2, xn_at, sq_at, early_loads)
            linear("in2", w_in, RING_AT, UNIT_AT, in_chunks, pick, preloaded=PIECES)

            sbqk = view(z[:, 0:1, 0:1], (Z2, NT), (HD, 12), (1, HD))
            sq12 = view(arena(sq_at, 1), (768, NT), (HD, 12), (1, HD))
            sqf = view(arena(sq_at, 1), (768, NT), (1, 768))
            ss12 = view(STAT[:, 0:24], (12, NT), (1, 12))
            ss4 = view(STAT[:, 32:40], (4, NT), (1, 4))
            vsq = view(arena(xn_at, 1), (256, NT), (HD, 4), (1, HD))
            uvv = view(uv[:, 0:1, 256:257], (512, NT), (HD, 4), (1, HD))
            acol = view(STAT[:, 64:76], (6, NT), (1, 6))
            ecol = view(STAT[:, 80:92], (6, NT), (1, 6))
            with nc.Block() as b:
                @b.sync
                def _(sp):
                    for q in range(PIECES):
                        linear_load(sp, "out2", w_out, RING_AT, out_chunks, q)

                @b.scalar
                def _(act):
                    nc.scalar.activation(uv, z[:, :, SG_UV:SG_UV + 512], ACT.Gelu_apprx_tanh
                                         ).then_inc(S("uv_gelu"), 1)
                    nc.scalar.activation(og, z[:, :, ML_O:ML_O + 384], ACT.Sigmoid).then_inc(S("og_ready"), 1)
                    act.wait_ge(S("f_ready"), 1)
                    nc.scalar.activation(row(2), row(1), ACT.Abs)
                    act.drain()
                    nc.scalar.activation(row(2), row(2), ACT.Exp, scale=-1.0)
                    act.drain()
                    nc.scalar.activation(row(2), row(2), ACT.Ln, bias=1.0).then_inc(S("f_log"), 1)
                    act.wait_ge(S("ml_conv_ready"), 1)
                    nc.scalar.activation(sgm, qkm, ACT.Sigmoid).then_inc(S("ml_sigmoid"), 1)
                    act.wait_ge(S("m_ready"), 1)
                    nc.scalar.activation(row(6), row(6), ACT.Exp, scale=-1.0).then_inc(S("em_ready"), 1)
                    for g in range(6):
                        act.wait_ge(S("sb_turned"), g + 1)
                        nc.scalar.copy(sb_hi[:, g, :], bank[g % 4][:, 0:T]).then_inc(S("sb_hi"), 1)
                    act.wait_ge(S("ml_silu"), 1)
                    nc.scalar.copy(HT_HI[:, 0:6, :], qkm)

                @b.gpsimd
                def _(pool):
                    pool.wait_ge(S("mix2_params"), N_PARAMS)
                    nc.gpsimd.tensor_tensor(sgw, sgw, const("tril_t", (0, SGG), (1, P)), ALU.mult)
                    pool.wait_ge(S("uv_gelu"), 1)
                    nc.gpsimd.tensor_tensor(vsq, uvv, uvv, ALU.mult).then_inc(S("sgv_squares"), 1)
                    pool.wait_ge(S("sb_squares"), 1)
                    pool_rstd(pool, STAT[:, 0:24], 1.0 / HD, 24).then_inc(S("sb_rstd"), 1)
                    nc.gpsimd.memset(vaug, 1.0)
                    pool.drain()
                    nc.gpsimd.tensor_copy(vaug[:, :, :, 0:HD],
                                          view(z[:, 0:1, ML_V:ML_V + 1], (Z2, NT), (HD, NH6), (1, HD)))
                    pool.wait_ge(S("sgv_sums"), 1)
                    pool_rstd(pool, STAT[:, 32:40], 1.0 / HD, 8)
                    pool.drain()
                    nc.gpsimd.tensor_tensor(uvv, uvv, view(ss4, (4, NT), (1, 4), (0, HD)), ALU.mult)
                    pool.drain()
                    uvf = view(uv[:, 0:1, 256:257], (512, NT), (1, 256))
                    nc.gpsimd.tensor_tensor(uvf, uvf, view(svg, (0, NT), (1, 256)), ALU.mult)

                @b.vector
                def _(dve):
                    tt = nc.vector.tensor_tensor
                    tt(sq12, sbqk, sbqk, ALU.mult)
                    dve.drain()
                    nc.vector.reduce_sum(ss12, sq12, AX).then_inc(S("sb_squares"), 1)
                    dve.wait_ge(S("if_turned"), 1)
                    dve.wait_ge(S("mix2_params"), N_PARAMS)
                    nc.vector.tensor_scalar(row(0), bank[7][0:NH6, 0:T], ifb[0:NH6, 0:1], None, ALU.add)
                    nc.vector.tensor_scalar(row(1), bank[7][0:NH6, T:2 * T], ifb[0:NH6, 1:2], None, ALU.add
                                            ).then_inc(S("f_ready"), 1)
                    for f in range(6):
                        nc.vector.tensor_scalar(qkm[:, f, :], qkc[:, f, :], conv[:, f, 3:4], conv[:, f, 4:5],
                                                ALU.mult, ALU.add)
                    for j in range(3):
                        dve.drain()
                        sh = 3 - j
                        for f in range(6):
                            last = nc.vector.scalar_tensor_tensor(
                                qkm[:, f, sh:T], qkc[:, f, 0:T - sh], conv[:, f, j:j + 1], qkm[:, f, sh:T],
                                ALU.mult, ALU.add)
                    last.then_inc(S("ml_conv_ready"), 1)
                    dve.wait_ge(S("sgv_squares"), 1)
                    nc.vector.reduce_sum(ss4, vsq, AX).then_inc(S("sgv_sums"), 1)
                    dve.wait_ge(S("sb_rstd"), 1)
                    tt(sq12, sbqk, view(ss12, (12, NT), (1, 12), (0, HD)), ALU.mult)
                    dve.drain()
                    tt(sqf, sqf, view(sbg, (0, NT), (1, 768)), ALU.mult).then_inc(S("sb_ready"), 1)
                    dve.wait_ge(S("f_log"), 1)
                    nc.vector.scalar_tensor_tensor(row(3), row(1), 0.0, row(2), ALU.min, ALU.subtract)
                    nc.vector.memset(row(7), 1.0)
                    dve.drain()
                    nc.vector.tensor_tensor_scan(row(4), row(7), row(3), 0.0, ALU.mult, ALU.add)
                    dve.drain()
                    tt(row(0), row(0), row(4), ALU.subtract)
                    nc.vector.memset(row(7), 0.0)
                    dve.drain()
                    nc.vector.tensor_tensor_scan(row(5), row(7), row(0), 0.0, ALU.max, ALU.max)
                    dve.drain()
                    tt(row(6), row(4), row(5), ALU.add).then_inc(S("m_ready"), 1)
                    dve.wait_ge(S("ml_sigmoid"), 1)
                    tt(qkm, qkm, sgm, ALU.mult).then_inc(S("ml_silu"), 1)
                    for g in range(6):
                        dve.wait_ge(S("sb_hi"), g + 1)
                        tt(sb_lo[:, g, :], bank[g % 4][:, 0:T], sb_hi[:, g, :], ALU.subtract).then_inc(S("sb_lo"), 1)
                    dve.wait_ge(S("cols_turned"), 1)
                    nc.vector.tensor_copy(acol, view(bank[6][:, 0:1], (6, NT), (1, 6)))
                    nc.vector.tensor_copy(ecol, view(bank[6][:, 16:17], (6, NT), (1, 6)))

                @b.tensor
                def _(pe):
                    for side in range(2):
                        for t in range(NT):
                            last = nc.tensor.transpose(bank[7][0:NH6, side * T + t * P:side * T + (t + 1) * P],
                                                       z[:, t, ML_IF + side * NH6:ML_IF + (side + 1) * NH6], ident)
                    last.then_inc(S("if_turned"), 1)
                    pe.wait_ge(S("sb_ready"), 1)
                    for g in range(6):
                        if g >= 4:
                            pe.wait_ge(S("sb_lo"), g - 3)
                        for t in range(NT):
                            last = nc.tensor.transpose(bank[g % 4][:, t * P:(t + 1) * P],
                                                       sqf[:, t, g * P:(g + 1) * P], ident)
                        last.then_inc(S("sb_turned"), 1)
                    pe.wait_ge(S("em_ready"), 1)
                    id6 = ident[0:NH6, 0:NH6]
                    for t in range(NT):
                        nc.tensor.transpose(bank[6][:, t * 6:t * 6 + 6], row(0)[:, t * P:(t + 1) * P], id6)
                    for t in range(NT):
                        last = nc.tensor.transpose(bank[6][:, 16 + t * 6:22 + t * 6],
                                                   row(6)[:, t * P:(t + 1) * P], id6)
                    last.then_inc(S("cols_turned"), 1)

            zs = [shaped(UNIT_AT + h * 512, 2, T) for h in range(NH6)]
            lg = [shaped(UNIT_AT + (NH6 + h) * 512, 2, T) for h in range(NH6)]
            soft = [shaped(UNIT_AT + (2 * NH6 + i) * 512, 2, T) for i in range(4)]
            sb_wt = [shaped(work_at + i * 512, 2, T) for i in range(2)]
            ml_arg = [shaped(work_at + 1024 + i * 512, 2, T) for i in range(2)]
            ml_wt = [shaped(work_at + 2048 + i * 512, 2, T) for i in range(2)]
            ml_p = [shaped(work_at + 3072 + i * 512, 2, T) for i in range(2)]
            ml_raw = shaped(sq_at, NT, NH6, 65)
            two = lambda bk: view(bk[:, :], (T, 2), (1, T))
            value_bank = [bank[4], bank[7]]
            with nc.Block() as b:
                @b.tensor
                def _(pe):
                    def scores(bk, q_hi, q_lo, k_hi, k_lo):
                        for k in range(2):
                            c = slice(k * P, (k + 1) * P)
                            last = mm3(bk[:, k * T:(k + 1) * T], k_hi[:, c], k_lo[:, c], q_hi, q_lo, True, True)
                        return last

                    def sb_scores(h):
                        if h >= 2:
                            pe.wait_ge(S("sb_scaled"), h - 1)
                        rows = slice((h % 2) * HD, (h % 2 + 1) * HD)
                        scores(bank[h % 2], sb_hi[rows, h // 2, :], sb_lo[rows, h // 2, :],
                               sb_hi[rows, 3 + h // 2, :], sb_lo[rows, 3 + h // 2, :]).then_inc(S("sb_scores"), 1)

                    def ml_scores(h):
                        if h < 2:
                            pe.wait_ge(S("sb_scaled"), NH6 - 1 + h)
                        else:
                            pe.wait_ge(S("ml_arg"), h - 1)
                            pe.wait_ge(S("ml_probs"), h - 1)
                        nc.tensor.matmul(bank[5 + h % 2][:, 0:T], const("pick", (1, P), parts=NH6, off=h * P),
                                         row(5), start=True, stop=True).then_inc(S("ml_m"), 1)
                        rows = slice((h % 2) * HD, (h % 2 + 1) * HD)
                        scores(bank[h % 2], HT_HI[rows, h // 2, :], HT_LO[rows, h // 2, :],
                               HT_HI[rows, 3 + h // 2, :], HT_LO[rows, 3 + h // 2, :]).then_inc(S("ml_scores"), 1)

                    def suffix_sums(h):
                        pe.wait_ge(S("sb_soft"), h + 1)
                        if h >= 2:
                            pe.wait_ge(S("sb_arg"), h - 1)
                        sfx, sp_ = bank[2 + h % 2], soft[h % 4]
                        nc.tensor.matmul(sfx[:, 0:T], const("suffix"), sp_[:, 0, :], start=True, stop=False)
                        nc.tensor.matmul(sfx[:, 0:T], const("ones"), sp_[:, 1, :], start=False, stop=True)
                        nc.tensor.matmul(sfx[:, T:2 * T], const("suffix"), sp_[:, 1, :], start=True, stop=True
                                         ).then_inc(S("sb_suffix"), 1)

                    def values(bk, w, v, n):
                        for t in range(NT):
                            for k in range(t + 1):
                                last = nc.tensor.matmul(bk[:, t * n:(t + 1) * n], w[:, k, t * P:(t + 1) * P], v(k),
                                                        start=(k == 0), stop=(k == t))
                        return last

                    for h in range(NH6):
                        sb_scores(h)
                    pe.wait_ge(S("ml_parts"), 1)
                    ml_scores(0)
                    ml_scores(1)
                    for h in range(NH6):
                        suffix_sums(h)
                        pe.wait_ge(S("ml_probs"), h + 1)
                        if h >= 1:
                            pe.wait_ge(S("ml_out"), h)
                        values(value_bank[0], ml_p[h % 2], lambda k: vaug[:, k, h, :], 65).then_inc(S("ml_values"), 1)
                        if h + 2 < NH6:
                            ml_scores(h + 2)
                        pe.wait_ge(S("sb_weight"), h + 1)
                        if h >= 1:
                            pe.wait_ge(S("sb_out"), h)
                        values(value_bank[1], sb_wt[h % 2], lambda k: z[:, k, SB_V + h * HD:SB_V + (h + 1) * HD], HD
                               ).then_inc(S("sb_values"), 1)
                    pe.wait_ge(S("ml_arg"), NH6)
                    for c in range(NT):
                        for g in range(SGG):
                            last = nc.tensor.matmul(bank[6][:, (c * SGG + g) * HD:(c * SGG + g + 1) * HD],
                                                    sgw[:, g, :], uv[:, c, 256 + g * HD:256 + (g + 1) * HD],
                                                    start=True, stop=True)
                    last.then_inc(S("sg_gate"), 1)

                @b.vector
                def _(dve):
                    tt, stt = nc.vector.tensor_tensor, nc.vector.scalar_tensor_tensor

                    def arg(h):
                        dve.wait_ge(S("ml_m"), h + 1)
                        if h >= 2:
                            dve.wait_ge(S("ml_weight"), h - 1)
                        for k in range(2):
                            last = stt(ml_arg[h % 2][:, k, :], bank[5 + h % 2][:, 0:T], acol[:, k, h:h + 1],
                                       const("causal_big", (T, 2), (1, T))[:, k, :], ALU.subtract, ALU.add)
                        last.then_inc(S("ml_arg"), 1)

                    def softplus(h):
                        dve.wait_ge(S("sb_log"), h + 1)
                        stt(lg[h], zs[h], 0.0, lg[h], ALU.max, ALU.add).then_inc(S("sb_softplus"), 1)

                    def sb_out(h):
                        dve.wait_ge(S("sb_values"), h + 1)
                        nc.vector.tensor_copy(ycat[:, :, h * HD:(h + 1) * HD],
                                              view(value_bank[1][:, 0:1], (HD, NT), (1, HD))).then_inc(S("sb_out"), 1)

                    for h in range(NH6):
                        dve.wait_ge(S("sb_scores"), h + 1)
                        nc.vector.tensor_scalar(zs[h], two(bank[h % 2]), HD ** -0.5, None, ALU.mult
                                                ).then_inc(S("sb_scaled"), 1)
                    arg(0)
                    arg(1)
                    softplus(0)
                    for h in range(NH6):
                        if h + 1 < NH6:
                            softplus(h + 1)
                        dve.wait_ge(S("ml_weight"), h + 1)
                        dve.wait_ge(S("ml_scores"), h + 1)
                        if h >= 2:
                            dve.wait_ge(S("ml_values"), h - 1)
                        stt(ml_p[h % 2], two(bank[h % 2]), HD ** -0.5, ml_wt[h % 2], ALU.mult, ALU.mult
                            ).then_inc(S("ml_probs"), 1)
                        dve.wait_ge(S("sb_suffix"), h + 1)
                        dve.wait_ge(S("sb_masked"), h + 1)
                        tt(lg[h], two(bank[2 + h % 2]), zs[h], ALU.subtract).then_inc(S("sb_arg"), 1)
                        dve.wait_ge(S("ml_values"), h + 1)
                        nc.vector.tensor_copy(ml_raw[:, :, h, :], view(value_bank[0][:, 0:1], (65, NT), (1, 65))
                                              ).then_inc(S("ml_out"), 1)
                        if h + 2 < NH6:
                            arg(h + 2)
                        if h >= 1:
                            sb_out(h - 1)
                    den = view(STAT[:, 96:108], (6, NT), (1, 6))
                    sums = ml_raw[:, :, :, 64]
                    dve.drain()
                    nc.vector.tensor_scalar(den, sums, -1.0, None, ALU.mult)
                    dve.drain()
                    tt(den, den, sums, ALU.max)
                    dve.drain()
                    tt(den, den, ecol, ALU.max)
                    dve.drain()
                    nc.vector.reciprocal(den, den)
                    dve.drain()
                    tt(view(ycat[:, 0:1, NH6 * HD:NH6 * HD + 1], (D, NT), (HD, NH6), (1, HD)), ml_raw[:, :, :, 0:HD],
                       view(STAT[:, 96:108], (6, NT), (1, 6), (0, HD)), ALU.mult)
                    sb_out(NH6 - 1)
                    dve.wait_ge(S("sg_gate"), 1)
                    for g in range(SGG):
                        o = (2 * NH6 + g) * HD
                        stt(ycat[:, :, o:o + HD], view(bank[6][:, g * HD:g * HD + 1], (SGG * HD, NT), (1, HD)),
                            sgb[:, g:g + 1], uv[:, :, g * HD:(g + 1) * HD], ALU.add, ALU.mult)

                @b.gpsimd
                def _(pool):
                    nc.gpsimd.tensor_tensor(HT_LO[:, 0:6, :], qkm, HT_HI[:, 0:6, :], ALU.subtract
                                            ).then_inc(S("ml_parts"), 1)
                    for h in range(NH6):
                        pool.wait_ge(S("sb_softplus"), h + 1)
                        if h >= 4:
                            pool.wait_ge(S("sb_suffix"), h - 3)
                        nc.gpsimd.tensor_tensor(soft[h % 4], lg[h], const("strict01", (T, 2), (1, T)), ALU.mult
                                                ).then_inc(S("sb_soft"), 1)
                        nc.gpsimd.tensor_tensor(zs[h], zs[h], const("strict_big", (T, 2), (1, T)), ALU.subtract
                                                ).then_inc(S("sb_masked"), 1)

                @b.scalar
                def _(act):
                    def ml_weight(h):
                        act.wait_ge(S("ml_arg"), h + 1)
                        if h >= 2:
                            act.wait_ge(S("ml_probs"), h - 1)
                        nc.scalar.activation(ml_wt[h % 2], ml_arg[h % 2], ACT.Exp, scale=-1.0
                                             ).then_inc(S("ml_weight"), 1)

                    for h in range(NH6):
                        act.wait_ge(S("sb_scaled"), h + 1)
                        nc.scalar.activation(lg[h], zs[h], ACT.Abs)
                        act.drain()
                        nc.scalar.activation(lg[h], lg[h], ACT.Exp, scale=-1.0)
                    ml_weight(0)
                    ml_weight(1)
                    act.drain()
                    for h in range(NH6):
                        nc.scalar.activation(lg[h], lg[h], ACT.Ln, bias=1.0).then_inc(S("sb_log"), 1)
                    for h in range(NH6):
                        act.wait_ge(S("sb_arg"), h + 1)
                        if h >= 2:
                            act.wait_ge(S("sb_values"), h - 1)
                        nc.scalar.activation(sb_wt[h % 2], lg[h], ACT.Exp, scale=-1.0).then_inc(S("sb_weight"), 1)
                        if h + 2 < NH6:
                            ml_weight(h + 2)

            ss16 = STAT[:, 128:160]
            sq16 = shaped(sq_at, NT, D)
            with nc.Block() as b:
                def gain(k):
                    return GAINS[:, 4, l, k:k + 1]

                @b.scalar
                def _(act):
                    for t in range(NT):
                        nc.scalar.activation(sq16[:, t, :], ycat[:, t, :], ACT.Square).then_inc(S("y_squares"), 1)
                    for k in range(KD):
                        act.wait_ge(S("y_turned"), k + 1)
                        nc.scalar.mul(HT_HI[:, k, :], bank[k][:, 0:T], gain(k)).then_inc(S("y_hi"), 1)

                @b.vector
                def _(dve):
                    tt = nc.vector.tensor_tensor
                    for t in range(NT):
                        dve.wait_ge(S("y_squares"), t + 1)
                        nc.vector.reduce_sum(ss16[:, 16 * t:16 * t + 16], view(sq16[:, t, :], (HD, 16), (1, HD)), AX
                                             ).then_inc(S("y_sums"), 1)
                    for t in range(NT):
                        dve.wait_ge(S("y_rstd"), t + 1)
                        y16 = view(ycat[:, t, :], (HD, 16), (1, HD))
                        tt(y16, y16, view(ss16[:, 16 * t:16 * t + 16], (1, 16), (0, HD)), ALU.mult)
                        dve.drain()
                        ym = ycat[:, t, NH6 * HD:2 * NH6 * HD]
                        tt(ym, ym, og[:, t, :], ALU.mult).then_inc(S("y_xn"), 1)
                    for k in range(KD):
                        dve.wait_ge(S("y_hi"), k + 1)
                        nc.vector.scalar_tensor_tensor(HT_LO[:, k, :], bank[k][:, 0:T], gain(k), HT_HI[:, k, :],
                                                       ALU.mult, ALU.subtract)

                @b.gpsimd
                def _(pool):
                    for t in range(NT):
                        pool.wait_ge(S("y_sums"), t + 1)
                        pool_rstd(pool, ss16[:, 16 * t:16 * t + 16], 1.0 / HD, 16).then_inc(S("y_rstd"), 1)

                @b.tensor
                def _(pe):
                    turn_all(pe, "y", ycat)

            m = shaped(xn_at, NT, D)

            def add_x(dve):
                dve.wait_ge(S("out2_taken_act"), 2)
                dve.drain()
                nc.vector.tensor_tensor(X[:, :, :], X[:, :, :], m[:, :, :], ALU.add)
            linear("out2", w_out, RING_AT, UNIT_AT, out_chunks,
                   lambda kind, t, n0, w: m[:, t, n0:n0 + w], preloaded=PIECES, extra_dve=add_x)
            peer(l)
            clear_all()

        def peer(l):
            G = shaped(0, T, P)
            GEND = T * P
            U_RAW, V_RAW = GEND, GEND + 2048
            U_PART, V_PART = GEND + 4096, GEND + 6144
            W_PART = GEND + 8192
            GA_AT = GEND + 9216
            SEL_AT = U_PART
            HOT_AT = SEL_AT + 3 * T
            sel = shaped(SEL_AT, 3, T)
            HOTS = 4
            hot = shaped(HOT_AT, HOTS, 2, 4, P)
            bare = shaped(HOT_AT + HOTS * 1024, HOTS, 2, P)
            its_numbers = view(STAT[:, 160:161], (4, HOTS), (1, 4))
            AHEAD_A_TURN = 3
            AHEAD = AHEAD_A_TURN * PH // 2
            ahead_at = HOT_AT + HOTS * 1280
            ahead = shaped(ahead_at, AHEAD, T)
            u_hi = [parts(U_PART + i * 1024, 512) for i in range(2)]
            u_lo = [parts(U_PART + i * 1024 + 512, 512) for i in range(2)]
            ahead_raw = [shaped(U_RAW + c * 1024, 2, 512) for c in range(AHEAD_A_TURN)]
            at = 0

            def take(n):
                nonlocal at
                at += n
                assert at <= GEND, at
                return at - n

            HT = shaped(take(KD * T), KD, T)
            q_ring = [shaped(take(2 * T), 2, T) for _ in range(2)]
            wq_at = take(4 * 1024)
            keys_at = take(NSET * NKEY)
            keysT = shaped(keys_at, PH, 2, NKEY)
            sc = [shaped(take(4 * NKEY), 2, NT, NKEY) for _ in range(2)]
            rest = shaped(take(4 * NKEY), 2, NT, NKEY)
            sv = shaped(take(64), 2, NT, TOPK)
            siu = shaped(take(64), 2, NT, TOPK).bitcast(U32)
            si = [shaped(take(64), 2, NT, TOPK) for _ in range(2)]
            best = shaped(take(2 * T), NT, T)
            rest2 = shaped(take(2 * T), NT, T)
            bv = shaped(take(32), NT, TOPK)
            bpu = shaped(take(32), NT, TOPK).bitcast(U32)
            ku = shaped(take(64), 2, NT, TOPK).bitcast(U32)
            kf = [shaped(take(64), 2, NT, TOPK) for _ in range(2)]
            eq = [shaped(take(1024), 2, NT * TOPK, TOPK) for _ in range(2)]
            idx = shaped(take(2 * NT * (PH + 1) * TOPK), 2, NT, PH + 1, TOPK)
            gate = shaped(take(T), NT, PH, TOPK)
            pad = arena(take(16), 1)
            xn_at, junk_at = take(NT * D), take(NT * D)

            def load_wq(sp, c, s):
                sp.dma_start(arena(wq_at + s * 1024, 1024), a["wq_tiles"][l, c, :, :]).then_inc(S(f"wq_loaded{s}"), 16)

            def load_ahead(sp, j, c):
                sp.dma_start(arena(U_RAW + c * 1024, 1024), a["u_tiles"][l, j, :, :]
                             ).then_inc(S(f"ahead_loaded{c}"), 16)

            def router_loads(sp):
                for s in range(4):
                    load_wq(sp, s, s)
                sp.dma_start(arena(keys_at, NSET * NKEY), a["keys_t"][l, :, :]).then_inc(S("keys_loaded"), 16)
                for c in range(AHEAD_A_TURN):
                    load_ahead(sp, c, c)

            norm_to_ht("peer", l, 3, xn_at, junk_at, router_loads, raw=HT)

            with nc.Block() as b:
                @b.sync
                def _(sp):
                    with sp.Fori(1, PH // 2) as it:
                        for s in range(4):
                            sp.wait_ge(S("q_filled"), it * 2 + (s // 2 - 1))
                            load_wq(sp, it * 4 + s, s)
                            if s >= 1:
                                c = s - 1
                                sp.wait_ge(S("ahead_lo"), it * (2 * AHEAD_A_TURN) + 2 * (c - AHEAD_A_TURN + 1))
                                load_ahead(sp, it * AHEAD_A_TURN + c, c)

                @b.tensor
                def _(pe):
                    pe.wait_ge(S("keys_loaded"), 16)

                    def queries(s, turn, h):
                        pe.wait_ge(S("q_taken"), h)
                        for side in range(2):
                            w = shaped(wq_at + (2 * s + side) * 1024, KD, P)
                            pe.wait_ge(S(f"wq_loaded{2 * s + side}"), turn)
                            for k in range(KD):
                                last = nc.tensor.matmul(bank[s][:, side * T:(side + 1) * T], w[:, k, :], HT[:, k, :],
                                                        start=(k == 0), stop=(k == KD - 1), skip_group_check=True)
                        last.then_inc(S("q_filled"), 1)

                    def score(s, h, h0):
                        pe.wait_ge(S("q_taken"), h + 2)
                        pe.wait_ge(S("sc_taken"), h)
                        for side in range(2):
                            for t in range(NT):
                                last = nc.tensor.matmul(bank[2 + s][:, (2 * side + t) * P:(2 * side + t + 1) * P],
                                                        q_ring[s][:, side, t * P:(t + 1) * P],
                                                        keysT[:, h0, side, :], start=True, stop=True,
                                                        skip_group_check=True)
                        last.then_inc(S("sc_filled"), 1)

                    def ahead_acts(c, n):
                        pe.wait_ge(S("ahead_taken"), n)
                        for i in range(2):
                            pe.wait_ge(S("ahead_lo"), n * 2 + (i - 1))
                            for k in range(4):
                                cols = slice(k * P, (k + 1) * P)
                                last = mm3(bank[4 + c][:, 0:T], u_hi[i][:, cols], u_lo[i][:, cols],
                                           HT_HI[:, 4 * i + k, :], HT_LO[:, 4 * i + k, :],
                                           i == 0 and k == 0, i == 1 and k == 3)
                            last.then_inc(S("ahead_used"), 1)

                    A = AHEAD_A_TURN
                    pe.sem_inc(S("ahead_used"), 2)
                    queries(0, 16, 1)
                    with pe.Fori(0, PH // 2 - 1) as it:
                        queries(1, it * 16 + 16, it * 2 + 2)
                        score(0, it * 2 + 1, it * 2)
                        ahead_acts(0, it * A + 1)
                        queries(0, it * 16 + 32, it * 2 + 3)
                        score(1, it * 2 + 2, it * 2 + 1)
                        ahead_acts(1, it * A + 2)
                        ahead_acts(2, it * A + 3)
                    queries(1, 8 * PH, PH)
                    score(0, PH - 1, PH - 2)
                    ahead_acts(0, AHEAD - 2)
                    score(1, PH, PH - 1)
                    ahead_acts(1, AHEAD - 1)
                    ahead_acts(2, AHEAD)

                @b.scalar
                def _(act):
                    act.sem_inc(S("q_taken"), 2)
                    act.sem_inc(S("sc_taken"), 2)
                    act.sem_inc(S("ahead_taken"), AHEAD_A_TURN)

                    def take_queries(s, n):
                        act.wait_ge(S("q_filled"), n)
                        nc.scalar.copy(q_ring[s], view(bank[s][:, :], (T, 2), (1, T))).then_inc(S("q_taken"), 1)

                    def take_scores(s, n):
                        act.wait_ge(S("sc_filled"), n)
                        act.wait_ge(S("sc_free"), n)
                        nc.scalar.copy(view(sc[s], (1, 4 * NKEY)), bank[2 + s][:, :]).then_inc(S("sc_taken"), 1)

                    def ahead_high(c, n, turn):
                        act.wait_ge(S(f"ahead_loaded{c}"), turn)
                        for i in range(2):
                            act.wait_ge(S("ahead_used"), n * 2 + (i - 1))
                            nc.scalar.copy(u_hi[i], ahead_raw[c][:, i, :]).then_inc(S("ahead_hi"), 1)

                    def ahead_gelu(c, n, n0):
                        act.wait_ge(S("ahead_used"), n * 2 + 2)
                        nc.scalar.activation(ahead[:, n0, :], bank[4 + c][:, 0:T], ACT.Gelu_apprx_tanh
                                             ).then_inc(S("ahead_taken"), 1)

                    with act.Fori(0, PH // 2) as it:
                        tile = it * AHEAD_A_TURN
                        take_queries(0, it * 2 + 1)
                        ahead_high(0, tile + 1, it * 16 + 16)
                        take_scores(0, it * 2 + 1)
                        take_queries(1, it * 2 + 2)
                        ahead_gelu(0, tile + 1, tile)
                        ahead_high(1, tile + 2, it * 16 + 16)
                        take_scores(1, it * 2 + 2)
                        ahead_gelu(1, tile + 2, tile + 1)
                        ahead_high(2, tile + 3, it * 16 + 16)
                        ahead_gelu(2, tile + 3, tile + 2)
                    act.wait_ge(S("gate_arg"), 1)
                    nc.scalar.activation(view(gate, (1, NT * P)), view(gate, (1, NT * P)), ACT.Exp
                                         ).then_inc(S("gate_exp"), 1)

                @b.vector
                def _(dve):
                    v = nc.vector
                    four = [(side, t) for side in range(2) for t in range(NT)]
                    dve.sem_inc(S("sc_free"), 2)

                    def sum_up(s, done, h1):
                        dve.wait_ge(S("si_free"), done)
                        for a_ in range(2):
                            v.reduce_sum(view(idx[:, a_, :, h1, :], ((PH + 1) * TOPK, NT), (1, TOPK)),
                                         view(eq[s][:, a_, :, :], (256, NT), (16, 16), (1, 16)), AX)

                    v.memset(view(eq[1], (1, 1024)), 0.0)
                    with dve.Fori(0, PH // 2) as it:
                        for s in range(2):
                            h = it * 2 + s
                            dve.wait_ge(S("sc_taken"), it * 2 + (s + 3))
                            v.memset(pad, 0.0)
                            for a_, t in four:
                                v.max(sv[:, a_, t, 0:8], sc[s][:, a_, t, :])
                            dve.drain()
                            for a_, t in four:
                                v.max_index(siu[:, a_, t, 0:8], sv[:, a_, t, 0:8], sc[s][:, a_, t, :])
                                v.match_replace(rest[:, a_, t, :], sv[:, a_, t, 0:8], sc[s][:, a_, t, :], -3e38)
                            dve.drain()
                            dve.sem_inc(S("sc_free"), 1)
                            for a_, t in four:
                                v.max(sv[:, a_, t, 8:16], rest[:, a_, t, :])
                            dve.drain()
                            for a_, t in four:
                                v.max_index(siu[:, a_, t, 8:16], sv[:, a_, t, 8:16], rest[:, a_, t, :])
                            for t in range(NT):
                                v.tensor_tensor(view(best[:, t, 0:1], (16, 16), (1, 16)),
                                                view(sv[:, 0, t, 0:1], (1, 16), (0, 16)),
                                                view(sv[:, 1, t, 0:1], (0, 16), (1, 16)), ALU.add)
                            dve.drain()
                            dve.wait_ge(S("si_free"), it * 2 + (s + 1))
                            v.tensor_copy(view(si[s], (1, 64)), view(siu, (1, 64)))
                            for t in range(NT):
                                v.max(bv[:, t, 0:8], best[:, t, :])
                            dve.drain()
                            for t in range(NT):
                                v.max_index(bpu[:, t, 0:8], bv[:, t, 0:8], best[:, t, :])
                                v.match_replace(rest2[:, t, :], bv[:, t, 0:8], best[:, t, :], -3e38)
                            dve.drain()
                            for t in range(NT):
                                v.max(bv[:, t, 8:16], rest2[:, t, :])
                            dve.drain()
                            for t in range(NT):
                                v.max_index(bpu[:, t, 8:16], bv[:, t, 8:16], rest2[:, t, :])
                            v.tensor_tensor(view(gate[:, :, h, 0:1], (P, NT), (1, 16)), bv,
                                            view(bv, (TOPK, NT), (0, 16)), ALU.subtract)
                            dve.drain()
                            flat = view(bpu, (1, 32))
                            v.tensor_scalar(view(ku[:, 0, :, :], (1, 32)), flat, 4, None, ALU.logical_shift_right)
                            v.tensor_scalar(view(ku[:, 1, :, :], (1, 32)), flat, 15, None, ALU.bitwise_and)
                            dve.drain()
                            v.tensor_copy(view(kf[s], (1, 64)), view(ku, (1, 64)))
                            dve.drain()
                            sum_up(1 - s, it * 2 + (s + 2), h)
                            for a_ in range(2):
                                last = v.tensor_tensor(eq[s][:, a_, :, :], view(kf[s][:, a_, :, :], (1, 32), (0, 16)),
                                                       const("iota", (0, 32), (1, 16)), ALU.is_equal)
                            last.then_inc(S("eq_ready"), 1)
                    sum_up(1, PH + 2, PH)
                    dve.sem_inc(S("gate_arg"), 1)
                    dve.wait_ge(S("gate_exp"), 1)
                    gs = STAT[:, 0:16]
                    g16 = view(gate, (16, 16), (1, 16))
                    v.reduce_sum(gs, g16, AX)
                    dve.drain()
                    v.reciprocal(gs, gs)
                    dve.drain()
                    v.tensor_tensor(g16, g16, view(gs, (1, 16), (0, 16)), ALU.mult)

                @b.gpsimd
                def _(pool):
                    pool.sem_inc(S("si_free"), 2)

                    def ahead_low(c, n):
                        for i in range(2):
                            pool.wait_ge(S("ahead_hi"), n * 2 + (i - 1))
                            nc.gpsimd.tensor_tensor(u_lo[i], ahead_raw[c][:, i, :], u_hi[i], ALU.subtract
                                                    ).then_inc(S("ahead_lo"), 1)

                    def times_numbers(s, n):
                        pool.wait_ge(S("eq_ready"), n)
                        for a_ in range(2):
                            e = view(eq[s][:, a_, :, :], (256, NT), (16, 16), (1, 16))
                            last = nc.gpsimd.tensor_tensor(e, e, view(si[s][:, a_, :, :], (TOPK, NT), (0, 16), (1, 16)),
                                                           ALU.mult)
                        last.then_inc(S("si_free"), 1)

                    for c in range(AHEAD_A_TURN):
                        ahead_low(c, c + 1)
                    times_numbers(0, 1)
                    with pool.Fori(1, PH // 2) as it:
                        tile = it * AHEAD_A_TURN
                        ahead_low(0, tile + 1)
                        times_numbers(1, it * 2)
                        ahead_low(1, tile + 2)
                        ahead_low(2, tile + 3)
                        times_numbers(0, it * 2 + 1)
                    times_numbers(1, PH)

            def load_u(sp, j, s):
                sp.dma_start(arena(U_RAW + s * 1024, 1024), a["u_tiles"][l, j, :, :]).then_inc(S(f"u_loaded{s}"), 16)

            def load_v(sp, j, s):
                sp.dma_start(arena(V_RAW + s * 1024, 1024), a["v_tiles"][l, j, :, :]).then_inc(S(f"v_loaded{s}"), 16)

            with nc.Block() as b:
                @b.sync
                def _(sp):
                    for s in range(2):
                        load_v(sp, s, s)
                        load_u(sp, AHEAD + s, s)

                @b.tensor
                def _(pe):
                    srcs = [view(idx[:, a_, :, 1, :], ((PH + 1) * TOPK, NT), (1, P)) for a_ in range(2)] + [
                        view(gate, (P, NT), (1, P))]
                    for i, src in enumerate(srcs):
                        for t in range(NT):
                            last = nc.tensor.transpose(bank[i][:, t * P:(t + 1) * P], src[:, t, :], ident)
                        last.then_inc(S("sel_turned"), 1)

                @b.vector
                def _(dve):
                    for i in range(3):
                        dve.wait_ge(S("sel_turned"), i + 1)
                        nc.vector.tensor_copy(sel[:, i, :], bank[i][:, 0:T])

            with nc.Block() as b:
                def numbers(side, tok, n):
                    return sel[:, side, bass.ds(tok, n)].unsqueeze(2).broadcast_to([P, n, P])

                DVE_ROWS = (2, 3, 2, 3)

                @b.vector
                def _(dve):
                    with dve.Fori(0, T // (4 * HOTS)) as it:
                        for s in range(HOTS):
                            tok = it * (4 * HOTS) + 4 * s
                            dve.wait_ge(S("hot_free"), it * HOTS + (s + 1))
                            nc.vector.tensor_tensor(bare[:, s, :, :], const("iota", (0, 2), (1, P)),
                                                    numbers(0, tok + 2, 2), ALU.is_equal).then_inc(S("hot_bare"), 1)
                            n = DVE_ROWS[s]
                            nc.vector.tensor_tensor(hot[:, s, 1, 0:n, :], const("iota", (0, n), (1, P)),
                                                    numbers(1, tok, n), ALU.is_equal)
                            for i in range(2):
                                one = bass.ds(tok + i, 1)
                                last = nc.vector.tensor_scalar(hot[:, s, 0, i, :], const("iota"), sel[:, 0, one],
                                                               sel[:, 2, one], ALU.is_equal, ALU.mult)
                            last.then_inc(S("hot_ready"), 1)

                @b.gpsimd
                def _(pool):
                    with pool.Fori(0, T // (4 * HOTS)) as it:
                        for s in range(HOTS):
                            pool.wait_ge(S("hot_free"), it * HOTS + (s + 1))
                            nc.gpsimd.tensor_copy(its_numbers[:, s, :], sel[:, 1, bass.ds(it * (4 * HOTS) + 4 * s, 4)])
                            pool.drain()
                            for i in range(DVE_ROWS[s], 4):
                                last = nc.gpsimd.tensor_scalar(hot[:, s, 1, i, :], const("iota"),
                                                               its_numbers[:, s, i:i + 1], None,
                                                               ALU.is_equal)
                            last.then_inc(S("hot_ready_pool"), 1)

                @b.tensor
                def _(pe):
                    pe.sem_inc(S("hot_free"), HOTS)
                    with pe.Fori(0, T // (4 * HOTS)) as it:
                        for s in range(HOTS):
                            pe.wait_ge(S("g_taken"), it * HOTS + (s + 1))
                            pe.wait_ge(S("hot_ready"), it * HOTS + (s + 1))
                            pe.wait_ge(S("hot_ready_pool"), it * HOTS + (s + 1))
                            pe.wait_ge(S("hot_ready_act"), it * HOTS + (s + 1))
                            for i in range(4):
                                last = nc.tensor.matmul(bank[s][:, i * P:(i + 1) * P], hot[:, s, 0, i, :],
                                                        hot[:, s, 1, i, :], start=True, stop=True,
                                                        skip_group_check=True)
                            last.then_inc(S("hot_free"), 1)

                @b.scalar
                def _(act):
                    act.sem_inc(S("g_taken"), HOTS)

                    def gates(s, n, tok):
                        act.wait_ge(S("hot_bare"), n)
                        for i in range(2):
                            last = nc.scalar.mul(hot[:, s, 0, 2 + i, :], bare[:, s, i, :],
                                                 sel[:, 2, bass.ds(tok + 2 + i, 1)])
                        last.then_inc(S("hot_ready_act"), 1)

                    def take_g(s, n, tok):
                        act.wait_ge(S("hot_free"), n + HOTS)
                        nc.scalar.copy(G[:, bass.ds(tok, 4), :], view(bank[s][:, :], (P, 4), (1, P))
                                       ).then_inc(S("g_taken"), 1)

                    gates(0, 1, 0)
                    with act.Fori(0, T // (4 * HOTS) - 1) as it:
                        for s in range(HOTS):
                            gates((s + 1) % HOTS, it * HOTS + (s + 2), it * (4 * HOTS) + 4 * (s + 1))
                            take_g(s, it * HOTS + (s + 1), it * (4 * HOTS) + 4 * s)
                    for n in range(T // 4 - HOTS, T // 4):
                        if n + 1 < T // 4:
                            gates((n + 1) % HOTS, n + 2, 4 * (n + 1))
                        take_g(n % HOTS, n + 1, 4 * n)

            NE = NKEY
            u_raw = [shaped(U_RAW + s * 1024, 2, 512) for s in range(2)]
            v_raw = [shaped(V_RAW + s * 1024, 2, 512) for s in range(2)]
            v_hi = [parts(V_PART + i * 1024, 512) for i in range(2)]
            v_lo = [parts(V_PART + i * 1024 + 512, 512) for i in range(2)]
            w_hi = [parts(W_PART + s * 512, T) for s in range(2)]
            w_lo = [parts(W_PART + s * 512 + T, T) for s in range(2)]
            ga = [arena(GA_AT + s * T, T) for s in range(2)]

            with nc.Block() as b:
                @b.sync
                def _(sp):
                    sp.wait_ge(S("u_lo"), 2)
                    load_u(sp, AHEAD + 2, 0)
                    with sp.Fori(1, AHEAD // 2 + 1) as it:
                        for s in range(2):
                            sp.wait_ge(S("v_lo"), it * 4 + 2 * (s - 1))
                            load_v(sp, it * 2 + s, s)
                    sp.wait_ge(S("u_lo"), 4)
                    load_u(sp, AHEAD + 3, 1)
                    with sp.Fori(AHEAD // 2 + 1, NE // 2 - 1) as it:
                        for s in range(2):
                            j = it * 2 + s
                            sp.wait_ge(S("v_lo"), it * 4 + 2 * (s - 1))
                            load_v(sp, j, s)
                            sp.wait_ge(S("u_lo"), it * 4 + (2 * (s + 1) - 2 * AHEAD))
                            load_u(sp, j + 2, s)
                    for s in range(2):
                        sp.wait_ge(S("v_lo"), 2 * (NE - 3 + s))
                        load_v(sp, NE - 2 + s, s)

                @b.tensor
                def _(pe):
                    pe.sem_inc(S("u_used"), 2)
                    pe.sem_inc(S("v_used"), 4)
                    for y in range(4):
                        nc.tensor.matmul(bank[y][:, :], ZERO[:, 0:P], ZERO[:, :], start=True, stop=False,
                                         skip_group_check=True)

                    def acts(s, j):
                        pe.wait_ge(S("act_taken"), j)
                        for i in range(2):
                            pe.wait_ge(S("u_lo"), j * 2 + (i - 1))
                            for k in range(4):
                                c = slice(k * P, (k + 1) * P)
                                last = mm3(bank[4 + s][:, 0:T], u_hi[i][:, c], u_lo[i][:, c],
                                           HT_HI[:, 4 * i + k, :], HT_LO[:, 4 * i + k, :],
                                           i == 0 and k == 0, i == 1 and k == 3)
                            last.then_inc(S("u_used"), 1)

                    def ys(s, j, stop=False):
                        pe.wait_ge(S("weight_ready"), j)
                        for n in range(2):
                            pe.wait_ge(S("v_lo"), j * 2 + (n - 1))
                            for t in range(NT):
                                c = slice(t * P, (t + 1) * P)
                                last = mm3(bank[2 * t + n][:, :], w_hi[s][:, c], w_lo[s][:, c], v_hi[n], v_lo[n],
                                           False, stop)
                            last.then_inc(S("v_used"), 1)

                    with pe.Fori(0, AHEAD // 2) as it:
                        for s in range(2):
                            ys(s, it * 2 + (s + 1))
                    acts(0, 1)
                    with pe.Fori(AHEAD // 2, NE // 2 - 1) as it:
                        acts(1, it * 2 + (2 - AHEAD))
                        ys(0, it * 2 + 1)
                        acts(0, it * 2 + (3 - AHEAD))
                        ys(1, it * 2 + 2)
                    acts(1, NE - AHEAD)
                    ys(0, NE - 1)
                    ys(1, NE, stop=True)

                @b.scalar
                def _(act):
                    act.sem_inc(S("act_taken"), 2)

                    def split_u(s, j, turn):
                        act.wait_ge(S(f"u_loaded{s}"), turn)
                        for i in range(2):
                            act.wait_ge(S("u_used"), j * 2 + (i - 1))
                            nc.scalar.copy(u_hi[i], u_raw[s][:, i, :]).then_inc(S("u_hi"), 1)

                    def gelu(s, j):
                        act.wait_ge(S("u_used"), j * 2 + 2)
                        act.wait_ge(S("ga_free"), j)
                        nc.scalar.activation(ga[s], bank[4 + s][:, 0:T], ACT.Gelu_apprx_tanh
                                             ).then_inc(S("act_taken"), 1)

                    def split_v(s, j, turn):
                        act.wait_ge(S(f"v_loaded{s}"), turn)
                        for i in range(2):
                            act.wait_ge(S("v_used"), j * 2 + (i + 1))
                            nc.scalar.copy(v_hi[i], v_raw[s][:, i, :]).then_inc(S("v_hi"), 1)

                    split_u(0, 1, 16)
                    with act.Fori(0, AHEAD // 2) as it:
                        for s in range(2):
                            split_v(s, it * 2 + (s + 1), it * 16 + 16)
                    split_u(1, 2, 16)
                    with act.Fori(AHEAD // 2, NE // 2 - 1) as it:
                        for s in range(2):
                            gelu(s, it * 2 + (s + 1 - AHEAD))
                            split_v(s, it * 2 + (s + 1), it * 16 + 16)
                            split_u(s, it * 2 + (s + 3 - AHEAD), it * 16 + (32 - 8 * AHEAD))
                    for s in range(2):
                        gelu(s, NE - AHEAD - 1 + s)
                        split_v(s, NE - 1 + s, 8 * NE)

                @b.vector
                def _(dve):
                    def split_u(s, j):
                        for i in range(2):
                            dve.wait_ge(S("u_hi"), j * 2 + (i - 1))
                            nc.vector.tensor_tensor(u_lo[i], u_raw[s][:, i, :], u_hi[i], ALU.subtract
                                                    ).then_inc(S("u_lo"), 1)

                    def split_v(s, j):
                        for i in range(2):
                            dve.wait_ge(S("v_hi"), j * 2 + (i - 1))
                            nc.vector.tensor_tensor(v_lo[i], v_raw[s][:, i, :], v_hi[i], ALU.subtract
                                                    ).then_inc(S("v_lo"), 1)

                    def weight(s, j, j0, act):
                        nc.vector.tensor_tensor(ga[s], act, G[:, :, j0], ALU.mult)
                        dve.drain()
                        dve.wait_ge(S("v_used"), j * 2)
                        nc.vector.tensor_copy(w_hi[s], ga[s])
                        dve.drain()
                        nc.vector.tensor_tensor(w_lo[s], ga[s], w_hi[s], ALU.subtract).then_inc(S("weight_ready"), 1)

                    def fresh_weight(s, j, j0):
                        dve.wait_ge(S("act_taken"), j + (2 - AHEAD))
                        weight(s, j, j0, ga[s])
                        dve.drain()
                        dve.sem_inc(S("ga_free"), 1)

                    split_u(0, 1)
                    with dve.Fori(0, AHEAD // 2) as it:
                        for s in range(2):
                            weight(s, it * 2 + (s + 1), it * 2 + s, ahead[:, it * 2 + s, :])
                            split_v(s, it * 2 + (s + 1))
                    dve.drain()
                    dve.sem_inc(S("ga_free"), 2)
                    split_u(1, 2)
                    with dve.Fori(AHEAD // 2, NE // 2 - 1) as it:
                        for s in range(2):
                            fresh_weight(s, it * 2 + (s + 1), it * 2 + s)
                            split_v(s, it * 2 + (s + 1))
                            split_u(s, it * 2 + (s + 3 - AHEAD))
                    for s in range(2):
                        fresh_weight(s, NE - 1 + s, NE - 2 + s)
                        split_v(s, NE - 1 + s)
                    dve.wait_ge(S("v_used"), 2 * NE + 4)
                    for t in range(NT):
                        for n in range(2):
                            xx = X[:, t, n * 512:(n + 1) * 512]
                            nc.vector.tensor_tensor(xx, xx, bank[2 * t + n][:, :], ALU.add)

        if 1 in blocks:
            with nc.Fori(0, L) as l:
                first_layer(l)
            for semaphore in semaphores.values():
                nc.release_semaphore(semaphore)
            semaphores.clear()
        if 2 in blocks:
            with nc.Fori(0, L) as l:
                second_layer(l)

        with nc.Block() as b:
            @b.sync
            def _(sp):
                sp.dma_start(out[0].rearrange("(t p) d -> p t d", p=P), X[:, :, :]).then_inc(S("stored"), 16)
                sp.wait_ge(S("stored"), 16)


def constants():
    c = [np.zeros((P, n), np.float32) for n in (NCONST, NCONST1, NCONST2)]

    def put(name, value):
        for array, plan in zip(c, (CONST, CONST1, CONST2)):
            if name in plan:
                at, width = plan[name]
                array[:, at:at + width] = np.asarray(value, np.float32).reshape(P, width)

    p = np.arange(P)
    tok = (np.arange(2)[None, :] * P + p[:, None])
    keys = np.arange(T)
    put("ident", np.eye(P))
    put("iota", np.broadcast_to(np.arange(P), (P, P)))
    col = tok % GRID
    start = np.clip(col - 8, 0, GRID - 16)[:, :, None]
    kc = keys[None, None, :] % GRID
    put("mask_na", np.where((kc >= start) & (kc < start + 16), 0.0, -BIG))
    put("mask_sw", np.where(np.abs(tok[:, :, None] - keys) <= 128, 0.0, -BIG))
    before = tok[:, :, None] < keys
    put("strict01", before)
    put("strict_big", np.where(before, 0.0, BIG))
    put("causal_big", np.where(tok[:, :, None] <= keys, 0.0, BIG))
    put("tril_t", p[:, None] <= p[None, :])
    put("suffix", p[:, None] >= p[None, :])
    put("ones", np.ones((P, P)))

    def angles(pos, dim):
        inv = np.float32(10000.0) ** (-np.arange(0, dim, 2, dtype=np.float32) / np.float32(dim))
        return (pos.astype(np.float32)[:, :, None] * inv.astype(np.float32)).astype(np.float32)

    for name, pos, dim in (("full", tok, 64), ("mla", tok, 32), ("row", tok // GRID, 32), ("col", tok % GRID, 32)):
        put("cos_" + name, np.cos(angles(pos, dim)))
        put("sin_" + name, np.sin(angles(pos, dim)))
    pick = np.zeros((P, NH6, P))
    for h in range(NH6):
        pick[h, h, :] = 1.0
    put("pick", pick)
    return c


def lay_out(i):
    f = {k: np.asarray(v) for k, v in i.items()}
    cols = lambda g: np.ascontiguousarray(g.reshape(L, -1, P).transpose(0, 2, 1))
    r = dict(zip(("consts", "consts1", "consts2"), constants()), x=f["x"])
    for k in ("w_in", "w_out", "w_down", "w_in_2", "w_out_2", "mla_w_uq", "mla_w_ukv", "sw_sink",
              "mix_post_gain", "ffn_post_gain", "sg_vn_g_2"):
        r[k] = f[k]
    r["norm_gains"] = np.ascontiguousarray(np.stack(
        [f[k].reshape(L, KD, P) for k in ("mix_pre_gain", "ffn_pre_gain", "norm1_g_2", "norm2_g_2", "out_g_2")]
    ).transpose(3, 0, 1, 2))
    r["mla_gain"] = np.concatenate([cols(f["mla_q_gain"]), cols(f["mla_kv_gain"])], axis=2)
    r["ax_gain"] = np.concatenate([np.tile(f["ax_q_gain"], (1, 4)), np.tile(f["ax_k_gain"], (1, 2))], axis=1)
    padded = np.zeros((L, 4, 15, 127), np.float32)
    padded[:, :, :, 48:79] = f["na_rpb"]
    c = np.arange(GRID)
    window = padded[:, :, :, c[None, :] - c[:, None] + 63]
    rows = np.stack([window[:, :, 7 - q:11 - q] for q in range(4)], axis=2)
    r["rpb_rows"] = np.ascontiguousarray(
        rows.reshape(L, 4, NT, 2, 4, GRID, GRID).transpose(0, 3, 5, 1, 2, 4, 6)).reshape(L, P, 4 * NT * T)
    r["w_up_tiles"] = np.ascontiguousarray(
        f["w_up"].reshape(L, KD, P, 2, NF, P).transpose(0, 4, 2, 3, 1, 5)).reshape(L, NF, P, 2 * KD * P)
    conv = np.concatenate([f["conv_w"], f["conv_b"][:, None]], axis=1)
    r["conv_params"] = np.ascontiguousarray(
        conv.reshape(L, 4, 2, NF, P).transpose(0, 4, 3, 2, 1)).reshape(L, P, NF * 8)
    r["sb_gain"] = np.concatenate([np.tile(f["sb_qn_g_2"], (1, NH6)), np.tile(f["sb_kn_g_2"], (1, NH6))], axis=1)
    conv = np.concatenate([f["ml_conv_w_2"], f["ml_conv_b_2"][:, None]], axis=1)
    r["ml_conv"] = np.ascontiguousarray(conv.reshape(L, 5, 6, P).transpose(0, 3, 2, 1))
    r["ml_if_b"] = np.ascontiguousarray(np.stack([f["ml_i_b_2"], f["ml_f_b_2"]], axis=2))
    r["sg_b_t"] = np.ascontiguousarray(f["sg_b_2"].transpose(0, 2, 1))
    r["sg_w_t"] = np.ascontiguousarray(f["sg_w_2"].transpose(0, 3, 1, 2))
    r["wq_tiles"] = np.ascontiguousarray(
        f["peer_wq_2"].reshape(L, KD, P, NSET, P).transpose(0, 3, 2, 1, 4)).reshape(L, NSET, P, KD * P)
    r["keys_t"] = np.ascontiguousarray(
        f["peer_keys_2"].reshape(L, NSET, NKEY, P).transpose(0, 3, 1, 2)).reshape(L, P, NSET * NKEY)
    r["u_tiles"] = np.ascontiguousarray(
        f["peer_u_2"].reshape(L, P, NKEY, KD, P).transpose(0, 2, 4, 3, 1)).reshape(L, NKEY, P, KD * P)
    r["v_tiles"] = np.ascontiguousarray(f["peer_v_2"].reshape(L, P, NKEY, D).transpose(0, 2, 1, 3))
    return r


def kernel(**inputs):
    import concourse.bacc as bacc
    from concourse.bass_utils import run_bass_kernel_spmd

    nc = bacc.Bacc("TRN2", target_bir_lowering=False, num_devices=1)
    arrays, args = {}, {}
    for name, v in lay_out(inputs).items():
        arrays[f"in_{name}"] = v
        args[name] = nc.dram_tensor(f"in_{name}", v.shape, mybir.dt.from_np(v.dtype), kind="ExternalInput").ap()
    out = nc.dram_tensor("out_x", (1, T, D), F32, kind="ExternalOutput").ap()
    build(nc, args, out)
    r = run_bass_kernel_spmd(nc, [arrays], core_ids=[0])
    return r.results[0]["out_x"]
```
